# Optimizing a Trainium2 kernel written in Bass

```python
import math
import jax, jax.numpy as jnp
from jax import lax
import numpy as np

D_MODEL = 1024
BATCH = 1
SEQ = 512
DEPTH = 1

N_MEM = 256
A_HEADS = 4
A_HEAD_DIM = 64
A_V_DIM = 2 * A_HEAD_DIM
B_GROUPS = ((128, 1), (512, 4), (2048, 16))
B_HEADS_PER_GROUP = 4
B_HEAD_DIM = 128
C_HEADS = 4
C_HEAD_DIM = 128
N_BRANCHES = 3
BRANCH_WIDTH = 512
D_FF = -(-8 * D_MODEL // (3 * 256)) * 256
Q_BLOCK = 128
EPS = 1e-6
ALIBI_MAX_BIAS = 8.0

A_QK_COLS = A_HEADS * 2 * A_HEAD_DIM
A_V_COLS = A_HEADS * A_V_DIM
B_COLS = len(B_GROUPS) * B_HEADS_PER_GROUP * B_HEAD_DIM
C_Q_COLS = C_HEADS * C_HEAD_DIM
IN_SIZES = (A_QK_COLS, A_QK_COLS, A_V_COLS, B_COLS, B_COLS, B_COLS, C_Q_COLS)
D_IN = sum(IN_SIZES)


def rms_norm(x, g):
    xf = x.astype(jnp.float32)
    y = xf * lax.rsqrt(jnp.mean(xf * xf, axis=-1, keepdims=True) + EPS)
    return (y * g.astype(jnp.float32)).astype(x.dtype)

def alibi_slopes(n):
    return jnp.exp2(-ALIBI_MAX_BIAS * jnp.arange(1, n + 1, dtype=jnp.float32) / n)

def diff_attention(q, k, v, slopes, lam):
    b, t, h, _, dh = q.shape
    nq = t // Q_BLOCK
    scale = dh ** -0.5
    pos_k = jnp.arange(t, dtype=jnp.int32)
    q_blocks = q.reshape(b, nq, Q_BLOCK, h, 2, dh).transpose(1, 0, 2, 3, 4, 5)
    starts = jnp.arange(nq, dtype=jnp.int32) * Q_BLOCK

    def one_block(args):
        qb, start = args
        s = jnp.einsum('bqhcd,bkhcd->bhcqk', qb, k).astype(jnp.float32) * scale
        pos_q = start + jnp.arange(Q_BLOCK, dtype=jnp.int32)
        dist = jnp.abs(pos_q[:, None] - pos_k[None, :]).astype(jnp.float32)
        s = s - slopes[None, :, None, None, None] * dist[None, None, None]
        p = jax.nn.softmax(s, axis=-1)
        p_diff = p[:, :, 0] - lam * p[:, :, 1]
        return jnp.einsum('bhqk,bkhe->bqhe', p_diff.astype(v.dtype), v)

    o = lax.map(one_block, (q_blocks, starts))
    return o.transpose(1, 0, 2, 3, 4).reshape(b, t, h, v.shape[-1])

def dilated_window_attention(q, k, v, slopes, window, dilation):
    b, t, h, hd = q.shape
    n_side = window // (2 * dilation)
    sub_len = t // dilation
    blk = n_side
    nb = -(-sub_len // blk)
    pad = nb * blk - sub_len

    def to_sub(a):
        return a.reshape(b, sub_len, dilation, h, hd).transpose(0, 2, 3, 1, 4)

    qs = jnp.pad(to_sub(q), ((0, 0), (0, 0), (0, 0), (0, pad), (0, 0)))
    qs = qs.reshape(b, dilation, h, nb, blk, hd)

    def windows(a):
        ap = jnp.pad(to_sub(a), ((0, 0), (0, 0), (0, 0), (blk, blk + pad), (0, 0)))
        ap = ap.reshape(b, dilation, h, nb + 2, blk, hd)
        return jnp.concatenate([ap[:, :, :, :-2], ap[:, :, :, 1:-1], ap[:, :, :, 2:]], axis=4)

    kw, vw = windows(k), windows(v)
    s = jnp.einsum('brhnqd,brhnkd->brhnqk', qs, kw).astype(jnp.float32) * hd ** -0.5
    q_idx = jnp.arange(nb)[:, None, None] * blk + jnp.arange(blk)[None, :, None]
    k_idx = (jnp.arange(nb)[:, None, None] - 1) * blk + jnp.arange(3 * blk)[None, None, :]
    rel = k_idx - q_idx
    valid = (jnp.abs(rel) <= n_side) & (k_idx >= 0) & (k_idx < sub_len)
    dist = (dilation * jnp.abs(rel)).astype(jnp.float32)
    s = s - slopes[None, None, :, None, None, None] * dist
    s = jnp.where(valid, s, -jnp.inf)
    lse = jax.nn.logsumexp(s, axis=-1)
    p = jnp.exp(s - lse[..., None])
    o = jnp.einsum('brhnqk,brhnkd->brhnqd', p.astype(v.dtype), vw)
    o = o.reshape(b, dilation, h, nb * blk, hd)[:, :, :, :sub_len]
    lse = lse.reshape(b, dilation, h, nb * blk)[:, :, :, :sub_len]
    o = o.transpose(0, 3, 1, 2, 4).reshape(b, t, h, hd)
    lse = lse.transpose(0, 3, 1, 2).reshape(b, t, h)
    return o, lse

def memory_attention(q, k, v):
    s = jnp.einsum('bthd,bnhd->bhtn', q, k).astype(jnp.float32) * q.shape[-1] ** -0.5
    p = jax.nn.softmax(s, axis=-1)
    return jnp.einsum('bhtn,bnhd->bthd', p.astype(v.dtype), v)

def first_inputs(seed: int = 0) -> dict:
    key = jax.random.key(seed)
    ks = jax.random.split(key, 32)
    L = DEPTH

    def nrm(k, shape, fan_in):
        return jax.random.normal(k, shape, jnp.float32) * fan_in ** -0.5

    def gain(k, shape):
        return 1.0 + 0.02 * jax.random.normal(k, shape, jnp.float32)

    def small(k, shape, scale):
        return scale * jax.random.normal(k, shape, jnp.float32)

    return {
        'x': jax.random.normal(ks[0], (BATCH, SEQ, D_MODEL), jnp.float32),
        'mem': jax.random.normal(ks[1], (BATCH, N_MEM, D_MODEL), jnp.float32),
        'norm_mix': gain(ks[2], (L, D_MODEL)),
        'w_in': nrm(ks[3], (L, D_MODEL, D_IN), D_MODEL),
        'w_gate': nrm(ks[4], (L, D_MODEL, N_BRANCHES * D_MODEL), D_MODEL),
        'b_gate': small(ks[5], (L, N_BRANCHES * D_MODEL), 0.02),
        'a_q_norm': gain(ks[6], (L, A_HEAD_DIM)),
        'a_k_norm': gain(ks[7], (L, A_HEAD_DIM)),
        'a_lambda_q1': small(ks[8], (L, A_HEAD_DIM), 0.1),
        'a_lambda_k1': small(ks[9], (L, A_HEAD_DIM), 0.1),
        'a_lambda_q2': small(ks[10], (L, A_HEAD_DIM), 0.1),
        'a_lambda_k2': small(ks[11], (L, A_HEAD_DIM), 0.1),
        'a_subln': gain(ks[12], (L, A_V_DIM)),
        'b_q_norm': gain(ks[13], (L, B_HEAD_DIM)),
        'b_k_norm': gain(ks[14], (L, B_HEAD_DIM)),
        'mem_norm': gain(ks[15], (L, D_MODEL)),
        'w_mem_kv': nrm(ks[16], (L, D_MODEL, 2 * C_HEADS * C_HEAD_DIM), D_MODEL),
        'c_q_norm': gain(ks[17], (L, C_HEAD_DIM)),
        'c_k_norm': gain(ks[18], (L, C_HEAD_DIM)),
        'w_branch': nrm(ks[19], (L, N_BRANCHES, BRANCH_WIDTH, D_MODEL), BRANCH_WIDTH),
        'w_out': nrm(ks[20], (L, D_MODEL, D_MODEL), D_MODEL),
        'norm_ffn': gain(ks[21], (L, D_MODEL)),
        'w_ffn_gate': nrm(ks[22], (L, D_MODEL, D_FF), D_MODEL),
        'w_ffn_up': nrm(ks[23], (L, D_MODEL, D_FF), D_MODEL),
        'w_ffn_down': nrm(ks[24], (L, D_FF, D_MODEL), D_FF),
    }

def first_block(x, mem, norm_mix, w_in, w_gate, b_gate, a_q_norm, a_k_norm, a_lambda_q1, a_lambda_k1,
              a_lambda_q2, a_lambda_k2, a_subln, b_q_norm, b_k_norm, mem_norm, w_mem_kv, c_q_norm,
              c_k_norm, w_branch, w_out, norm_ffn, w_ffn_gate, w_ffn_up, w_ffn_down):
    b, t, d = x.shape
    n_mem = mem.shape[1]
    n_groups = len(B_GROUPS)
    offsets = [int(o) for o in np.cumsum(IN_SIZES)[:-1]]
    slopes_a = alibi_slopes(A_HEADS)
    slopes_b = alibi_slopes(n_groups * B_HEADS_PER_GROUP).reshape(n_groups, B_HEADS_PER_GROUP)
    for l in range(DEPTH):
        lambda_init = 0.8 - 0.6 * math.exp(-0.3 * l)
        h = rms_norm(x, norm_mix[l])
        aq, ak, av, bq, bk, bv, cq = jnp.split(h @ w_in[l], offsets, axis=-1)

        aq = rms_norm(aq.reshape(b, t, A_HEADS, 2, A_HEAD_DIM), a_q_norm[l])
        ak = rms_norm(ak.reshape(b, t, A_HEADS, 2, A_HEAD_DIM), a_k_norm[l])
        av = av.reshape(b, t, A_HEADS, A_V_DIM)
        lam = (jnp.exp(jnp.sum(a_lambda_q1[l] * a_lambda_k1[l]).astype(jnp.float32))
               - jnp.exp(jnp.sum(a_lambda_q2[l] * a_lambda_k2[l]).astype(jnp.float32)) + lambda_init)
        out_a = diff_attention(aq, ak, av, slopes_a, lam)
        out_a = (rms_norm(out_a, a_subln[l]) * (1.0 - lambda_init)).reshape(b, t, BRANCH_WIDTH)

        bq = rms_norm(bq.reshape(b, t, n_groups, B_HEADS_PER_GROUP, B_HEAD_DIM), b_q_norm[l])
        bk = rms_norm(bk.reshape(b, t, n_groups, B_HEADS_PER_GROUP, B_HEAD_DIM), b_k_norm[l])
        bv = bv.reshape(b, t, n_groups, B_HEADS_PER_GROUP, B_HEAD_DIM)
        outs, lses = [], []
        for g, (window, dilation) in enumerate(B_GROUPS):
            o, lse = dilated_window_attention(bq[:, :, g], bk[:, :, g], bv[:, :, g], slopes_b[g], window, dilation)
            outs.append(o)
            lses.append(lse)
        wts = jax.nn.softmax(jnp.stack(lses, axis=2), axis=2)
        out_b = jnp.sum(wts[..., None].astype(bv.dtype) * jnp.stack(outs, axis=2), axis=2)
        out_b = out_b.reshape(b, t, BRANCH_WIDTH)

        m = rms_norm(mem, mem_norm[l])
        kv = (m @ w_mem_kv[l]).reshape(b, n_mem, 2, C_HEADS, C_HEAD_DIM)
        ck = rms_norm(kv[:, :, 0], c_k_norm[l])
        cv = kv[:, :, 1]
        cq = rms_norm(cq.reshape(b, t, C_HEADS, C_HEAD_DIM), c_q_norm[l])
        out_c = memory_attention(cq, ck, cv).reshape(b, t, BRANCH_WIDTH)

        branches = jnp.einsum('btgc,gcd->btgd', jnp.stack([out_a, out_b, out_c], axis=2), w_branch[l])
        gates = jax.nn.sigmoid(h @ w_gate[l] + b_gate[l]).reshape(b, t, N_BRANCHES, d)
        x = x + jnp.sum(gates * branches, axis=2) @ w_out[l]

        h2 = rms_norm(x, norm_ffn[l])
        x = x + (jax.nn.silu(h2 @ w_ffn_gate[l]) * (h2 @ w_ffn_up[l])) @ w_ffn_down[l]
    return x


DEPTH_2 = 2

CHUNK = 64
D_MIX = D_MODEL
D_A = D_MIX // 2
D_B = D_MIX - D_A
HGRN_KDIM = 128
HGRN_HEADS = D_A // HGRN_KDIM
HGRN_VDIM = D_A // HGRN_HEADS
POOL_WINDOWS = (2, 4, 8, 16)
POOL_GROUPS = len(POOL_WINDOWS)
POOL_CH = D_B // POOL_GROUPS
D_IN_2 = 4 * D_A + D_B
D_FF_2 = ((8 * D_MODEL // 3) + 127) // 128 * 128
XA_HEADS = 4
XA_HEAD_DIM = D_MODEL // XA_HEADS


def rmsnorm(x, g):
    xf = x.astype(jnp.float32)
    y = xf * lax.rsqrt(jnp.mean(xf * xf, axis=-1, keepdims=True) + EPS)
    return (y * g.astype(jnp.float32)).astype(x.dtype)

def swiglu(h, w1, w3, w2):
    return (jax.nn.silu(h @ w1) * (h @ w3)) @ w2

def hgrn2_chunkwise(q, k, v, log_f):
    B, T, H, K = q.shape
    V = v.shape[-1]
    nc = T // CHUNK

    def to_chunks(a):
        return a.reshape(B, nc, CHUNK, H, a.shape[-1]).transpose(1, 0, 3, 2, 4)

    causal = jnp.tril(jnp.ones((CHUNK, CHUNK), dtype=bool))[:, :, None]

    def step(S, inp):
        qc, kc, vc, gc = inp
        b = jnp.cumsum(gc, axis=2)
        o_inter = jnp.einsum('bhtk,bhkv->bhtv', qc * jnp.exp(b), S)
        rel = b[:, :, :, None, :] - b[:, :, None, :, :]
        decay = jnp.exp(jnp.where(causal, rel, -jnp.inf))
        A = jnp.einsum('bhtk,bhsk,bhtsk->bhts', qc, kc, decay)
        o = o_inter + jnp.einsum('bhts,bhsv->bhtv', A, vc)
        b_last = b[:, :, -1:, :]
        S = jnp.exp(b_last[:, :, 0, :, None]) * S + jnp.einsum(
            'bhsk,bhsv->bhkv', kc * jnp.exp(b_last - b), vc)
        return S, o

    S0 = jnp.zeros((B, H, K, V), jnp.float32)
    _, o = lax.scan(step, S0, (to_chunks(q), to_chunks(k), to_chunks(v), to_chunks(log_f)))
    return o.transpose(1, 0, 3, 2, 4).reshape(B, T, H, V)

def hgrn2_mixer(q_in, f_in, i_in, g_in, lb, norm_g):
    B, T, _ = q_in.shape
    shp = (B, T, HGRN_HEADS, HGRN_KDIM)
    q = q_in.astype(jnp.float32).reshape(shp)
    z = f_in.astype(jnp.float32).reshape(shp)
    lbh = lb.reshape(HGRN_HEADS, HGRN_KDIM)
    log_f = jnp.logaddexp(jnp.log(lbh), jnp.log1p(-lbh) + jax.nn.log_sigmoid(z))
    k = (1.0 - lbh) * jax.nn.sigmoid(-z)
    v = i_in.astype(jnp.float32).reshape(B, T, HGRN_HEADS, HGRN_VDIM)
    o = hgrn2_chunkwise(q, k, v, log_f)
    o = o * lax.rsqrt(jnp.mean(o * o, axis=-1, keepdims=True) + EPS)
    o = o * norm_g.astype(jnp.float32).reshape(HGRN_HEADS, HGRN_VDIM)
    o = o.reshape(B, T, D_A) * jax.nn.silu(g_in.astype(jnp.float32))
    return o.astype(q_in.dtype)

def multiscale_pool(u, pool_w, pool_scale):
    B, T, _ = u.shape
    uf = u.astype(jnp.float32).reshape(B, T, POOL_GROUPS, POOL_CH)
    cs = jnp.cumsum(uf, axis=1)
    t_count = jnp.arange(1, T + 1, dtype=jnp.float32)
    outs = []
    for j, w in enumerate(POOL_WINDOWS):
        csj = cs[:, :, j]
        prev = jnp.pad(csj, ((0, 0), (w, 0), (0, 0)))[:, :T]
        mean = (csj - prev) / jnp.minimum(t_count, w)[None, :, None]
        outs.append(mean - uf[:, :, j])
    p = jnp.stack(outs, axis=2)
    y = jnp.einsum('btgc,gcd->btgd', p, pool_w.astype(jnp.float32)).reshape(B, T, D_B)
    return (y * pool_scale.astype(jnp.float32)).astype(u.dtype)

def mem_cross_attention(h, mem_n, wq, wkv, wo):
    B, T, _ = h.shape
    M = mem_n.shape[1]
    q = (h @ wq).reshape(B, T, XA_HEADS, XA_HEAD_DIM)
    kv = (mem_n @ wkv).reshape(B, M, 2, XA_HEADS, XA_HEAD_DIM)
    k, v = kv[:, :, 0], kv[:, :, 1]
    s = jnp.einsum('bthd,bmhd->bhtm', q, k).astype(jnp.float32) * (XA_HEAD_DIM ** -0.5)
    p = jax.nn.softmax(s, axis=-1).astype(h.dtype)
    o = jnp.einsum('bhtm,bmhd->bthd', p, v).reshape(B, T, D_MODEL)
    return o @ wo

def second_inputs(seed: int = 0) -> dict:
    key = jax.random.key(seed)
    ks = jax.random.split(key, 24)
    f32 = jnp.float32

    def nrm(k, shape, scale):
        return jax.random.normal(k, shape, f32) * scale

    def gain(k, shape):
        return 1.0 + 0.1 * jax.random.normal(k, shape, f32)

    L, D, F = DEPTH_2, D_MODEL, D_FF_2
    return {
        'x': nrm(ks[0], (BATCH, SEQ, D), 1.0),
        'mem': nrm(ks[1], (BATCH, N_MEM, D), 1.0),
        'ffn1_norm': gain(ks[2], (L, D)),
        'ffn1_w1': nrm(ks[3], (L, D, F), D ** -0.5),
        'ffn1_w3': nrm(ks[4], (L, D, F), D ** -0.5),
        'ffn1_w2': nrm(ks[5], (L, F, D), F ** -0.5),
        'mix_norm': gain(ks[6], (L, D)),
        'w_in': nrm(ks[7], (L, D, D_IN_2), D ** -0.5),
        'lb_logits': nrm(ks[8], (L, D_A), 1.0),
        'hgrn_norm': gain(ks[9], (L, D_A)),
        'pool_w': nrm(ks[10], (L, POOL_GROUPS, POOL_CH, POOL_CH), POOL_CH ** -0.5),
        'pool_scale': gain(ks[11], (L, D_B)),
        'w_out': nrm(ks[12], (L, D_MIX, D), D_MIX ** -0.5),
        'xa_norm': gain(ks[13], (L, D)),
        'mem_norm': gain(ks[14], (L, D)),
        'xa_wq': nrm(ks[15], (L, D, D), D ** -0.5),
        'xa_wkv': nrm(ks[16], (L, D, 2 * D), D ** -0.5),
        'xa_wo': nrm(ks[17], (L, D, D), D ** -0.5),
        'ffn2_norm': gain(ks[18], (L, D)),
        'ffn2_w1': nrm(ks[19], (L, D, F), D ** -0.5),
        'ffn2_w3': nrm(ks[20], (L, D, F), D ** -0.5),
        'ffn2_w2': nrm(ks[21], (L, F, D), F ** -0.5),
        'final_norm': gain(ks[22], (D,)),
    }

def second_block(x, mem, ffn1_norm, ffn1_w1, ffn1_w3, ffn1_w2, mix_norm, w_in, lb_logits,
              hgrn_norm, pool_w, pool_scale, w_out, xa_norm, mem_norm, xa_wq, xa_wkv,
              xa_wo, ffn2_norm, ffn2_w1, ffn2_w3, ffn2_w2, final_norm):
    lb_all = jnp.cumsum(jax.nn.softmax(lb_logits.astype(jnp.float32), axis=0), axis=0)
    lb_all = lb_all - lb_all[0:1]
    splits = [D_A, 2 * D_A, 3 * D_A, 4 * D_A]
    for l in range(DEPTH_2):
        x = x + 0.5 * swiglu(rmsnorm(x, ffn1_norm[l]), ffn1_w1[l], ffn1_w3[l], ffn1_w2[l])
        h = rmsnorm(x, mix_norm[l])
        proj = h @ w_in[l]
        q_a, f_a, i_a, g_a, u_b = jnp.split(proj, splits, axis=-1)
        o_a = hgrn2_mixer(q_a, f_a, i_a, g_a, lb_all[l], hgrn_norm[l])
        o_b = multiscale_pool(u_b, pool_w[l], pool_scale[l])
        x = x + jnp.concatenate([o_a, o_b], axis=-1) @ w_out[l]
        x = x + mem_cross_attention(rmsnorm(x, xa_norm[l]), rmsnorm(mem, mem_norm[l]),
                                    xa_wq[l], xa_wkv[l], xa_wo[l])
        x = x + 0.5 * swiglu(rmsnorm(x, ffn2_norm[l]), ffn2_w1[l], ffn2_w3[l], ffn2_w2[l])
    return rmsnorm(x, final_norm)


def setup_inputs(seed=0):
    out = dict(first_inputs(seed))
    for name, value in second_inputs(seed + 1).items():
        if name != "x":
            out[name + "_2"] = value
    return out


def reference(
    x, mem, norm_mix, w_in, w_gate, b_gate, a_q_norm, a_k_norm, a_lambda_q1, a_lambda_k1,
    a_lambda_q2, a_lambda_k2, a_subln, b_q_norm, b_k_norm, mem_norm, w_mem_kv, c_q_norm,
    c_k_norm, w_branch, w_out, norm_ffn, w_ffn_gate, w_ffn_up, w_ffn_down, mem_2, ffn1_norm_2,
    ffn1_w1_2, ffn1_w3_2, ffn1_w2_2, mix_norm_2, w_in_2, lb_logits_2, hgrn_norm_2, pool_w_2,
    pool_scale_2, w_out_2, xa_norm_2, mem_norm_2, xa_wq_2, xa_wkv_2, xa_wo_2, ffn2_norm_2,
    ffn2_w1_2, ffn2_w3_2, ffn2_w2_2, final_norm_2,
):
    x = first_block(
        x, mem, norm_mix, w_in, w_gate, b_gate, a_q_norm, a_k_norm, a_lambda_q1, a_lambda_k1,
        a_lambda_q2, a_lambda_k2, a_subln, b_q_norm, b_k_norm, mem_norm, w_mem_kv, c_q_norm,
        c_k_norm, w_branch, w_out, norm_ffn, w_ffn_gate, w_ffn_up, w_ffn_down,
    )
    return second_block(
        x, mem_2, ffn1_norm_2, ffn1_w1_2, ffn1_w3_2, ffn1_w2_2, mix_norm_2, w_in_2, lb_logits_2,
        hgrn_norm_2, pool_w_2, pool_scale_2, w_out_2, xa_norm_2, mem_norm_2, xa_wq_2, xa_wkv_2,
        xa_wo_2, ffn2_norm_2, ffn2_w1_2, ffn2_w3_2, ffn2_w2_2, final_norm_2,
    )


_drawn_inputs = setup_inputs


def setup_inputs(seed=0):
    import zlib

    import numpy as np

    out = dict(_drawn_inputs(seed))
    spreads = {}
    factors = {'b_gate': 8.0,
     'a_q_norm': 4.396,
     'a_k_norm': 4.758,
     'a_lambda_k1': 8.0,
     'a_lambda_q2': 8.0,
     'a_subln': 4.902,
     'b_q_norm': 8.0,
     'b_k_norm': 8.0,
     'mem_norm': 8.0,
     'c_q_norm': 8.0,
     'c_k_norm': 8.0,
     'norm_ffn': 2.847,
     'xa_norm_2': 5.387,
     'mem_norm_2': 3.686,
     'ffn2_norm_2': 4.833}
    for name, (base, spread) in spreads.items():
        noise = np.random.default_rng([zlib.crc32(name.encode()), seed]).standard_normal(out[name].shape)
        drawn = base * np.exp(spread * noise) if base else spread * noise
        out[name] = __import__('jax').numpy.asarray(drawn.astype(out[name].dtype))
    for name, factor in factors.items():
        out[name] = (out[name] * factor).astype(out[name].dtype)
    return out
```

```python
import math
from contextlib import ExitStack

import numpy as np

import concourse.bass as bass
from concourse import mybir

P = 128
F32 = mybir.dt.float32
F32R = mybir.dt.float32r
U8 = mybir.dt.uint8
ACT = mybir.ActivationFunctionType
ALU = mybir.AluOpType
AX = mybir.AxisListType

T = 512
NT = T // P
D = 1024
DC = D // P
NM = 256
NF = 2816 // P
EPS = 1e-6
NHEAD = 4
UT = 8
RAW = 3
RING = 4
LAMBDA_INIT = 0.8 - 0.6 * math.exp(0.0)
LAYERS = 2

KB = 1024


def column_plan():
    plan, at = {}, 0
    names = [("norm_mix", 8), ("norm_ffn", 8), ("b_gate", 24), ("mem_norm", 8), ("a_q_norm", 1), ("a_k_norm", 1),
             ("a_subln", 1), ("b_q_norm", 1), ("b_k_norm", 1), ("c_q_norm", 1), ("c_k_norm", 1)]
    for l in range(LAYERS):
        names += [(f"ffn1_norm_2_{l}", 8), (f"mix_norm_2_{l}", 8), (f"hgrn_norm_2_{l}", 4), (f"pool_scale_2_{l}", 4),
                  (f"xa_norm_2_{l}", 8), (f"mem_norm_2_{l}", 8), (f"ffn2_norm_2_{l}", 8), (f"lb_logits_2_{l}", 4)]
    names += [("final_norm_2", 8), ("lambdas", 4)]
    for name, n in names:
        plan[name] = (at, n)
        at += n
    return plan, at


COLS, NCOL = column_plan()


class Schedule:

    def __init__(self):
        self.steps = []
        self.units = []
        self.njobs = 0
        self.nsq = 0
        self.sq_reader = {}
        self.last_sum = None
        self.nbias = 0

    def step(self, kind, /, **a):
        if kind in ("refresh", "memfresh", "hnorm"):
            a["sq"] = self.nsq % 2
            a["sq_free"] = self.sq_reader.get(a["sq"])
            self.nsq += 1
            self.sq_reader[a["sq"]] = (("hsum", a["id"]) if kind == "hnorm" else
                                       ("xs" if kind == "refresh" else "ms", (a["n"], a["m"])))
        if kind in ("refresh", "memfresh") and a["m"] == 0:
            a["ssum_free"] = self.last_sum
        if kind in ("rstd", "rstdm"):
            self.last_sum = ("sum", (kind, a["n"]))
        if kind == "bias":
            self.nbias += 1
        if kind == "score":
            a["nbias"] = self.nbias
        self.steps.append((kind, a))

    def unit(self, name, l, tiles):
        self.units.append((name, l, tiles))

    def job(self, tile0, nk, /, **a):
        self.step("job", j=self.njobs, tile0=tile0, nk=nk, **a)
        self.njobs += 1
        return self.njobs - 1

    def column(self, name, l, column, /, **a):
        t0 = len(self.units) * UT
        self.unit(name, l, [(k, column) for k in range(DC)])
        return self.job(t0, DC, **a)


def build_schedule():
    s = Schedule()
    step, column = s.step, s.column
    step("setup")
    for m in range(DC):
        step("refresh", n=0, m=m, gain="norm_mix")
    step("rstd", n=0)

    def hnorm(id, src, gain, ones, n, dim, need):
        step("hnorm", id=id, src=src, gain=gain, ones=ones, n=n, dim=dim, need=need)

    needx = {k: [("xl", (0, k))] for k in range(DC)}
    for h in range(NHEAD):
        for w, (c, g) in enumerate((("Q", "a_q_norm"), ("K", "a_k_norm"))):
            j = column("w_in", 0, 4 * w + h, rhs="x", n=T, evac="scale", dst=("A" + c, h), need=needx)
            needx = {}
            hnorm(("A" + c, h), ("A" + c, h), g, "halves", T, 64, [("evac", j)])
        j = column("w_in", 0, 8 + h, rhs="x", n=T, evac="scale", dst=("VT", h % 2), free=[("v", ("A", h - 2))] if h >= 2 else [])
        step("vturn", id=("A", h), src=("VT", h % 2), nt=NT, dst=("AV", h), need=("evac", j))
    gates = iter(range(DC))

    def gate_chunk(n, m, dst, free=()):
        j = column("w_gate", 0, 8 * n + m, rhs="x", n=T, evac="scale", dst=dst, free=list(free))
        step("gate", n=n, m=m, dst=dst, need=("evac", j))

    tiles = [dict(kind="A", h=h, t=t, need=[("hn", ("AQ", h)), ("hn", ("AK", h))], need_v=[("v", ("A", h))])
             for h in range(NHEAD) for t in range(NT)]
    i = 0

    def attend(tiles, fill, need_first=()):
        nonlocal i
        for k, a in enumerate(tiles):
            a["i"] = i
            if a["t"] == 0 and a["kind"] in "AB":
                step("bias", kind=a["kind"], h=a["h"], after=("nmax", i - 1) if i else None)
            step("score", **a)
            if k:
                step("turn", **tiles[k - 1])
                fill()
                if a["t"] == 0:
                    step("pv", **tiles[k - 1])
            i += 1
        step("turn", **tiles[-1])
        fill()
        step("pv", **tiles[-1])

    def fill_a():
        m = next(gates, None)
        if m is not None:
            gate_chunk(0, m, ("Y", m))

    attend(tiles, fill_a)
    for m in gates:
        gate_chunk(0, m, ("Y", m))
    for h in range(NHEAD):
        hnorm(("AO", h), ("AO", h), "a_subln", "ones", T, P, [("pvd", ("A", h))])
        step("split", id=("A", h), src=("AO", h), dst=("OA", h), need=[("hn", ("AO", h))])

    def branch(n, o):
        for jj in range(DC // 2):
            if n:
                for m in (2 * jj, 2 * jj + 1):
                    gate_chunk(n, m, ("GT", m % 2))
            t0 = len(s.units) * UT
            s.unit("w_branch", n, [(k, 2 * jj + mm) for mm in range(2) for k in range(4)])
            for mm in range(2):
                m = 2 * jj + mm
                need = {k: [("olo", ("ABC"[n], k))] for k in range(4)} if m == 0 else {}
                s.job(t0 + 4 * mm, 4, rhs=o, n=T, evac="branch", b=n, m=m, need=need)

    branch(0, "OA")

    def b_jobs(h):
        out = []
        for g in range(3):
            for w, (c, gain) in enumerate((("Q", "b_q_norm"), ("K", "b_k_norm"))):
                def go(g=g, w=w, c=c, gain=gain):
                    dst = (f"B{c}{h % 2}", g)
                    free = [("score", b_tiles[h - 2][-1]["i"])] if h >= 2 else []
                    j = column("w_in", 0, 12 + 12 * w + 4 * g + h, rhs="x", n=T, evac="scale", dst=dst, free=free)
                    hnorm((f"B{c}{g}", h), dst, gain, "ones", T, P, [("evac", j)])
                out.append(go)

            def go(g=g):
                free = [("v", ("B", h, g - 1))] if g else ([("v", ("B", h - 1, 2))] if h else [("v", ("A", 3))])
                j = column("w_in", 0, 36 + 4 * g + h, rhs="x", n=T, evac="scale", dst=("VT", g % 2), free=free)
                step("vturn", id=("B", h, g), src=("VT", g % 2), nt=NT, dst=(f"BV{h % 2}", g), need=("evac", j),
                     dfree=[("pv", b_tiles[h - 2][-1]["i"])] if h >= 2 else [])
            out.append(go)
        return out

    b_tiles = [[dict(kind="B", h=h, t=t, need=[("hn", (f"B{c}{g}", h)) for c in "QK" for g in range(3)],
                     need_v=[("v", ("B", h, g)) for g in range(3)]) for t in range(NT)] for h in range(NHEAD)]
    for go in b_jobs(0):
        go()
    for h in range(NHEAD):
        todo = b_jobs(h + 1) if h + 1 < NHEAD else []

        def fill_b():
            for _ in range(3):
                if todo:
                    todo.pop(0)()
        attend(b_tiles[h], fill_b)
        while todo:
            todo.pop(0)()
    branch(1, "OB")

    def memory(n, load, gain):
        step("memload", n=n, which=load, after=("evac", s.njobs - 1))
        for m in range(DC):
            step("memfresh", n=n, m=m, gain=gain)
        step("rstdm", n=n)

    memory(0, 0, "mem_norm")
    for h in range(NHEAD):
        j = column("w_in", 0, 48 + h, rhs="x", n=T, evac="scale", dst=("CQ", h))
        hnorm(("CQ", h), ("CQ", h), "c_q_norm", "ones", T, P, [("evac", j)])
    needm = {k: [("ml", (0, k))] for k in range(DC)}
    for h in range(NHEAD):
        j = column("w_mem_kv", 0, h, rhs="mem", n=NM, evac="scalem", dst=("CK", h), need=needm)
        needm = {}
        hnorm(("CK", h), ("CK", h), "c_k_norm", "ones", NM, P, [("evac", j)])
        j = column("w_mem_kv", 0, 4 + h, rhs="mem", n=NM, evac="scalem", dst=("VT", h % 2),
                   free=[("v", ("C", h - 2))] if h >= 2 else [("v", ("B", 3, 2))])
        step("vturn", id=("C", h), src=("VT", h % 2), nt=NM // P, dst=("CV", h), need=("evac", j))
    attend([dict(kind="C", h=h, t=t, need=[("hn", ("CQ", h)), ("hn", ("CK", h))], need_v=[("v", ("C", h))])
            for h in range(NHEAD) for t in range(NT)], lambda: None)
    branch(2, "OC")
    step("reload")
    norm = 1
    for m in range(DC):
        need = {k: [("ylo", k)] for k in range(DC)} if m == 0 else {}
        j = column("w_out", 0, m, rhs="y", n=T, evac="resid", m=m, c=1.0, need=need)
        step("refresh", n=norm, m=m, gain="norm_ffn", need=("evac", j))
    step("rstd", n=norm)

    def ffn(w1, w3, w2, l, c, n, gain_next, back=False):
        t0 = len(s.units) * UT
        for f in range(NF):
            for w in (w1, w3):
                s.unit(w, l, [(k, f) for k in range(DC)])
        step("ffn", n=n, unit0=t0 // UT)
        t1 = len(s.units) * UT
        order = [(k, m) for m in range(DC) for k in range(NF)]
        for u in range(0, len(order), UT):
            s.unit(w2, l, order[u:u + UT])
        for m in range(DC):
            j = s.job(t1 + m * NF, NF, rhs="h", n=T, evac="back" if back else "resid", m=m, c=c, first=(m == 0), norm=n)
            step("refresh", n=n + 1, m=m, gain=gain_next, need=("x", m) if back else ("evac", j))
        step("rstd", n=n + 1)

    ffn("w_ffn_gate", "w_ffn_up", "w_ffn_down", 0, 1.0, 1, "ffn1_norm_2_0", back=True)
    norm = 2

    for l in range(LAYERS):
        ffn("ffn1_w1_2", "ffn1_w3_2", "ffn1_w2_2", l, 0.5, norm, f"mix_norm_2_{l}")
        norm += 1
        needx = {k: [("xl", (norm, k))] for k in range(DC)}

        def pair_jobs(pr, between=()):
            nonlocal needx
            between = list(between)
            for hh in range(2):
                h = 2 * pr + hh
                for w, c in enumerate(("HQ", "HF", None, "HG")):
                    if c:
                        column("w_in_2", l, 4 * w + h, rhs="x", n=T, evac="scale", dst=(f"{c}{pr}", hh), need=needx)
                        needx = {}
                    else:
                        free = [("v", (l, h - 2))] if h >= 2 else []
                        j = column("w_in_2", l, 8 + h, rhs="x", n=T, evac="scale", dst=("HVT", hh), free=free)
                        step("vturn", id=(l, h), src=("HVT", hh), nt=NT, dst=(f"HV{pr}", hh), need=("evac", j))
                    if between:
                        between.pop(0)()
            step("hprep", l=l, pr=pr, need=("evac", s.njobs - 1))

        def pool_job(g):
            column("w_in_2", l, 16 + g, rhs="x", n=T, evac="scale", dst=("U", 0))
            step("poolsum", l=l, g=g)

        def pool_rest(g):
            step("pool", l=l, g=g)
            step("split", id=("M", l, 4 + g), src=("U", 1), dst=("MIX", 4 + g), need=[("pooled", (l, g))])

        step("poolload", l=l, after=("evac", s.njobs - 1))
        pair_jobs(0, [w for g in range(4) for w in (lambda g=g: pool_job(g), lambda g=g: pool_rest(g))])
        for pr in range(2):
            for li in range(10):
                step("level", l=l, pr=pr, li=li)
            if pr == 0:
                pair_jobs(1)
            for hh in range(2):
                h = 2 * pr + hh
                step("hout", l=l, pr=pr, hh=hh)
                hnorm(("H", l, h), ("HO", hh), f"hgrn_norm_2_{l}:{h}", "ones", T, P, [("ho", (l, h))])
                step("hgate", l=l, pr=pr, hh=hh)
                step("split", id=("M", l, h), src=("HO", hh), dst=("MIX", h), need=[("hgated", (l, h))])
        norm += 1
        for m in range(DC):
            need = {k: [("olo", ("M", l, k))] for k in range(DC)} if m == 0 else {}
            j = column("w_out_2", l, m, rhs="mix", n=T, evac="resid", m=m, c=1.0, need=need)
            step("refresh", n=norm, m=m, gain=f"xa_norm_2_{l}", need=("evac", j))
        step("rstd", n=norm)
        memory(1 + l, 1, f"mem_norm_2_{l}")
        needx, jq, jk = {k: [("xl", (norm, k))] for k in range(DC)}, [], []
        for c in range(DC):
            jq.append(column("xa_wq_2", l, c, rhs="x", n=T, evac="scale", dst=("XQ", c), need=needx))
            needx = {}
        needm = {k: [("ml", (1 + l, k))] for k in range(DC)}
        for c in range(DC):
            jk.append(column("xa_wkv_2", l, c, rhs="mem", n=NM, evac="scalem", dst=("XK", c), need=needm))
            needm = {}
        for c in range(DC):
            free = [("v", ("X", l, c - 2))] if c >= 2 else [("v", (l, 3))]
            j = column("xa_wkv_2", l, 8 + c, rhs="mem", n=NM, evac="scalem", dst=("VT", c % 2), free=free)
            step("vturn", id=("X", l, c), src=("VT", c % 2), nt=NM // P, dst=("XV", c), need=("evac", j))
        attend([dict(kind="X", h=h, t=t, l=l, need=[("evac", jq[2 * h + 1]), ("evac", jk[2 * h + 1])],
                     need_v=[("v", ("X", l, 2 * h + 1))]) for h in range(NHEAD) for t in range(NT)], lambda: None)
        norm += 1
        for m in range(DC):
            need = {k: [("olo", ("X", l, k))] for k in range(DC)} if m == 0 else {}
            j = column("xa_wo_2", l, m, rhs="xo", n=T, evac="resid", m=m, c=1.0, need=need)
            step("refresh", n=norm, m=m, gain=f"ffn2_norm_2_{l}", need=("evac", j))
        step("rstd", n=norm)
        last = l == LAYERS - 1
        ffn("ffn2_w1_2", "ffn2_w3_2", "ffn2_w2_2", l, 0.5, norm, "final_norm_2" if last else f"ffn1_norm_2_{l + 1}")
        norm += 1
    step("final", n=norm)
    return s


SCHEDULE = build_schedule()
NU = len(SCHEDULE.units)


class Counts:

    def __init__(self, known=None):
        self.known = known
        self.now = {}
        self.at = {}

    def mark(self, name, key, n=1):
        self.now[name] = self.now.get(name, 0) + n
        self.at[(name, key)] = self.now[name]

    def value(self, name, key):
        if self.known is None:
            return 1
        return self.known[(name, key)]


RAISES = {
    "pe": ["unit_free", "job_mid", "sum", "hsum", "score", "turned", "vt", "pv", "lev", "ho_mm", "pool_mm", "lam_mm"],
    "act": ["sq", "xh", "sd", "msq", "mh", "msd", "hsq", "hsd", "exp", "pt", "v", "ohi", "gate", "yhi", "silu",
            "sigm", "lam_exp", "lb_exp", "hgs"],
    "dve": ["setup", "xs", "xl", "rstd", "ms", "ml", "rstdm", "evac", "x", "hrec", "hn", "max", "nmax", "pn", "pvd",
            "olo", "y", "ylo", "fg", "fu", "fm", "fhh", "fhl", "fin", "hprep", "qkt", "lvd", "ho", "hgated",
            "pooled", "ptmp"],
    "pool": ["unit_hi", "unit_ready"],
}
DMAS = ["d_x", "d_consts", "d_bias", "d_mem", "d_reload", "d_poolw", "d_out"]


def program(nc, dram, counts):
    ctx = ExitStack()
    with ctx:
        sems = {n: ctx.enter_context(nc.semaphore(n)) for ns in RAISES.values() for n in ns}
        sems.update({n: ctx.enter_context(nc.semaphore(n)) for n in DMAS})
        raw_landed = [ctx.enter_context(nc.semaphore(f"raw_landed{k}")) for k in range(RAW)]
        engine_of = {n: e for e, ns in RAISES.items() for n in ns}
        last = {}

        def sig(name, key=None):
            counts.mark(name, key)
            last[engine_of[name]] = (sems[name], counts.now[name])
            return sems[name], 1

        def on(name, key=None):
            return sems[name], counts.value(name, key)

        def own(engine):
            return last[engine]

        base = (nc.sbuf_base + 31) // 32 * 32
        top = [base]

        def fixed(name, shape, dt=F32):
            size = int(np.prod(shape[1:])) * (1 if dt == U8 else 4)
            t = nc.alloc_sbuf_tensor_at(name, shape, dt, offset=top[0])
            top[0] += (size + 31) // 32 * 32
            return t

        raw = [fixed(f"raw{k}", [P, UT * P]) for k in range(RAW)]
        whi = [fixed(f"whi{k}", [P, UT * P], F32R) for k in range(RING)]
        wlo = [fixed(f"wlo{k}", [P, UT * P], F32R) for k in range(RING)]
        X = fixed("x_res", [P, DC, T])
        XH = fixed("x_hi", [P, DC, T], F32R)
        XL = fixed("x_lo", [P, DC, T], F32R)
        RSTD = fixed("rstd_x", [P, T])
        RSTDM = fixed("rstd_mem", [P, NM])
        SSUM = fixed("sq_sum", [P, T])
        SQ = fixed("sq", [P, 2, T])
        cols = fixed("cols", [P, NCOL])
        ones = fixed("ones", [P, P])
        halves = fixed("halves", [P, P])
        ident = fixed("ident", [P, P])
        masks = fixed("masks", [P, 7, P], U8)
        poolrec = fixed("poolrec", [P, 4, 16])
        small = fixed("small", [P, 64])
        arena = top[0]

        def area(name, kb, shape, dt=F32):
            size = int(np.prod(shape[1:])) * 4
            assert arena + kb * KB + size <= nc.sbuf_usable_end, (name, kb, size, nc.sbuf_usable_end - arena)
            return nc.alloc_sbuf_tensor_at(name, shape, dt, offset=arena + int(kb * KB))

        masks_f = area("masks_f", 0, [P, 7, P])
        AQ, AK, AV = (area(n, o, [P, NHEAD, T]) for n, o in (("a_q", 0), ("a_k", 8), ("a_v", 16)))
        AO = area("a_out", 42, [P, NHEAD, T])
        OAH, OAL = (area(n, o, [P, NHEAD, T], F32R) for n, o in (("oa_hi", 0), ("oa_lo", 8)))
        BQ = [area(f"b_q{s}", o, [P, 3, T]) for s, o in ((0, 24), (1, 0))]
        BK = [area(f"b_k{s}", o + 6, [P, 3, T]) for s, o in ((0, 24), (1, 0))]
        BV = [area(f"b_v{s}", o + 12, [P, 3, T]) for s, o in ((0, 24), (1, 0))]
        OBH, OBL = (area(n, o, [P, NHEAD, T], F32R) for n, o in (("ob_hi", 42), ("ob_lo", 50)))
        BIAS = area("bias", 58, [P, NT * 768])
        CQ = area("c_q", 0, [P, NHEAD, T])
        CK = area("c_k", 8, [P, NHEAD, NM])
        CV = area("c_v", 12, [P, NHEAD, NM])
        OCH, OCL = (area(n, o, [P, NHEAD, T], F32R) for n, o in (("oc_hi", 16), ("oc_lo", 24)))
        MRAW = area("mem_raw", 48, [P, DC, NM])
        MH, ML = (area(n, o, [P, DC, NM], F32R) for n, o in (("mem_hi", 32), ("mem_lo", 40)))
        SP = area("probs", 70, [P, 2, 1024])
        PT = area("probs_t", 78, [P, 6, T])
        SD = area("sd", 90, [P, T])
        REC = area("rec", 92, [P, T])
        VT = area("vt_sb", 94, [P, 2, T])
        GT = area("gate_sb", 98, [P, 2, T])
        HH, HL = (area(n, o, [P, NF, T], F32R) for n, o in (("h_hi", 0), ("h_lo", 44)))
        FG, FU, FS, FM = (area(n, o, [P, T]) for n, o in (("ffn_g", 88), ("ffn_u", 90), ("ffn_s", 92), ("ffn_m", 94)))
        HQ = [area(f"h_q{s}", o, [P, 2, T]) for s, o in ((0, 0), (1, 42))]
        HF = [area(f"h_f{s}", o, [P, 2, T]) for s, o in ((0, 4), (1, 46))]
        HK = area("h_k", 8, [P, 2, T])
        HS = area("h_suf", 12, [P, 2, T])
        QT, KT = (area(n, o, [P, 2, T]) for n, o in (("h_qt", 16), ("h_kt", 20)))
        HG = [area(f"h_g{s}", o, [P, 2, T]) for s, o in ((0, 24), (1, 50))]
        HV = [area(f"h_v{s}", o, [P, 2, T]) for s, o in ((0, 28), (1, 54))]
        AD = area("h_ad", 32, [P, 2, NT, P])
        A128 = area("h_a128", 36, [P, 2, 2, P])
        A256 = area("h_a256", 38, [P, 2, 2, 2 * P])
        HVT = area("hvt_sb", 58, [P, 2, T])
        MIXH, MIXL = (area(n, o, [P, DC, T], F32R) for n, o in (("mix_hi", 62), ("mix_lo", 78)))
        UB = area("pool_u", 94, [P, 3, T])
        HSD, HREC, HO = area("h_sd", 100, [P, T]), area("h_rec", 20, [P, T]), area("h_o", 16, [P, 2, T])
        PW = area("pool_w_sb", 38, [P, 4, P])
        XQ = area("x_q", 0, [P, DC, T])
        XK = area("x_k", 16, [P, DC, NM])
        XV = area("x_v", 24, [P, DC, NM])
        XOH, XOL = (area(n, o, [P, DC, T], F32R) for n, o in (("xo_hi", 32), ("xo_lo", 48)))
        YH, YL = (area(n, o, [P, DC, T], F32R) for n, o in (("y_hi", 32), ("y_lo", 48)))

        bufs = {"AQ": AQ, "AK": AK, "AV": AV, "AO": AO, "VT": VT, "GT": GT, "Y": X, "CQ": CQ, "CK": CK, "CV": CV,
                "BQ0": BQ[0], "BQ1": BQ[1], "BK0": BK[0], "BK1": BK[1], "BV0": BV[0], "BV1": BV[1],
                "HQ0": HQ[0], "HQ1": HQ[1], "HF0": HF[0], "HF1": HF[1], "HG0": HG[0], "HG1": HG[1],
                "HV0": HV[0], "HV1": HV[1], "HVT": HVT, "HO": HO, "U": UB, "XQ": XQ, "XK": XK, "XV": XV}
        parts = {"x": (XH, XL), "h": (HH, HL), "mem": (MH, ML), "OA": (OAH, OAL), "OB": (OBH, OBL),
                 "OC": (OCH, OCL), "mix": (MIXH, MIXL), "xo": (XOH, XOL), "y": (YH, YL)}

        def buf(where):
            return bufs[where[0]][:, where[1], :]

        def col(name, m=0):
            return cols[:, COLS[name][0] + m:COLS[name][0] + m + 1]

        def gain_of(name):
            base, _, m = name.partition(":")
            return col(base, int(m or 0))

        LAM = small[:, 4:5]

        def lb(l, m):
            return small[:, 28 + 8 * l + m:29 + 8 * l + m]

        def one_minus_lb(l, m):
            return small[:, 32 + 8 * l + m:33 + 8 * l + m]

        def pair_of(first, i):
            return small[:, first + 2 * (i % 2):first + 2 * (i % 2) + 2]

        PS = ctx.enter_context(nc.psum_tensor("ps", [P, 8, T], F32))
        flat = PS[:, :, :].rearrange("p b n -> p (b n)")
        S = flat[:, 0:2 * T]
        TR = flat[:, 2 * T:4 * T]
        O = PS[:, 7, :]

        def bank(j):
            return PS[:, 4 + j % 3, :]

        def job_done(a):
            end = a["tile0"] + a["nk"]
            return on("unit_free", end // UT - 1) if end % UT == 0 else on("job_mid", a["j"])

        jobs = [a for k, a in SCHEDULE.steps if k == "job"]
        kinds = {"A": 4, "B": 6, "C": 2, "X": 2}

        def out_key(a):
            return ("X", a["l"], 2 * a["h"]) if a["kind"] == "X" else (a["kind"], a["h"])

        block = ctx.enter_context(nc.Block())

        @block.sync
        def _(sp):
            sp.dma_start(X[:, :, :], dram["x"]).then_inc(sems["d_x"], 16)
            step = RAW * RING

            def load(i, c):
                if not (isinstance(i, int) and i * step + c < RAW):
                    sp.wait_ge(sems["unit_ready"], i * step + (c - RAW + 1))
                src = dram["weights"][bass.ds(i * step + c, 1)].rearrange("a p n -> (a p) n")
                sp.dma_start(raw[c % RAW][:, :], src).then_inc(raw_landed[c % RAW], 16)

            for c in range(step):
                load(0, c)
            with sp.Fori(1, NU // step) as i:
                for c in range(step):
                    load(i, c)
            assert NU % step
            for c in range(NU % step):
                load(NU // step, c)
            for m in range(DC):
                sp.wait_ge(*on("fin", m))
                sp.dma_start(dram["out"][:, m, :], X[:, m, :]).then_inc(sems["d_out"], 16)
            sp.wait_ge(sems["d_out"], 16 * DC)

        @block.gpsimd
        def _(pool):
            step = RAW * RING

            def await_unit(i, c):
                pool.wait_ge(raw_landed[c % RAW], (i * RING + (c // RAW + 1)) * 16)
                if not (isinstance(i, int) and i * step + c < RING):
                    pool.wait_ge(sems["unit_free"], i * step + (c - RING + 1))

            def high(c):
                pool.tensor_scalar(whi[c % RING][:, :], raw[c % RAW][:, :], 1.0, 0.0, ALU.mult,
                                   ALU.add).then_inc(sems["unit_hi"], 1)

            def split(i, c, more=True):
                if more:
                    await_unit(i, c + 1)
                pool.wait_ge(sems["unit_hi"], i * step + (c + 1))
                pool.tensor_tensor(wlo[c % RING][:, :], raw[c % RAW][:, :], whi[c % RING][:, :].bitcast(F32),
                                   ALU.subtract).then_inc(sems["unit_ready"], 1)
                if more:
                    high(c + 1)

            await_unit(0, 0)
            high(0)
            for c in range(step):
                split(0, c)
            with pool.Fori(1, NU // step) as i:
                for c in range(step):
                    split(i, c)
            for c in range(NU % step):
                split(NU // step, c, c + 1 < NU % step)

        @block.tensor
        def _(pe):
            free = {}

            def wait_free(slot):
                if slot in free:
                    pe.wait_ge(*on(*free[slot]))

            def three(out, hi, lo, xhi, xlo, start, stop):
                pe.matmul(out, hi, xhi, start=start, stop=False)
                pe.matmul(out, hi, xlo, start=False, stop=False)
                return pe.matmul(out, lo, xhi, start=False, stop=stop)

            for kind, a in SCHEDULE.steps:
                if kind == "setup":
                    pe.wait_ge(sems["d_consts"], 96)
                    pe.wait_ge(*on("setup", "prod"))
                    pe.matmul(O[:, 0:2], ones[0:64, :], small[0:64, 0:2], start=True, stop=True)\
                        .then_inc(*sig("lam_mm"))
                    free["O"] = ("lam_exp", None)
                elif kind in ("rstd", "rstdm"):
                    mem = kind == "rstdm"
                    n = NM if mem else T
                    pe.wait_ge(*on("ms" if mem else "xs", (a["n"], DC - 1)))
                    wait_free("O")
                    pe.matmul(O[:, 0:n], ones[:, :], SSUM[:, 0:n], start=True, stop=True)\
                        .then_inc(*sig("sum", (kind, a["n"])))
                    free["O"] = ("msd" if mem else "sd", a["n"])
                elif kind == "job":
                    xhi, xlo = parts[a["rhs"]]
                    n = a["n"]
                    out = bank(a["j"])[:, 0:n]
                    if a["j"] >= 3:
                        pe.wait_ge(*on("evac", a["j"] - 3))
                    for k in range(a["nk"]):
                        tile = a["tile0"] + k
                        c = tile % UT
                        if c == 0 or k == 0:
                            pe.wait_ge(sems["unit_ready"], tile // UT + 1)
                        for key in a.get("need", {}).get(k, []):
                            pe.wait_ge(*on(*key))
                        if a.get("first"):
                            pe.wait_ge(sems["fhl"], counts.value("fhl", ("base", a["norm"])) + k + 1)
                        hi = whi[tile // UT % RING][:, c * P:(c + 1) * P]
                        lo = wlo[tile // UT % RING][:, c * P:(c + 1) * P]
                        mm = three(out, hi, lo, xhi[:, k, 0:n], xlo[:, k, 0:n], k == 0, k == a["nk"] - 1)
                        if c == UT - 1:
                            mm.then_inc(*sig("unit_free", tile // UT))
                        elif k == a["nk"] - 1:
                            mm.then_inc(*sig("job_mid", a["j"]))
                elif kind == "hnorm":
                    pe.wait_ge(*on("hsq", a["id"]))
                    wait_free("O")
                    lhs = halves if a["ones"] == "halves" else ones
                    pe.matmul(O[:, 0:a["n"]], lhs[:, :], SQ[:, a["sq"], 0:a["n"]], start=True, stop=True)\
                        .then_inc(*sig("hsum", a["id"]))
                    free["O"] = ("hsd", a["id"])
                elif kind == "vturn":
                    pe.wait_ge(*on(*a["need"]))
                    wait_free("T")
                    src = buf(a["src"])
                    for t in range(a["nt"]):
                        mm = pe.transpose(TR[:, t * P:(t + 1) * P], src[:, t * P:(t + 1) * P], ident[:, :])
                    mm.then_inc(*sig("vt", a["id"]))
                    free["T"] = ("v", a["id"])
                elif kind == "score":
                    i, h, t, what = a["i"], a["h"], a["t"], a["kind"]
                    if t == 0:
                        for key in a["need"]:
                            pe.wait_ge(*on(*key))
                    wait_free("S")
                    tt = slice(t * P, (t + 1) * P)
                    if what == "A":
                        for c in range(2):
                            r = slice(64 * c, 64 * c + 64)
                            mm = pe.matmul(S[:, c * T:(c + 1) * T], AQ[r, h, tt], AK[r, h, :], start=True, stop=True)
                    elif what == "B":
                        q, k = BQ[h % 2], BK[h % 2]
                        pe.matmul(S[:, 0:T], q[:, 0, tt], k[:, 0, :], start=True, stop=True)
                        for g in (1, 2):
                            o = T + (g - 1) * P
                            mm = pe.matmul(S[:, o:o + P], q[:, g, tt], k[:, g, tt], start=True, stop=True)
                    elif what == "C":
                        mm = pe.matmul(S[:, 0:NM], CQ[:, h, tt], CK[:, h, :], start=True, stop=True)
                    else:
                        for c in range(2):
                            mm = pe.matmul(S[:, 0:NM], XQ[:, 2 * h + c, tt], XK[:, 2 * h + c, :],
                                           start=(c == 0), stop=(c == 1))
                    mm.then_inc(*sig("score", i))
                    free["S"] = ("nmax", i) if what in "AB" else ("exp", i)
                elif kind == "turn":
                    i = a["i"]
                    pe.wait_ge(*on("pn", i))
                    wait_free("T")
                    for c in range(kinds[a["kind"]]):
                        mm = pe.transpose(TR[:, c * P:(c + 1) * P], SP[:, i % 2, c * P:(c + 1) * P], ident[:, :])
                    mm.then_inc(*sig("turned", i))
                    free["T"] = ("pt", i)
                elif kind == "pv":
                    i, h, what = a["i"], a["h"], a["kind"]
                    pe.wait_ge(*on("pt", i))
                    for key in a["need_v"]:
                        pe.wait_ge(*on(*key))
                    wait_free("O")
                    if what == "A":
                        for c in range(NT):
                            mm = pe.matmul(O, AV[:, h, c * P:(c + 1) * P], PT[:, c, :], start=(c == 0), stop=(c == NT - 1))
                    elif what == "B":
                        v = BV[h % 2]
                        pe.matmul(O, v[:, 0, 0:P], PT[:, 0, :], start=True, stop=False)
                        for g in (1, 2):
                            for c in range(NT):
                                tt = slice(c * P, (c + 1) * P)
                                pe.matmul(O[:, tt], v[:, g, tt], PT[:, 3 + g, tt], start=False, stop=False,
                                          skip_group_check=True)
                        for c in range(1, NT):
                            mm = pe.matmul(O, v[:, 0, c * P:(c + 1) * P], PT[:, c, :], start=False, stop=(c == NT - 1))
                    elif what == "C":
                        for c in range(2):
                            mm = pe.matmul(O, CV[:, h, c * P:(c + 1) * P], PT[:, c, :], start=(c == 0), stop=(c == 1))
                    else:
                        for c in range(2):
                            mm = pe.matmul(O, XV[:, 2 * h, c * P:(c + 1) * P], PT[:, c, :], start=(c == 0), stop=(c == 1))
                        mm.then_inc(*sig("pv", (i, 0)))
                        wait_free("T")
                        for c in range(2):
                            mm = pe.matmul(TR[:, 0:T], XV[:, 2 * h + 1, c * P:(c + 1) * P], PT[:, c, :],
                                           start=(c == 0), stop=(c == 1))
                        free["T"] = ("olo", ("X", a["l"], 2 * h + 1))
                    mm.then_inc(*sig("pv", i))
                    free["O"] = ("pvd", ("A", h)) if what == "A" else ("olo", out_key(a))
                elif kind == "ffn":
                    n, u0 = a["n"], a["unit0"]
                    fg0, fu0 = counts.value("fg", ("base", n)), counts.value("fu", ("base", n))
                    for slot in "ST":
                        wait_free(slot)

                    def gate_up(i):
                        for jj in range(2):
                            for w, (name, first) in enumerate((("fg", fg0), ("fu", fu0))):
                                c = 2 * jj + w
                                pe.wait_ge(sems["unit_ready"], i * 4 + (u0 + c + 1))
                                if not isinstance(i, int):
                                    pe.wait_ge(sems[name], i * 2 + (first + jj - 1))
                                for k in range(DC):
                                    if isinstance(i, int) and jj == 0 and w == 0:
                                        pe.wait_ge(*on("xl", (n, k)))
                                    cc = slice(k * P, (k + 1) * P)
                                    r = (u0 + c) % RING
                                    mm = three(PS[:, c, :], whi[r][:, cc], wlo[r][:, cc], XH[:, k, :], XL[:, k, :],
                                               k == 0, k == DC - 1)
                                mm.then_inc(sems["unit_free"], 1)

                    gate_up(0)
                    with pe.Fori(1, NF // 2) as i:
                        gate_up(i)
                    for u in range(2 * NF):
                        counts.mark("unit_free", u0 + u)
                    free["S"] = free["T"] = ("fu", ("end", n))
                elif kind == "level":
                    l, pr, li = a["l"], a["pr"], a["li"]
                    slot, out = ("S", S) if li % 2 == 0 else ("T", TR)
                    pe.wait_ge(*on("hprep", (l, pr)) if li == 0 else on("qkt", (l, pr, li)))
                    wait_free(slot)
                    q, k = (HQ[pr], HK) if li == 0 else (QT, KT)
                    for hh in range(2):
                        o = hh * T
                        if li <= 7:
                            pairs = [(c, c, c + 1, c) for c in range(NT)]
                        elif li == 8:
                            pairs = [(0, 1, 2, 0), (2, 3, 4, 1)]
                        else:
                            pairs = [(0, 2, 4, 0), (1, 2, 4, 2)]
                        for sc, t0, t1, at in pairs:
                            w = (t1 - t0) * P
                            mm = pe.matmul(out[:, o + at * P:o + at * P + w], k[:, hh, sc * P:(sc + 1) * P],
                                           q[:, hh, t0 * P:t1 * P], start=True, stop=True)
                    mm.then_inc(*sig("lev", (l, pr, li)))
                    free[slot] = ("lvd", (l, pr, li))
                elif kind == "hout":
                    l, pr, hh = a["l"], a["pr"], a["hh"]
                    pe.wait_ge(*on("lvd", (l, pr, 9)))
                    pe.wait_ge(*on("v", (l, 2 * pr + hh)))
                    wait_free("O")
                    v = HV[pr][:, hh, :]
                    near, far = A128[:, hh, :, :], A256[:, hh, :, :]
                    terms = [[(0, AD[:, hh, 0, :])],
                             [(1, AD[:, hh, 1, :]), (0, near[:, 0, :])],
                             [(2, AD[:, hh, 2, :]), (0, far[:, 0, 0:P]), (1, far[:, 1, 0:P])],
                             [(3, AD[:, hh, 3, :]), (2, near[:, 1, :]), (0, far[:, 0, P:2 * P]), (1, far[:, 1, P:2 * P])]]
                    for t, group in enumerate(terms):
                        for x, (sc, w) in enumerate(group):
                            mm = pe.matmul(O[:, t * P:(t + 1) * P], v[:, sc * P:(sc + 1) * P], w, start=(x == 0),
                                           stop=(x == len(group) - 1))
                    mm.then_inc(*sig("ho_mm", (l, 2 * pr + hh)))
                    free["O"] = ("ho", (l, 2 * pr + hh))
                elif kind == "pool":
                    l, g = a["l"], a["g"]
                    pe.wait_ge(*on("ptmp", (l, g)))
                    pe.wait_ge(sems["d_poolw"], 16 * (l + 1))
                    wait_free("O")
                    pe.matmul(O, PW[:, g, :], UB[:, pool_slot(g), :], start=True, stop=True).then_inc(*sig("pool_mm", (l, g)))
                    free["O"] = ("pooled", (l, g))

        @block.scalar
        def _(act):
            def copy(out, in_, scale=1.0):
                return act.activation(out, in_, ACT.Copy, scale=scale)

            sd_reader = [None]
            for kind, a in SCHEDULE.steps:
                if kind == "setup":
                    for t, name in ((cols, "cols"), (ones, "ones"), (halves, "halves"), (ident, "ident"),
                                    (masks_f, "masks"), (poolrec, "poolrec")):
                        act.dma_start(t[tuple([slice(None)] * len(t.shape))], dram[name]).then_inc(sems["d_consts"], 16)
                    act.wait_ge(*on("lam_mm"))
                    act.activation(small[:, 2:4], O[:, 0:2], ACT.Exp).then_inc(*sig("lam_exp"))
                    act.wait_ge(*on("setup", "lbd"))
                    act.activation(small[:, 12:20], small[:, 12:20], ACT.Exp).then_inc(*sig("lb_exp"))
                elif kind == "refresh":
                    n, m = a["n"], a["m"]
                    if n == 0:
                        act.wait_ge(sems["d_x"], 16)
                        act.wait_ge(sems["d_consts"], 96)
                    else:
                        act.wait_ge(*on(*a["need"]))
                    if a["sq_free"]:
                        act.wait_ge(*on(*a["sq_free"]))
                    act.activation(SQ[:, a["sq"], :], X[:, m, :], ACT.Square).then_inc(*sig("sq", (n, m)))
                    if a["gain"] != "final_norm_2":
                        copy(XH[:, m, :], X[:, m, :], col(a["gain"], m)).then_inc(*sig("xh", (n, m)))
                elif kind == "memload":
                    if a["after"]:
                        act.wait_ge(*on(*a["after"]))
                    act.dma_start(MRAW[:, :, :], dram[f"mem{a['which']}"]).then_inc(sems["d_mem"], 16)
                elif kind == "memfresh":
                    n, m = a["n"], a["m"]
                    act.wait_ge(sems["d_mem"], 16 * (n + 1))
                    act.wait_ge(*on(*a["sq_free"]))
                    act.activation(SQ[:, a["sq"], 0:NM], MRAW[:, m, :], ACT.Square).then_inc(*sig("msq", (n, m)))
                    copy(MH[:, m, :], MRAW[:, m, :], col(a["gain"], m)).then_inc(*sig("mh", (n, m)))
                elif kind == "rstd":
                    act.wait_ge(*on("sum", (kind, a["n"])))
                    act.activation(RSTD[:, :], O, ACT.Sqrt, bias=EPS, scale=1.0 / D).then_inc(*sig("sd", a["n"]))
                elif kind == "rstdm":
                    act.wait_ge(*on("sum", (kind, a["n"])))
                    act.activation(RSTDM[:, :], O[:, 0:NM], ACT.Sqrt, bias=EPS, scale=1.0 / D).then_inc(*sig("msd", a["n"]))
                elif kind == "hnorm":
                    for key in a["need"]:
                        act.wait_ge(*on(*key))
                    act.wait_ge(*on(*a["sq_free"]))
                    act.activation(SQ[:, a["sq"], 0:a["n"]], buf(a["src"]), ACT.Square).then_inc(*sig("hsq", a["id"]))
                    act.wait_ge(*on("hsum", a["id"]))
                    if sd_reader[0] is not None:
                        act.wait_ge(*on("hrec", sd_reader[0]))
                    sd = HSD if a["id"][0] == "H" else SD
                    act.activation(sd[:, 0:a["n"]], O[:, 0:a["n"]], ACT.Sqrt, bias=EPS,
                                   scale=1.0 / a["dim"]).then_inc(*sig("hsd", a["id"]))
                    sd_reader[0] = a["id"]
                elif kind == "vturn":
                    act.wait_ge(*on("vt", a["id"]))
                    for key in a.get("dfree", []):
                        act.wait_ge(*on(*key))
                    copy(buf(a["dst"]), TR[:, 0:a["nt"] * P]).then_inc(*sig("v", a["id"]))
                elif kind == "gate":
                    act.wait_ge(*on(*a["need"]))
                    act.activation(buf(a["dst"]), buf(a["dst"]), ACT.Sigmoid,
                                   bias=col("b_gate", 8 * a["n"] + a["m"])).then_inc(*sig("gate", (a["n"], a["m"])))
                elif kind == "bias":
                    if a["after"]:
                        act.wait_ge(*on(*a["after"]))
                    w = NT * (T if a["kind"] == "A" else 768)
                    act.dma_start(BIAS[:, 0:w], dram["bias" + a["kind"]][a["h"]]).then_inc(sems["d_bias"], 16)
                elif kind == "score":
                    i, what = a["i"], a["kind"]
                    act.wait_ge(*on("nmax", i))
                    nmx, tot = pair_of(48, i), pair_of(52, i)
                    if what == "A":
                        for c in range(2):
                            p = SP[:, i % 2, c * T:(c + 1) * T]
                            act.activation(p, p, ACT.Exp, bias=nmx[:, c:c + 1], accum_out=tot[:, c:c + 1])\
                                .then_inc(*sig("exp", i))
                    elif what == "B":
                        p = SP[:, i % 2, 0:768]
                        act.activation(p, p, ACT.Exp, bias=nmx[:, 0:1], accum_out=tot[:, 0:1]).then_inc(*sig("exp", i))
                    else:
                        if i >= 2:
                            act.wait_ge(*on("turned", i - 2))
                        act.activation(SP[:, i % 2, 0:NM], S[:, 0:NM], ACT.Exp, bias=nmx[:, 0:1],
                                       scale=1.0 if what == "C" else 256 ** -0.5,
                                       accum_out=tot[:, 0:1]).then_inc(*sig("exp", i))
                elif kind == "turn":
                    i, t, nk = a["i"], a["t"], kinds[a["kind"]]
                    act.wait_ge(*on("turned", i))
                    if t == 0 and i:
                        act.wait_ge(*on("pv", i - 1))
                    copy(PT[:, 0:nk, t * P:(t + 1) * P],
                         TR[:, 0:nk * P].rearrange("p (c q) -> p c q", c=nk)).then_inc(*sig("pt", i))
                elif kind == "pv":
                    i, h, what = a["i"], a["h"], a["kind"]
                    if what == "X":
                        act.wait_ge(*on("pv", (i, 0)))
                        copy(XOH[:, 2 * h, :], O).then_inc(*sig("ohi", out_key(a)))
                        act.wait_ge(*on("pv", i))
                        copy(XOH[:, 2 * h + 1, :], TR[:, 0:T]).then_inc(*sig("ohi", ("X", a["l"], 2 * h + 1)))
                    elif what != "A":
                        act.wait_ge(*on("pv", i))
                        copy(parts["O" + what][0][:, h, :], O).then_inc(*sig("ohi", out_key(a)))
                elif kind == "split":
                    for key in a["need"]:
                        act.wait_ge(*on(*key))
                    hi = (OAH if a["dst"][0] == "OA" else MIXH)[:, a["dst"][1], :]
                    copy(hi, buf(a["src"])).then_inc(*sig("ohi", a["id"]))
                elif kind == "job" and a["evac"] == "branch" and a["b"] == 2:
                    act.wait_ge(*on("y", (2, a["m"])))
                    copy(YH[:, a["m"], :], X[:, a["m"], :]).then_inc(*sig("yhi", a["m"]))
                elif kind == "reload":
                    act.wait_ge(*on("ylo", DC - 1))
                    act.wait_ge(*own("act"))
                    act.dma_start(X[:, :, :], dram["x"]).then_inc(sems["d_reload"], 16)
                elif kind == "ffn":
                    n = a["n"]
                    fg0 = counts.value("fg", ("base", n))
                    counts.at[("silu", ("base", n))] = counts.now.get("silu", 0)

                    def silu(i):
                        for jj in range(2):
                            act.wait_ge(sems["fg"], i * 2 + (fg0 + jj + 1))
                            act.activation(FS[:, :], FG[:, :], ACT.Silu).then_inc(sems["silu"], 1)

                    silu(0)
                    with act.Fori(1, NF // 2) as i:
                        silu(i)
                    counts.mark("silu", ("end", n), NF)
                    last["act"] = (sems["silu"], counts.now["silu"])
                elif kind == "poolload":
                    act.wait_ge(*on(*a["after"]))
                    act.dma_start(PW[:, :, :], dram["pool_w"][:, a["l"]]).then_inc(sems["d_poolw"], 16)
                elif kind == "hprep":
                    l, pr = a["l"], a["pr"]
                    act.wait_ge(*on(*a["need"]))
                    if pr:
                        act.wait_ge(*on("lvd", (l, 0, 9)))
                    act.activation(HK[:, :, :], HF[pr][:, :, :], ACT.Sigmoid, scale=-1.0).then_inc(*sig("sigm", (l, pr, 0)))
                    act.wait_ge(*own("act"))
                    act.activation(HF[pr][:, :, :], HF[pr][:, :, :], ACT.Sigmoid).then_inc(*sig("sigm", (l, pr, 1)))
                    act.activation(HG[pr][:, :, :], HG[pr][:, :, :], ACT.Silu).then_inc(*sig("hgs", (l, pr)))

        @block.vector
        def _(dve):
            def after_own():
                if "dve" in last:
                    dve.wait_ge(*own("dve"))

            for kind, a in SCHEDULE.steps:
                if kind == "setup":
                    dve.wait_ge(sems["d_consts"], 96)
                    dve.tensor_copy(masks[:, :, :], masks_f[:, :, :]).then_inc(*sig("setup", "masks"))
                    la = COLS["lambdas"][0]
                    dve.tensor_tensor(small[0:64, 0:2], cols[0:64, la:la + 4:2], cols[0:64, la + 1:la + 4:2],
                                      ALU.mult).then_inc(*sig("setup", "prod"))
                    for name, c in (("a_q_norm", 64 ** -0.5), ("b_q_norm", P ** -0.5), ("c_q_norm", P ** -0.5),
                                    ("a_subln", 1.0 - LAMBDA_INIT)):
                        dve.tensor_scalar(col(name), col(name), c, None, ALU.mult).then_inc(*sig("setup", name))
                    l0, l1 = (cols[:, COLS[f"lb_logits_2_{l}"][0]:COLS[f"lb_logits_2_{l}"][0] + 4] for l in range(2))
                    mx, e0, e1, tot = small[:, 8:12], small[:, 12:16], small[:, 16:20], small[:, 20:24]
                    dve.tensor_tensor(mx, l0, l1, ALU.max).then_inc(*sig("setup", "lbm"))
                    after_own()
                    dve.tensor_tensor(e0, l0, mx, ALU.subtract).then_inc(*sig("setup", "lbd0"))
                    dve.tensor_tensor(e1, l1, mx, ALU.subtract).then_inc(*sig("setup", "lbd"))
                    dve.wait_ge(*on("lb_exp"))
                    dve.tensor_tensor(tot, e0, e1, ALU.add).then_inc(*sig("setup", "lbs"))
                    after_own()
                    dve.reciprocal(small[:, 24:28], tot).then_inc(*sig("setup", "lbr"))
                    after_own()
                    dve.memset(small[:, 28:32], 0.0).then_inc(*sig("setup", "lb0"))
                    dve.memset(small[:, 32:36], 1.0).then_inc(*sig("setup", "lb0n"))
                    dve.tensor_tensor(small[:, 36:40], e1, small[:, 24:28], ALU.mult).then_inc(*sig("setup", "lb1"))
                    dve.tensor_tensor(small[:, 40:44], e0, small[:, 24:28], ALU.mult).then_inc(*sig("setup", "lb1n"))
                    dve.wait_ge(*on("lam_exp"))
                    dve.scalar_tensor_tensor(LAM, small[:, 2:3], LAMBDA_INIT, small[:, 3:4], ALU.add, ALU.subtract)\
                        .then_inc(*sig("setup", "lam"))
                elif kind in ("refresh", "memfresh"):
                    n, m = a["n"], a["m"]
                    mem = kind == "memfresh"
                    w = NM if mem else T
                    sq = SQ[:, a["sq"], 0:w]
                    after_own()
                    dve.wait_ge(*on("msq" if mem else "sq", (n, m)))
                    if m == 0:
                        if a["ssum_free"]:
                            dve.wait_ge(*on(*a["ssum_free"]))
                        dve.tensor_copy(SSUM[:, 0:w], sq).then_inc(*sig("ms" if mem else "xs", (n, m)))
                    else:
                        dve.tensor_tensor(SSUM[:, 0:w], SSUM[:, 0:w], sq, ALU.add)\
                            .then_inc(*sig("ms" if mem else "xs", (n, m)))
                    if a["gain"] != "final_norm_2":
                        src, hi, lo = (MRAW, MH, ML) if mem else (X, XH, XL)
                        dve.wait_ge(*on("mh" if mem else "xh", (n, m)))
                        dve.scalar_tensor_tensor(lo[:, m, :], src[:, m, :], col(a["gain"], m),
                                                 hi[:, m, :].bitcast(F32), ALU.mult, ALU.subtract)\
                            .then_inc(*sig("ml" if mem else "xl", (n, m)))
                elif kind == "rstd":
                    dve.wait_ge(*on("sd", a["n"]))
                    dve.reciprocal(RSTD[:, :], RSTD[:, :]).then_inc(*sig("rstd", a["n"]))
                elif kind == "rstdm":
                    dve.wait_ge(*on("msd", a["n"]))
                    dve.reciprocal(RSTDM[:, :], RSTDM[:, :]).then_inc(*sig("rstdm", a["n"]))
                elif kind == "job":
                    out = bank(a["j"])[:, 0:a["n"]]
                    m = a.get("m")
                    for key in a.get("free", []):
                        dve.wait_ge(*on(*key))
                    after_own()
                    dve.wait_ge(*job_done(a))
                    if a["evac"] in ("scale", "scalem"):
                        r = RSTD[:, :] if a["evac"] == "scale" else RSTDM[:, :]
                        dve.tensor_tensor(buf(a["dst"])[:, 0:a["n"]], out, r, ALU.mult).then_inc(*sig("evac", a["j"]))
                    elif a["evac"] == "resid":
                        if a["rhs"] == "y" and m == 0:
                            dve.wait_ge(sems["d_reload"], 16)
                        dve.scalar_tensor_tensor(X[:, m, :], out, a["c"], X[:, m, :], ALU.mult, ALU.add)\
                            .then_inc(*sig("evac", a["j"]))
                    elif a["evac"] == "back":
                        dve.tensor_tensor(FG[:, :], out, X[:, m, :], ALU.add).then_inc(*sig("evac", a["j"]))
                        after_own()
                        dve.tensor_copy(X[:, m, :].rearrange("p (s r) -> p s r", r=NT),
                                        FG[:, :].rearrange("p (r s) -> p s r", r=NT)).then_inc(*sig("x", m))
                    else:
                        b = a["b"]
                        dve.wait_ge(*on("gate", (b, m)))
                        y = X[:, m, :]
                        if b == 0:
                            dve.tensor_tensor(y, out, y, ALU.mult).then_inc(*sig("evac", a["j"]))
                        else:
                            g = GT[:, m % 2, :]
                            dve.tensor_tensor(g, out, g, ALU.mult).then_inc(*sig("evac", a["j"]))
                            after_own()
                            dve.tensor_tensor(y, y, g, ALU.add).then_inc(*sig("y", (b, m)))
                            if b == 2:
                                dve.wait_ge(*on("yhi", m))
                                dve.tensor_tensor(YL[:, m, :], y, YH[:, m, :].bitcast(F32), ALU.subtract)\
                                    .then_inc(*sig("ylo", m))
                elif kind == "hnorm":
                    n = a["n"]
                    sd, rec = (HSD, HREC) if a["id"][0] == "H" else (SD, REC)
                    after_own()
                    dve.wait_ge(*on("hsd", a["id"]))
                    dve.reciprocal(rec[:, 0:n], sd[:, 0:n]).then_inc(*sig("hrec", a["id"]))
                    after_own()
                    dve.scalar_tensor_tensor(buf(a["src"]), buf(a["src"]), gain_of(a["gain"]), rec[:, 0:n],
                                             ALU.mult, ALU.mult).then_inc(*sig("hn", a["id"]))
                elif kind == "score":
                    i, t, what = a["i"], a["t"], a["kind"]
                    mx, nmx = pair_of(44, i), pair_of(48, i)
                    after_own()
                    if t == 0 and what in "AB":
                        dve.wait_ge(sems["d_bias"], 16 * a["nbias"])
                    if i >= 2 and what in "AB":
                        dve.wait_ge(*on("turned", i - 2))
                    dve.wait_ge(*on("score", i))
                    n = 1
                    if what == "A":
                        n = 2
                        for c in range(2):
                            dve.tensor_tensor_reduce(SP[:, i % 2, c * T:(c + 1) * T], S[:, c * T:(c + 1) * T],
                                                     BIAS[:, t * T:(t + 1) * T], 1.0, -1e30, ALU.add, ALU.max,
                                                     mx[:, c:c + 1]).then_inc(*sig("max", i))
                    elif what == "B":
                        dve.tensor_tensor_reduce(SP[:, i % 2, 0:768], S[:, 0:768], BIAS[:, t * 768:(t + 1) * 768],
                                                 1.0, -1e30, ALU.add, ALU.max, mx[:, 0:1]).then_inc(*sig("max", i))
                    else:
                        dve.tensor_reduce(mx[:, 0:1], S[:, 0:NM], AX.X, ALU.max).then_inc(*sig("max", i))
                    after_own()
                    dve.tensor_scalar(nmx[:, 0:n], mx[:, 0:n], -(256 ** -0.5) if what == "X" else -1.0, None,
                                      ALU.mult).then_inc(*sig("nmax", i))
                elif kind == "turn":
                    i, what = a["i"], a["kind"]
                    tot, rs = pair_of(52, i), pair_of(56, i)
                    n = 2 if what == "A" else 1
                    w = kinds[what] * P
                    after_own()
                    dve.wait_ge(*on("exp", i))
                    dve.reciprocal(rs[:, 0:n], tot[:, 0:n]).then_inc(*sig("ptmp", ("r", i)))
                    after_own()
                    p = SP[:, i % 2, 0:w]
                    if what == "A":
                        q = SP[:, i % 2, T:2 * T]
                        dve.tensor_scalar(q, q, rs[:, 1:2], LAM, ALU.mult, ALU.mult).then_inc(*sig("ptmp", ("q", i)))
                        after_own()
                        dve.scalar_tensor_tensor(p, p, rs[:, 0:1], q, ALU.mult, ALU.subtract).then_inc(*sig("pn", i))
                    else:
                        dve.tensor_scalar(p, p, rs[:, 0:1], None, ALU.mult).then_inc(*sig("pn", i))
                elif kind == "pv":
                    h, what = a["h"], a["kind"]
                    after_own()
                    if what == "A":
                        dve.wait_ge(*on("pv", a["i"]))
                        dve.tensor_copy(AO[:, h, :], O).then_inc(*sig("pvd", ("A", h)))
                    elif what == "X":
                        for c, src in ((0, O), (1, TR[:, 0:T])):
                            key = ("X", a["l"], 2 * h + c)
                            dve.wait_ge(*on("ohi", key))
                            dve.tensor_tensor(XOL[:, 2 * h + c, :], src, XOH[:, 2 * h + c, :].bitcast(F32),
                                              ALU.subtract).then_inc(*sig("olo", key))
                    else:
                        hi, lo = parts["O" + what]
                        dve.wait_ge(*on("ohi", out_key(a)))
                        dve.tensor_tensor(lo[:, h, :], O, hi[:, h, :].bitcast(F32), ALU.subtract)\
                            .then_inc(*sig("olo", out_key(a)))
                elif kind == "split":
                    hi, lo = (OAH, OAL) if a["dst"][0] == "OA" else (MIXH, MIXL)
                    c = a["dst"][1]
                    after_own()
                    dve.wait_ge(*on("ohi", a["id"]))
                    dve.tensor_tensor(lo[:, c, :], buf(a["src"]), hi[:, c, :].bitcast(F32), ALU.subtract)\
                        .then_inc(*sig("olo", a["id"]))
                elif kind == "ffn":
                    n, u0 = a["n"], a["unit0"]
                    first = {w: counts.now.get(w, 0) for w in ("fg", "fu", "fm", "fhh", "fhl")}
                    for w in first:
                        counts.at[(w, ("base", n))] = first[w]
                    silu0 = counts.value("silu", ("base", n))
                    three_d = [P, 1, T]

                    def chunk(i, jj):
                        peeled = isinstance(i, int)
                        f = i * 2 + jj

                        def at(w):
                            return i * 2 + (first[w] + jj + 1)
                        if peeled and jj == 0:
                            after_own()
                        else:
                            dve.wait_ge(sems["fhl"], i * 2 + (first["fhl"] + jj))
                        dve.wait_ge(sems["unit_free"], i * 4 + (u0 + 2 * jj + 1))
                        dve.tensor_tensor(FG[:, :], PS[:, 2 * jj, :], RSTD[:, :], ALU.mult).then_inc(sems["fg"], 1)
                        dve.wait_ge(sems["unit_free"], i * 4 + (u0 + 2 * jj + 2))
                        dve.tensor_tensor(FU[:, :], PS[:, 2 * jj + 1, :], RSTD[:, :], ALU.mult).then_inc(sems["fu"], 1)
                        dve.wait_ge(sems["silu"], i * 2 + (silu0 + jj + 1))
                        dve.wait_ge(sems["fu"], at("fu"))
                        dve.tensor_tensor(FM[:, :], FS[:, :], FU[:, :], ALU.mult).then_inc(sems["fm"], 1)
                        dve.wait_ge(sems["fm"], at("fm"))
                        fm = FM[:, :].rearrange("p (a n) -> p a n", a=1)
                        hh = HH[:, f:f + 1, :] if peeled else HH[:, bass.ds(f, 1), :]
                        hl = HL[:, f:f + 1, :] if peeled else HL[:, bass.ds(f, 1), :]
                        dve.tensor_scalar(hh, fm, 1.0, None, ALU.mult).then_inc(sems["fhh"], 1)
                        dve.wait_ge(sems["fhh"], at("fhh"))
                        dve.tensor_tensor(hl, fm, hh.bitcast(F32), ALU.subtract).then_inc(sems["fhl"], 1)

                    for jj in range(2):
                        chunk(0, jj)
                    with dve.Fori(1, NF // 2) as i:
                        for jj in range(2):
                            chunk(i, jj)
                    for w in first:
                        counts.mark(w, ("end", n), NF)
                    last["dve"] = (sems["fhl"], counts.now["fhl"])
                elif kind == "hprep":
                    l, pr = a["l"], a["pr"]
                    after_own()
                    dve.memset(HS[:, :, :], 1.0).then_inc(*sig("hprep", (l, pr, "s")))
                    for hh in range(2):
                        h = 2 * pr + hh
                        dve.wait_ge(*on("sigm", (l, pr, 1)))
                        dve.tensor_scalar(HK[:, hh, :], HK[:, hh, :], one_minus_lb(l, h), None, ALU.mult)\
                            .then_inc(*sig("hprep", (l, pr, "k", hh)))
                        dve.tensor_scalar(HF[pr][:, hh, :], HF[pr][:, hh, :], one_minus_lb(l, h), lb(l, h),
                                          ALU.mult, ALU.add).then_inc(*sig("hprep", (l, pr) if hh else (l, pr, "f")))
                elif kind == "level":
                    l, pr, li = a["l"], a["pr"], a["li"]

                    def blocks(t, h):
                        return t[:, :, :].rearrange("p a t -> p (a t)").rearrange("p (b two h) -> p b two h", two=2, h=h)
                    q, pre, size = HQ[pr], HF[pr], 1 << max(li - 1, 0)
                    if li == 1:
                        after_own()
                        dve.tensor_tensor(QT[:, :, :], q[:, :, :], pre[:, :, :], ALU.mult)\
                            .then_inc(*sig("qkt", (l, pr, "q", li)))
                        dve.tensor_copy(KT[:, :, :], HK[:, :, :]).then_inc(*sig("qkt", (l, pr, li)))
                    elif li > 1:
                        after_own()
                        dve.wait_ge(*on("lev", (l, pr, li - 1)))
                        dve.tensor_tensor(blocks(QT, size)[:, :, 1, :], blocks(q, size)[:, :, 1, :],
                                          blocks(pre, size)[:, :, 1, :], ALU.mult).then_inc(*sig("qkt", (l, pr, "q", li)))
                        dve.tensor_tensor(blocks(KT, size)[:, :, 0, :], blocks(HK, size)[:, :, 0, :],
                                          blocks(HS, size)[:, :, 0, :], ALU.mult).then_inc(*sig("qkt", (l, pr, li)))
                    if 1 <= li < 9:
                        b, s = blocks(pre, size), blocks(HS, size)
                        nb = 2 * T // (2 * size)
                        after_own()
                        dve.tensor_tensor(s[:, :, 0, :], s[:, :, 0, :],
                                          b[:, :, 1, size - 1:size].broadcast_to([P, nb, size]), ALU.mult)\
                            .then_inc(*sig("qkt", (l, pr, "s", li)))
                        after_own()
                        dve.tensor_tensor(b[:, :, 1, :], b[:, :, 1, :],
                                          b[:, :, 0, size - 1:size].broadcast_to([P, nb, size]), ALU.mult)\
                            .then_inc(*sig("qkt", (l, pr, "p", li)))
                    src = S if li % 2 == 0 else TR
                    tiles = src.rearrange("p (c t) -> p c t", t=P)
                    ad = AD[:, :, :, :].rearrange("p a c t -> p (a c) t")
                    after_own()
                    dve.wait_ge(*on("lev", (l, pr, li)))
                    if li == 0:
                        dve.tensor_tensor(ad, tiles, ident[:, :].rearrange("p (a t) -> p a t", a=1)
                                          .broadcast_to([P, 2 * NT, P]), ALU.mult).then_inc(*sig("lvd", (l, pr, li)))
                    elif li <= 7:
                        dve.copy_predicated(ad, masks[:, li - 1:li, :].broadcast_to([P, 2 * NT, P]), tiles)\
                            .then_inc(*sig("lvd", (l, pr, li)))
                    elif li == 8:
                        dve.tensor_copy(A128[:, :, :, :].rearrange("p a c t -> p a (c t)"),
                                        src.rearrange("p (a t) -> p a t", a=2)[:, :, 0:2 * P])\
                            .then_inc(*sig("lvd", (l, pr, li)))
                    else:
                        dve.tensor_copy(A256[:, :, :, :].rearrange("p a c t -> p (a c t)"), src)\
                            .then_inc(*sig("lvd", (l, pr, li)))
                elif kind == "hout":
                    h = 2 * a["pr"] + a["hh"]
                    after_own()
                    dve.wait_ge(*on("ho_mm", (a["l"], h)))
                    dve.tensor_copy(HO[:, a["hh"], :], O).then_inc(*sig("ho", (a["l"], h)))
                elif kind == "hgate":
                    h = 2 * a["pr"] + a["hh"]
                    after_own()
                    dve.wait_ge(*on("hgs", (a["l"], a["pr"])))
                    dve.tensor_tensor(HO[:, a["hh"], :], HO[:, a["hh"], :], HG[a["pr"]][:, a["hh"], :], ALU.mult)\
                        .then_inc(*sig("hgated", (a["l"], h)))
                elif kind == "poolsum":
                    l, g = a["l"], a["g"]
                    w = 2 << g
                    cur, d = 0, 1
                    while d < w:
                        nxt = 1 if cur != 1 else 2
                        after_own()
                        dve.tensor_tensor(UB[:, nxt, d:T], UB[:, cur, d:T], UB[:, cur, 0:T - d], ALU.add)\
                            .then_inc(*sig("ptmp", (l, g, d)))
                        dve.tensor_copy(UB[:, nxt, 0:d], UB[:, cur, 0:d]).then_inc(*sig("ptmp", (l, g, d, "h")))
                        cur, d = nxt, 2 * d
                    assert cur == pool_slot(g)
                    s = UB[:, cur, :]
                    after_own()
                    dve.tensor_tensor(s[:, 0:w], s[:, 0:w], poolrec[:, g, 0:w], ALU.mult).then_inc(*sig("ptmp", (l, g, "a")))
                    after_own()
                    dve.tensor_tensor(s[:, 0:w], s[:, 0:w], UB[:, 0, 0:w], ALU.subtract).then_inc(*sig("ptmp", (l, g, "b")))
                    dve.scalar_tensor_tensor(s[:, w:T], s[:, w:T], 1.0 / w, UB[:, 0, w:T], ALU.mult, ALU.subtract)\
                        .then_inc(*sig("ptmp", (l, g)))
                elif kind == "pool":
                    l, g = a["l"], a["g"]
                    after_own()
                    dve.wait_ge(*on("pool_mm", (l, g)))
                    dve.tensor_scalar(UB[:, 1, :], O, col(f"pool_scale_2_{l}", g), None, ALU.mult)\
                        .then_inc(*sig("pooled", (l, g)))
                elif kind == "final":
                    for m in range(DC):
                        after_own()
                        dve.scalar_tensor_tensor(X[:, m, :], X[:, m, :], col("final_norm_2", m), RSTD[:, :],
                                                 ALU.mult, ALU.mult).then_inc(*sig("fin", m))


def pool_slot(g):
    return 1 if g % 2 == 0 else 2


def tokens_by_residue(a):
    return a.reshape(T // NT, NT, *a.shape[1:]).swapaxes(0, 1).reshape(a.shape)


def feature_major(a):
    return np.ascontiguousarray(a.T.reshape(DC, P, a.shape[0]).transpose(1, 0, 2))


def distance_constants():
    pos = tokens_by_residue(np.arange(T))
    dist = np.abs(pos[:, None] - pos[None, :]).astype(np.float32)
    out_of = np.float32(-1e30)
    slopes_a = [2.0 ** (-8.0 * (i + 1) / NHEAD) for i in range(NHEAD)]
    slopes_b = np.exp2(-8.0 * np.arange(1, 13, dtype=np.float32) / np.float32(12)).astype(np.float32).reshape(3, NHEAD)
    bias_a = np.stack([(-np.float32(s) * dist).reshape(NT, P, T).transpose(1, 0, 2).reshape(P, -1) for s in slopes_a])
    sub = np.arange(P)
    rel = np.abs(sub[:, None] - sub[None, :])
    bias_b = []
    for h in range(NHEAD):
        g0 = np.where(dist <= 64, -slopes_b[0, h] * dist, out_of).reshape(NT, P, T).transpose(1, 0, 2)
        g1 = np.where(rel <= 64, -slopes_b[1, h] * (4 * rel).astype(np.float32), out_of)
        g2 = np.where(rel % 4 == 0, -slopes_b[2, h] * (4 * rel).astype(np.float32), out_of)
        rest = np.broadcast_to(np.concatenate([g1, g2], 1)[:, None, :], (P, NT, 2 * P))
        bias_b.append(np.concatenate([g0, rest], 2).reshape(P, -1))
    return bias_a.astype(np.float32), np.stack(bias_b).astype(np.float32)


def constants():
    t = np.arange(P)
    masks = []
    for li in range(7):
        h = 1 << li
        same = t[:, None] // (2 * h) == t[None, :] // (2 * h)
        masks.append(same & (t[:, None] % (2 * h) < h) & (t[None, :] % (2 * h) >= h))
    rec = np.zeros((P, 4, 16), np.float32)
    for g in range(4):
        rec[:, g, :] = 1.0 / np.minimum(np.arange(1, 17), 2 << g)
    half = (t[:, None] // 64 == t[None, :] // 64).astype(np.float32)
    bias_a, bias_b = distance_constants()
    return {"ones": np.ones((P, P), np.float32), "halves": half, "ident": np.eye(P, dtype=np.float32),
            "masks": np.ascontiguousarray(np.stack(masks, 1)).astype(np.float32), "poolrec": rec,
            "biasA": bias_a, "biasB": bias_b}


def weight_units(inputs):
    out = np.empty((NU, P, UT * P), np.float32)
    for u, (name, l, tiles) in enumerate(SCHEDULE.units):
        w = inputs[name][0, l] if name == "w_branch" else inputs[name][l]
        for c, (r, k) in enumerate(tiles):
            out[u, :, c * P:(c + 1) * P] = w[r * P:(r + 1) * P, k * P:(k + 1) * P]
    return out


def vector_columns(inputs):
    out = np.zeros((P, NCOL), np.float32)
    for name, (at, n) in COLS.items():
        if name == "lambdas":
            for c, w in enumerate(("a_lambda_q1", "a_lambda_k1", "a_lambda_q2", "a_lambda_k2")):
                out[0:64, at + c] = inputs[w][0]
            continue
        base, l = (name[:-2], int(name[-1])) if name[-2:] in ("_0", "_1") else (name, 0)
        v = inputs[base] if base == "final_norm_2" else inputs[base][l]
        if v.size == 64:
            out[0:64, at] = out[64:P, at] = v
        else:
            out[:, at:at + n] = v.reshape(n, P).T
    return out


def kernel(**inputs):
    import concourse.bacc as bacc
    from concourse.bass_utils import run_bass_kernel_spmd as run

    inputs = {k: np.asarray(v) for k, v in inputs.items()}
    arrays = {"weights": weight_units(inputs), "cols": vector_columns(inputs),
              "x": feature_major(tokens_by_residue(inputs["x"][0])),
              "mem0": feature_major(inputs["mem"][0]), "mem1": feature_major(inputs["mem_2"][0]),
              "pool_w": np.ascontiguousarray(inputs["pool_w_2"].transpose(2, 0, 1, 3)), **constants()}
    known = None
    for _ in range(2):
        nc = bacc.Bacc("TRN2", target_bir_lowering=False, num_devices=1)
        dram = {k: nc.dram_tensor(f"in_{k}", a.shape, mybir.dt.from_np(a.dtype), kind="ExternalInput").ap()
                for k, a in arrays.items()}
        dram["out"] = nc.dram_tensor("out_x", (P, DC, T), F32, kind="ExternalOutput").ap()
        counts = Counts(known)
        program(nc, dram, counts)
        known = counts.at
    got = run(nc, [{f"in_{k}": a for k, a in arrays.items()}], core_ids=[0])
    out = got.results[0]["out_x"]
    return out.transpose(2, 1, 0).reshape(1, T, D)
```

```python
import math
from contextlib import ExitStack

import numpy as np

import concourse.bass as bass
from concourse import mybir

P = 128
F32 = mybir.dt.float32
F32R = mybir.dt.float32r
U8 = mybir.dt.uint8
ACT = mybir.ActivationFunctionType
ALU = mybir.AluOpType
AX = mybir.AxisListType

T = 512
NT = T // P
D = 1024
DC = D // P
NM = 256
NF = 2816 // P
EPS = 1e-6
NHEAD = 4
UT = 8
RAW = 3
SQS = 2
RING = 4
LAMBDA_INIT = 0.8 - 0.6 * math.exp(0.0)
LAYERS = 2

KB = 1024


def column_plan():
    plan, at = {}, 0
    names = [("norm_mix", 8), ("norm_ffn", 8), ("b_gate", 24), ("mem_norm", 8), ("a_q_norm", 1), ("a_k_norm", 1),
             ("a_subln", 1), ("b_q_norm", 1), ("b_k_norm", 1), ("c_q_norm", 1), ("c_k_norm", 1)]
    for l in range(LAYERS):
        names += [(f"ffn1_norm_2_{l}", 8), (f"mix_norm_2_{l}", 8), (f"hgrn_norm_2_{l}", 4), (f"pool_scale_2_{l}", 4),
                  (f"xa_norm_2_{l}", 8), (f"mem_norm_2_{l}", 8), (f"ffn2_norm_2_{l}", 8), (f"lb_logits_2_{l}", 4)]
    names += [("final_norm_2", 8), ("lambdas", 4)]
    for name, n in names:
        plan[name] = (at, n)
        at += n
    return plan, at


COLS, NCOL = column_plan()


class Schedule:

    def __init__(self):
        self.steps = []
        self.units = []
        self.njobs = 0
        self.nsq = 0
        self.sq_reader = {}
        self.last_sum = None
        self.nbias = 0
        self.norms = []
        self.later = []

    def step(self, kind, /, **a):
        if kind in ("refresh", "memfresh", "hsq"):
            a["sq"] = self.nsq % SQS
            a["sq_free"] = self.sq_reader.get(a["sq"])
            self.nsq += 1
            self.sq_reader[a["sq"]] = (("hsum", a["id"]) if kind == "hsq" else
                                       ("xs" if kind == "refresh" else "ms", (a["n"], a["m"])))
        if kind in ("refresh", "memfresh") and a["m"] == 0:
            a["ssum_free"] = self.last_sum
        if kind in ("rstd", "rstdm"):
            self.last_sum = ("sum", (kind, a["n"]))
        if kind == "bias":
            self.nbias += 1
        if kind == "score":
            a["nbias"] = self.nbias
        self.steps.append((kind, a))

    def unit(self, name, l, tiles):
        self.units.append((name, l, tiles))

    def job(self, tile0, nk, /, **a):
        j = self.njobs
        self.njobs += 1
        self.step("job", j=j, tile0=tile0, nk=nk, **a)
        norms, self.norms = self.norms, []
        for kind, n in norms:
            self.step(kind, n=n)
        self.step("evac", j=j, tile0=tile0, nk=nk, **a)
        self.flush()
        return j

    def column(self, name, l, column, /, **a):
        t0 = len(self.units) * UT
        self.unit(name, l, [(k, column) for k in range(DC)])
        return self.job(t0, DC, **a)

    def flush(self):
        later, self.later = self.later, []
        for go in later:
            go()

    def defer(self, go):
        self.later.append(go)


def spread(work, slots):
    state = [0, 0]

    def fill():
        state[1] += 1
        upto = len(work) * min(state[1], slots) // slots
        while state[0] < upto:
            state[0] += 1
            work[state[0] - 1]()
    return fill


def build_schedule():
    s = Schedule()
    step, column = s.step, s.column
    step("setup")
    for m in range(DC):
        step("refresh", n=0, m=m, gain="norm_mix")
    s.norms.append(("rstd", 0))

    def hnorm(id, src, gain, ones, n, dim, need):
        step("hsq", id=id, src=src, n=n, need=need)
        sq = s.steps[-1][1]["sq"]
        s.defer(lambda: step("hnorm", id=id, src=src, gain=gain, ones=ones, n=n, dim=dim, sq=sq))

    def vturn(**a):
        s.defer(lambda: step("vturn", **a))

    needx = {k: [("xl", (0, k))] for k in range(DC)}
    for h in range(NHEAD):
        for w, (c, g) in enumerate((("Q", "a_q_norm"), ("K", "a_k_norm"))):
            j = column("w_in", 0, 4 * w + h, rhs="x", n=T, evac="scale", dst=("A" + c, h), need=needx)
            needx = {}
            hnorm(("A" + c, h), ("A" + c, h), g, "halves", T, 64, [("evac", j)])
        j = column("w_in", 0, 8 + h, rhs="x", n=T, evac="scale", dst=("VT", h % 2), free=[("v", ("A", h - 2))] if h >= 2 else [])
        vturn(id=("A", h), src=("VT", h % 2), nt=NT, dst=("AV", h), need=("evac", j))

    def gate_chunk(n, m, dst, free=()):
        j = column("w_gate", 0, 8 * n + m, rhs="x", n=T, evac="scale", dst=dst, free=list(free))
        step("gate", n=n, m=m, dst=dst, need=("evac", j))

    i = 0

    def attend(tiles, work, after_pv=None):
        nonlocal i
        fill = spread(work, 2 * len(tiles))
        for k, a in enumerate(tiles):
            a["i"] = i
            if a["t"] == 0 and a["kind"] in "AB":
                step("bias", kind=a["kind"], h=a["h"], after=("nmax", i - 1) if i else None)
            step("score", **a)
            fill()
            if k:
                step("turn", **tiles[k - 1])
                fill()
                if a["t"] == 0:
                    step("pv", **tiles[k - 1])
                    if after_pv:
                        after_pv(tiles[k - 1]["h"])
            i += 1
        fill()
        step("turn", **tiles[-1])
        step("pv", **tiles[-1])
        if after_pv:
            after_pv(tiles[-1]["h"])

    def branch(n, o, gate_dst, gates_done):
        for jj in range(DC // 2):
            if not gates_done:
                for m in (2 * jj, 2 * jj + 1):
                    gate_chunk(n, m, gate_dst(m))
            t0 = len(s.units) * UT
            s.unit("w_branch", n, [(k, 2 * jj + mm) for mm in range(2) for k in range(4)])
            for mm in range(2):
                m = 2 * jj + mm
                need = {k: [("olo", ("ABC"[n], k))] for k in range(4)} if m == 0 else {}
                s.job(t0 + 4 * mm, 4, rhs=o, n=T, evac="branch", b=n, m=m, need=need, gate=gate_dst(m))

    def b_jobs(h):
        out = []
        for g in range(3):
            for w, (c, gain) in enumerate((("Q", "b_q_norm"), ("K", "b_k_norm"))):
                def go(g=g, w=w, c=c, gain=gain):
                    dst = (f"B{c}{h % 2}", g)
                    free = [("score", b_tiles[h - 2][-1]["i"])] if h >= 2 else []
                    j = column("w_in", 0, 12 + 12 * w + 4 * g + h, rhs="x", n=T, evac="scale", dst=dst, free=free)
                    hnorm((f"B{c}{g}", h), dst, gain, "ones", T, P, [("evac", j)])
                out.append(go)

            def go(g=g):
                nv = 3 * h + g
                free = [("v", ("B", *divmod(nv - 2, 3)))] if nv >= 2 else [("v", ("A", 2 + nv))]
                j = column("w_in", 0, 36 + 4 * g + h, rhs="x", n=T, evac="scale", dst=("VT", nv % 2), free=free)
                vturn(id=("B", h, g), src=("VT", nv % 2), nt=NT, dst=(f"BV{h % 2}", g), need=("evac", j),
                      dfree=[("pv", b_tiles[h - 2][-1]["i"])] if h >= 2 else [])
            out.append(go)
        return out

    b_tiles = [[dict(kind="B", h=h, t=t, need=[("hn", (f"B{c}{g}", h)) for c in "QK" for g in range(3)],
                     need_v=[("v", ("B", h, g)) for g in range(3)]) for t in range(NT)] for h in range(NHEAD)]
    a_tiles = [dict(kind="A", h=h, t=t, need=[("hn", ("AQ", h)), ("hn", ("AK", h))], need_v=[("v", ("A", h))])
               for h in range(NHEAD) for t in range(NT)]
    gates_a = [lambda m=m: gate_chunk(0, m, ("Y", m)) for m in range(DC)]
    first_b = b_jobs(0)
    gates_a[0]()
    attend(a_tiles, gates_a[1:] + first_b[:7],
           lambda h: hnorm(("AO", h), ("AO", h), "a_subln", "ones", T, P, [("pvd", ("A", h))]))
    first_b[7]()
    for h in range(NHEAD):
        step("split", id=("A", h), src=("AO", h), dst=("OA", h), need=[("hn", ("AO", h))])
    first_b[8]()
    branch(0, "OA", lambda m: ("Y", m), True)
    s.flush()

    c_queries = []
    for h in range(NHEAD):
        def go(h=h):
            j = column("w_in", 0, 48 + h, rhs="x", n=T, evac="scale", dst=("CQ", h))
            hnorm(("CQ", h), ("CQ", h), "c_q_norm", "ones", T, P, [("evac", j)])
        c_queries.append(go)
    for h in range(NHEAD):
        attend(b_tiles[h], b_jobs(h + 1) if h + 1 < NHEAD else c_queries)
        s.flush()

    def memory(n, which, gain):
        return ([lambda: step("memload", n=n, which=which, after=("evac", s.njobs - 1))]
                + [lambda m=m: step("memfresh", n=n, m=m, gain=gain) for m in range(DC)]
                + [lambda: s.norms.append(("rstdm", n))])

    for go in memory(0, 0, "mem_norm"):
        go()
    norms, s.norms = s.norms, []
    branch(1, "OB", lambda m: ("GT", m % 2), False)
    s.norms = norms
    needm = {k: [("ml", (0, k))] for k in range(DC)}
    for h in range(NHEAD):
        j = column("w_mem_kv", 0, h, rhs="mem", n=NM, evac="scalem", dst=("CK", h), need=needm)
        needm = {}
        hnorm(("CK", h), ("CK", h), "c_k_norm", "ones", NM, P, [("evac", j)])
        j = column("w_mem_kv", 0, 4 + h, rhs="mem", n=NM, evac="scalem", dst=("VT", h % 2),
                   free=[("v", ("C", h - 2))] if h >= 2 else [("v", ("B", 3, 2))])
        vturn(id=("C", h), src=("VT", h % 2), nt=NM // P, dst=("CV", h), need=("evac", j))
    gates_c = [lambda m=m: gate_chunk(2, m, ("GC", m)) for m in range(DC)]
    gates_c[0]()
    attend([dict(kind="C", h=h, t=t, need=[("hn", ("CQ", h)), ("hn", ("CK", h))], need_v=[("v", ("C", h))])
            for h in range(NHEAD) for t in range(NT)], gates_c[1:])
    branch(2, "OC", lambda m: ("GC", m), True)
    step("reload")
    norm = 1
    for m in range(DC):
        need = {k: [("ylo", k)] for k in range(DC)} if m == 0 else {}
        j = column("w_out", 0, m, rhs="y", n=T, evac="resid", m=m, c=1.0, need=need)
        step("refresh", n=norm, m=m, gain="norm_ffn", need=("evac", j))

    def ffn(w1, w3, w2, l, c, n, gain_next, back=False):
        t0 = len(s.units) * UT
        for f in range(NF):
            for w in (w1, w3):
                s.unit(w, l, [(k, f) for k in range(DC)])
        step("ffn", n=n, unit0=t0 // UT)
        t1 = len(s.units) * UT
        order = [(k, m) for m in range(DC) for k in range(NF)]
        for u in range(0, len(order), UT):
            s.unit(w2, l, order[u:u + UT])
        for m in range(DC):
            j = s.job(t1 + m * NF, NF, rhs="h", n=T, evac="back" if back else "resid", m=m, c=c, first=(m == 0), norm=n)
            step("refresh", n=n + 1, m=m, gain=gain_next, need=("x", m) if back else ("evac", j))

    ffn("w_ffn_gate", "w_ffn_up", "w_ffn_down", 0, 1.0, 1, "ffn1_norm_2_0", back=True)
    norm = 2

    for l in range(LAYERS):
        ffn("ffn1_w1_2", "ffn1_w3_2", "ffn1_w2_2", l, 0.5, norm, f"mix_norm_2_{l}")
        norm += 1
        s.norms.append(("rstd", norm))
        needx = {k: [("xl", (norm, k))] for k in range(DC)}

        def pair_jobs(pr):
            out = []
            for hh in range(2):
                h = 2 * pr + hh
                for w, c in enumerate(("HQ", "HF", None, "HG")):
                    def go(h=h, hh=hh, w=w, c=c):
                        nonlocal needx
                        if c:
                            column("w_in_2", l, 4 * w + h, rhs="x", n=T, evac="scale", dst=(f"{c}{pr}", hh), need=needx)
                            needx = {}
                        else:
                            free = [("v", (l, h - 2))] if h >= 2 else []
                            j = column("w_in_2", l, 8 + h, rhs="x", n=T, evac="scale", dst=("HVT", hh), free=free)
                            vturn(id=(l, h), src=("HVT", hh), nt=NT, dst=(f"HV{pr}", hh), need=("evac", j))
                    out.append(go)
            return out

        def pool_job(g):
            column("w_in_2", l, 16 + g, rhs="x", n=T, evac="scale", dst=("U", 0))
            step("poolsum", l=l, g=g)

        def pool_rest(g):
            step("pool", l=l, g=g)
            step("split", id=("M", l, 4 + g), src=("U", 1), dst=("MIX", 4 + g), need=[("pooled", (l, g))])

        def levels(pr, work):
            step("hprep", l=l, pr=pr, need=("evac", s.njobs - 1))
            fill = spread(work, 10)
            for li in range(10):
                step("level", l=l, pr=pr, li=li)
                fill()
            s.flush()

        def heads_out(pr):
            def norm_of(hh):
                h = 2 * pr + hh
                step("hsq", id=("H", l, h), src=(f"HO{pr}", hh), n=T, need=[("ho", (l, h))])
                sq = s.steps[-1][1]["sq"]
                return lambda: step("hnorm", id=("H", l, h), src=(f"HO{pr}", hh), gain=f"hgrn_norm_2_{l}:{h}",
                                    ones="ones", n=T, dim=P, sq=sq)

            def end(hh):
                h = 2 * pr + hh
                step("hgate", l=l, pr=pr, hh=hh)
                step("split", id=("M", l, h), src=(f"HO{pr}", hh), dst=("MIX", h), need=[("hgated", (l, h))])
            step("hout", l=l, pr=pr, hh=0)
            first = norm_of(0)
            step("hout", l=l, pr=pr, hh=1)
            second = norm_of(1)
            return [first, lambda: end(0), second, lambda: end(1)]

        step("poolload", l=l, after=("evac", s.njobs - 1))
        rests = [w for g in range(4) for w in (lambda g=g: pool_job(g), lambda g=g: pool_rest(g))]
        for go, other in zip(pair_jobs(0), rests):
            go()
            other()
        s.flush()
        levels(0, pair_jobs(1))
        rest = heads_out(0)
        first, second = memory(1 + l, 1, f"mem_norm_2_{l}"), []
        rest[0]()
        rest[1]()
        jk = []
        needm = {k: [("ml", (1 + l, k))] for k in range(DC)}
        for c in range(DC):
            def go(c=c):
                nonlocal needm
                jk.append(column("xa_wkv_2", l, c, rhs="mem2", n=NM, evac="scalem", dst=("XK", c), need=needm))
                needm = {}
            second.append(go)
        for c in range(DC):
            def go(c=c):
                free = [("v", ("X", l, c - 2))] if c >= 2 else []
                j = column("xa_wkv_2", l, 8 + c, rhs="mem2", n=NM, evac="scalem", dst=("VT", c % 2), free=free)
                vturn(id=("X", l, c), src=("VT", c % 2), nt=NM // P, dst=("XV", c), need=("evac", j))
            second.append(go)
        first[0]()
        rest[2]()
        rest[3]()
        for go in first[1:]:
            go()
        levels(1, second[:14])
        rest = heads_out(1)
        second[14]()
        rest[0]()
        rest[1]()
        second[15]()
        rest[2]()
        rest[3]()
        s.flush()
        norm += 1
        for m in range(DC):
            need = {k: [("olo", ("M", l, k))] for k in range(DC)} if m == 0 else {}
            j = column("w_out_2", l, m, rhs="mix", n=T, evac="resid", m=m, c=1.0, need=need)
            step("refresh", n=norm, m=m, gain=f"xa_norm_2_{l}", need=("evac", j))
        s.norms.append(("rstd", norm))
        needx, jq = {k: [("xl", (norm, k))] for k in range(DC)}, {}
        queries = []
        for c in range(DC):
            def go(c=c):
                nonlocal needx
                jq[c] = column("xa_wq_2", l, c, rhs="x", n=T, evac="scale", dst=("XQ", c), need=needx)
                needx = {}
            queries.append(go)
        for go in queries[:4]:
            go()
        for h in range(NHEAD):
            attend([dict(kind="X", h=h, t=t, l=l, need=[("evac", jq[2 * h + 1]), ("evac", jk[2 * h + 1])],
                         need_v=[("v", ("X", l, 2 * h + 1))]) for t in range(NT)],
                   {0: queries[4:6], 1: queries[6:7], 2: queries[7:8]}.get(h, []))
        norm += 1
        for m in range(DC):
            need = {k: [("olo", ("X", l, k))] for k in range(DC)} if m == 0 else {}
            j = column("xa_wo_2", l, m, rhs="xo", n=T, evac="resid", m=m, c=1.0, need=need)
            step("refresh", n=norm, m=m, gain=f"ffn2_norm_2_{l}", need=("evac", j))
        last = l == LAYERS - 1
        ffn("ffn2_w1_2", "ffn2_w3_2", "ffn2_w2_2", l, 0.5, norm, "final_norm_2" if last else f"ffn1_norm_2_{l + 1}")
        norm += 1
    step("rstd", n=norm)
    step("final", n=norm)
    return s


SCHEDULE = build_schedule()
NU = len(SCHEDULE.units)


class Counts:

    def __init__(self, known=None):
        self.known = known
        self.now = {}
        self.at = {}

    def mark(self, name, key, n=1):
        self.now[name] = self.now.get(name, 0) + n
        self.at[(name, key)] = self.now[name]

    def value(self, name, key):
        if self.known is None:
            return 1
        return self.known[(name, key)]


RAISES = {
    "pe": ["unit_free", "job_mid", "sum", "hsum", "score", "turned", "vt", "pv", "lev", "ho_mm", "pool_mm", "lam_mm"],
    "act": ["sq", "xh", "sd", "msq", "mh", "msd", "hsq", "hsd", "exp", "pt", "v", "ohi", "gate", "yhi", "silu",
            "sigm", "lam_exp", "lb_exp", "hgs"],
    "dve": ["setup", "xs", "xl", "rstd", "ms", "ml", "rstdm", "evac", "x", "hrec", "hn", "max", "nmax", "pn", "pvd",
            "olo", "y", "ylo", "fg", "fu", "fm", "fhh", "fhl", "fin", "hprep", "qkt", "lvd", "ho", "hgated",
            "pooled", "ptmp"],
    "pool": ["unit_hi", "unit_ready"],
}
DMAS = ["d_x", "d_consts", "d_bias", "d_mem", "d_reload", "d_poolw", "d_out"]


def program(nc, dram, counts):
    ctx = ExitStack()
    with ctx:
        sems = {n: ctx.enter_context(nc.semaphore(n)) for ns in RAISES.values() for n in ns}
        sems.update({n: ctx.enter_context(nc.semaphore(n)) for n in DMAS})
        raw_landed = [ctx.enter_context(nc.semaphore(f"raw_landed{k}")) for k in range(RAW)]
        engine_of = {n: e for e, ns in RAISES.items() for n in ns}
        last = {}

        def sig(name, key=None):
            counts.mark(name, key)
            last[engine_of[name]] = (sems[name], counts.now[name])
            return sems[name], 1

        def on(name, key=None):
            return sems[name], counts.value(name, key)

        def own(engine):
            return last[engine]

        base = (nc.sbuf_base + 31) // 32 * 32
        top = [base]

        def fixed(name, shape, dt=F32):
            size = int(np.prod(shape[1:])) * (1 if dt == U8 else 4)
            t = nc.alloc_sbuf_tensor_at(name, shape, dt, offset=top[0])
            top[0] += (size + 31) // 32 * 32
            return t

        raw = [fixed(f"raw{k}", [P, UT * P]) for k in range(RAW)]
        whi = [fixed(f"whi{k}", [P, UT * P], F32R) for k in range(RING)]
        wlo = [fixed(f"wlo{k}", [P, UT * P], F32R) for k in range(RING)]
        X = fixed("x_res", [P, DC, T])
        xh_at = top[0]
        XH = fixed("x_hi", [P, DC, T], F32R)
        XL = fixed("x_lo", [P, DC, T], F32R)
        RSTD = fixed("rstd_x", [P, T])
        RSTDM = fixed("rstd_mem", [P, NM])
        SSUM = fixed("sq_sum", [P, T])
        SQ = fixed("sq", [P, 2, T])
        cols = fixed("cols", [P, NCOL])
        ones = fixed("ones", [P, P])
        halves = fixed("halves", [P, P])
        ident = fixed("ident", [P, P])
        masks = fixed("masks", [P, 7, P], U8)
        poolrec = fixed("poolrec", [P, 4, 16])
        small = fixed("small", [P, 64])
        arena = top[0]

        def area(name, kb, shape, dt=F32):
            size = int(np.prod(shape[1:])) * 4
            assert arena + kb * KB + size <= nc.sbuf_usable_end, (name, kb, size, nc.sbuf_usable_end - arena)
            return nc.alloc_sbuf_tensor_at(name, shape, dt, offset=arena + int(kb * KB))

        masks_f = area("masks_f", 0, [P, 7, P])
        AQ, AK, AV = (area(n, o, [P, NHEAD, T]) for n, o in (("a_q", 0), ("a_k", 8), ("a_v", 16)))
        AO = area("a_out", 42, [P, NHEAD, T])
        OAH, OAL = (area(n, o, [P, NHEAD, T], F32R) for n, o in (("oa_hi", 0), ("oa_lo", 8)))
        BQ = [area(f"b_q{s}", o, [P, 3, T]) for s, o in ((0, 24), (1, 0))]
        BK = [area(f"b_k{s}", o + 6, [P, 3, T]) for s, o in ((0, 24), (1, 0))]
        BV = [area(f"b_v{s}", o + 12, [P, 3, T]) for s, o in ((0, 24), (1, 0))]
        OBH, OBL = (area(n, o, [P, NHEAD, T], F32R) for n, o in (("ob_hi", 42), ("ob_lo", 50)))
        BIAS = area("bias", 58, [P, NT * 768])
        CQ = area("c_q", 24, [P, NHEAD, T])
        CK = area("c_k", 32, [P, NHEAD, NM])
        CV = area("c_v", 36, [P, NHEAD, NM])
        OCH, OCL = (area(n, o, [P, NHEAD, T], F32R) for n, o in (("oc_hi", 0), ("oc_lo", 8)))
        GC = area("gate_c", 54, [P, DC, T])
        MRAW = area("mem_raw", 16, [P, DC, NM])
        MH, ML = (area(n, o, [P, DC, NM], F32R) for n, o in (("mem_hi", 0), ("mem_lo", 8)))
        MRAW2 = [area("mem_raw2a", 58, [P, DC // 2, NM]), area("mem_raw2b", 94, [P, DC // 2, NM])]
        MH2 = nc.alloc_sbuf_tensor_at("mem2_hi", [P, DC, NM], F32R, offset=xh_at)
        ML2 = nc.alloc_sbuf_tensor_at("mem2_lo", [P, DC, NM], F32R, offset=xh_at + 8 * KB)

        def mem_tensors(n, m):
            if n == 0:
                return MRAW[:, m, :], MH, ML
            return MRAW2[m // 4][:, m % 4, :], MH2, ML2
        SP = area("probs", 70, [P, 2, 1024])
        PT = area("probs_t", 78, [P, 6, T])
        SD = area("sd", 90, [P, T])
        REC = area("rec", 92, [P, T])
        VT = area("vt_sb", 94, [P, 2, T])
        GT = area("gate_sb", 98, [P, 2, T])
        HH, HL = (area(n, o, [P, NF, T], F32R) for n, o in (("h_hi", 0), ("h_lo", 44)))
        FG, FU, FS, FM = (area(n, o, [P, T]) for n, o in (("ffn_g", 88), ("ffn_u", 90), ("ffn_s", 92), ("ffn_m", 94)))
        HQ = [area(f"h_q{s}", o, [P, 2, T]) for s, o in ((0, 0), (1, 42))]
        HF = [area(f"h_f{s}", o, [P, 2, T]) for s, o in ((0, 4), (1, 46))]
        HK = area("h_k", 8, [P, 2, T])
        HS = area("h_suf", 12, [P, 2, T])
        QT, KT = (area(n, o, [P, 2, T]) for n, o in (("h_qt", 16), ("h_kt", 20)))
        HG = [area(f"h_g{s}", o, [P, 2, T]) for s, o in ((0, 24), (1, 50))]
        HV = [area(f"h_v{s}", o, [P, 2, T]) for s, o in ((0, 28), (1, 54))]
        AD = area("h_ad", 32, [P, 2, NT, P])
        A128 = area("h_a128", 36, [P, 2, 2, P])
        A256 = area("h_a256", 38, [P, 2, 2, 2 * P])
        HVT = area("hvt_sb", 58, [P, 2, T])
        MIXH, MIXL = (area(n, o, [P, DC, T], F32R) for n, o in (("mix_hi", 62), ("mix_lo", 78)))
        UB = area("pool_u", 94, [P, 3, T])
        HSD = area("h_sd", 100, [P, T])
        HREC = [area(f"h_rec{s}", o, [P, T]) for s, o in ((0, 4), (1, 46))]
        HO = [area(f"h_o{s}", o, [P, 2, T]) for s, o in ((0, 0), (1, 42))]
        PW = area("pool_w_sb", 38, [P, 4, P])
        XQ = area("x_q", 8, [P, DC, T])
        XK = area("x_k", 0, [P, DC, NM])
        XV = area("x_v", 24, [P, DC, NM])
        XOH, XOL = (area(n, o, [P, DC, T], F32R) for n, o in (("xo_hi", 32), ("xo_lo", 48)))
        YH, YL = (area(n, o, [P, DC, T], F32R) for n, o in (("y_hi", 32), ("y_lo", 48)))

        bufs = {"AQ": AQ, "AK": AK, "AV": AV, "AO": AO, "VT": VT, "GT": GT, "Y": X, "CQ": CQ, "CK": CK, "CV": CV,
                "BQ0": BQ[0], "BQ1": BQ[1], "BK0": BK[0], "BK1": BK[1], "BV0": BV[0], "BV1": BV[1],
                "HQ0": HQ[0], "HQ1": HQ[1], "HF0": HF[0], "HF1": HF[1], "HG0": HG[0], "HG1": HG[1],
                "HV0": HV[0], "HV1": HV[1], "HVT": HVT, "HO0": HO[0], "HO1": HO[1], "GC": GC, "U": UB, "XQ": XQ, "XK": XK, "XV": XV}
        parts = {"x": (XH, XL), "h": (HH, HL), "mem": (MH, ML), "mem2": (MH2, ML2), "OA": (OAH, OAL), "OB": (OBH, OBL),
                 "OC": (OCH, OCL), "mix": (MIXH, MIXL), "xo": (XOH, XOL), "y": (YH, YL)}

        def buf(where):
            return bufs[where[0]][:, where[1], :]

        def col(name, m=0):
            return cols[:, COLS[name][0] + m:COLS[name][0] + m + 1]

        def gain_of(name):
            base, _, m = name.partition(":")
            return col(base, int(m or 0))

        LAM = small[:, 4:5]

        def lb(l, m):
            return small[:, 28 + 8 * l + m:29 + 8 * l + m]

        def one_minus_lb(l, m):
            return small[:, 32 + 8 * l + m:33 + 8 * l + m]

        def pair_of(first, i):
            return small[:, first + 2 * (i % 2):first + 2 * (i % 2) + 2]

        PS = ctx.enter_context(nc.psum_tensor("ps", [P, 8, T], F32))
        flat = PS[:, :, :].rearrange("p b n -> p (b n)")
        S = flat[:, 0:2 * T]
        TR = flat[:, 2 * T:4 * T]
        O = PS[:, 7, :]

        def bank(j):
            return PS[:, 4 + j % 3, :]

        def job_done(a):
            end = a["tile0"] + a["nk"]
            return on("unit_free", end // UT - 1) if end % UT == 0 else on("job_mid", a["j"])

        jobs = [a for k, a in SCHEDULE.steps if k == "job"]
        kinds = {"A": 4, "B": 6, "C": 2, "X": 2}

        def out_key(a):
            return ("X", a["l"], 2 * a["h"]) if a["kind"] == "X" else (a["kind"], a["h"])

        block = ctx.enter_context(nc.Block())

        @block.sync
        def _(sp):
            sp.dma_start(X[:, :, :], dram["x"]).then_inc(sems["d_x"], 16)
            step = RAW * RING

            def load(i, c):
                if not (isinstance(i, int) and i * step + c < RAW):
                    sp.wait_ge(sems["unit_ready"], i * step + (c - RAW + 1))
                src = dram["weights"][bass.ds(i * step + c, 1)].rearrange("a p n -> (a p) n")
                sp.dma_start(raw[c % RAW][:, :], src).then_inc(raw_landed[c % RAW], 16)

            for c in range(step):
                load(0, c)
            with sp.Fori(1, NU // step) as i:
                for c in range(step):
                    load(i, c)
            assert NU % step
            for c in range(NU % step):
                load(NU // step, c)
            for m in range(DC):
                sp.wait_ge(*on("fin", m))
                sp.dma_start(dram["out"][:, m, :], X[:, m, :]).then_inc(sems["d_out"], 16)
            sp.wait_ge(sems["d_out"], 16 * DC)

        @block.gpsimd
        def _(pool):
            step = RAW * RING

            def await_unit(i, c):
                pool.wait_ge(raw_landed[c % RAW], (i * RING + (c // RAW + 1)) * 16)
                if not (isinstance(i, int) and i * step + c < RING):
                    pool.wait_ge(sems["unit_free"], i * step + (c - RING + 1))

            def high(c):
                pool.tensor_scalar(whi[c % RING][:, :], raw[c % RAW][:, :], 1.0, 0.0, ALU.mult,
                                   ALU.add).then_inc(sems["unit_hi"], 1)

            def split(i, c, more=True):
                if more:
                    await_unit(i, c + 1)
                pool.wait_ge(sems["unit_hi"], i * step + (c + 1))
                pool.tensor_tensor(wlo[c % RING][:, :], raw[c % RAW][:, :], whi[c % RING][:, :].bitcast(F32),
                                   ALU.subtract).then_inc(sems["unit_ready"], 1)
                if more:
                    high(c + 1)

            await_unit(0, 0)
            high(0)
            for c in range(step):
                split(0, c)
            with pool.Fori(1, NU // step) as i:
                for c in range(step):
                    split(i, c)
            for c in range(NU % step):
                split(NU // step, c, c + 1 < NU % step)

        @block.tensor
        def _(pe):
            free = {}

            def wait_free(slot):
                if slot in free:
                    pe.wait_ge(*on(*free[slot]))

            def three(out, hi, lo, xhi, xlo, start, stop):
                pe.matmul(out, hi, xhi, start=start, stop=False)
                pe.matmul(out, hi, xlo, start=False, stop=False)
                return pe.matmul(out, lo, xhi, start=False, stop=stop)

            def norm_sum(kind, norm):
                mem = kind == "rstdm"
                n = NM if mem else T
                pe.wait_ge(*on("ms" if mem else "xs", (norm, DC - 1)))
                wait_free("O")
                pe.matmul(O[:, 0:n], ones[:, :], SSUM[:, 0:n], start=True, stop=True)\
                    .then_inc(*sig("sum", (kind, norm)))
                free["O"] = ("msd" if mem else "sd", norm)

            for kind, a in SCHEDULE.steps:
                if kind == "setup":
                    pe.wait_ge(sems["d_consts"], 96)
                    pe.wait_ge(*on("setup", "prod"))
                    pe.matmul(O[:, 0:2], ones[0:64, :], small[0:64, 0:2], start=True, stop=True)\
                        .then_inc(*sig("lam_mm"))
                    free["O"] = ("lam_exp", None)
                elif kind in ("rstd", "rstdm"):
                    norm_sum(kind, a["n"])
                elif kind == "job":
                    xhi, xlo = parts[a["rhs"]]
                    n = a["n"]
                    out = bank(a["j"])[:, 0:n]
                    if a["j"] >= 3:
                        pe.wait_ge(*on("evac", a["j"] - 3))
                    for k in range(a["nk"]):
                        tile = a["tile0"] + k
                        c = tile % UT
                        if c == 0 or k == 0:
                            pe.wait_ge(sems["unit_ready"], tile // UT + 1)
                        for key in a.get("need", {}).get(k, []):
                            pe.wait_ge(*on(*key))
                        if a.get("first"):
                            pe.wait_ge(sems["fhl"], counts.value("fhl", ("base", a["norm"])) + k + 1)
                        hi = whi[tile // UT % RING][:, c * P:(c + 1) * P]
                        lo = wlo[tile // UT % RING][:, c * P:(c + 1) * P]
                        mm = three(out, hi, lo, xhi[:, k, 0:n], xlo[:, k, 0:n], k == 0, k == a["nk"] - 1)
                        if c == UT - 1:
                            mm.then_inc(*sig("unit_free", tile // UT))
                        elif k == a["nk"] - 1:
                            mm.then_inc(*sig("job_mid", a["j"]))
                elif kind == "hnorm":
                    pe.wait_ge(*on("hsq", a["id"]))
                    wait_free("O")
                    lhs = halves if a["ones"] == "halves" else ones
                    pe.matmul(O[:, 0:a["n"]], lhs[:, :], SQ[:, a["sq"], 0:a["n"]], start=True, stop=True)\
                        .then_inc(*sig("hsum", a["id"]))
                    free["O"] = ("hsd", a["id"])
                elif kind == "vturn":
                    pe.wait_ge(*on(*a["need"]))
                    wait_free("T")
                    src = buf(a["src"])
                    for t in range(a["nt"]):
                        mm = pe.transpose(TR[:, t * P:(t + 1) * P], src[:, t * P:(t + 1) * P], ident[:, :])
                    mm.then_inc(*sig("vt", a["id"]))
                    free["T"] = ("v", a["id"])
                elif kind == "score":
                    i, h, t, what = a["i"], a["h"], a["t"], a["kind"]
                    if t == 0:
                        for key in a["need"]:
                            pe.wait_ge(*on(*key))
                    wait_free("S")
                    tt = slice(t * P, (t + 1) * P)
                    if what == "A":
                        for c in range(2):
                            r = slice(64 * c, 64 * c + 64)
                            mm = pe.matmul(S[:, c * T:(c + 1) * T], AQ[r, h, tt], AK[r, h, :], start=True, stop=True)
                    elif what == "B":
                        q, k = BQ[h % 2], BK[h % 2]
                        pe.matmul(S[:, 0:T], q[:, 0, tt], k[:, 0, :], start=True, stop=True)
                        for g in (1, 2):
                            o = T + (g - 1) * P
                            mm = pe.matmul(S[:, o:o + P], q[:, g, tt], k[:, g, tt], start=True, stop=True)
                    elif what == "C":
                        mm = pe.matmul(S[:, 0:NM], CQ[:, h, tt], CK[:, h, :], start=True, stop=True)
                    else:
                        for c in range(2):
                            mm = pe.matmul(S[:, 0:NM], XQ[:, 2 * h + c, tt], XK[:, 2 * h + c, :],
                                           start=(c == 0), stop=(c == 1))
                    mm.then_inc(*sig("score", i))
                    free["S"] = ("nmax", i) if what in "AB" else ("exp", i)
                elif kind == "turn":
                    i = a["i"]
                    pe.wait_ge(*on("pn", i))
                    wait_free("T")
                    for c in range(kinds[a["kind"]]):
                        mm = pe.transpose(TR[:, c * P:(c + 1) * P], SP[:, i % 2, c * P:(c + 1) * P], ident[:, :])
                    mm.then_inc(*sig("turned", i))
                    free["T"] = ("pt", i)
                elif kind == "pv":
                    i, h, what = a["i"], a["h"], a["kind"]
                    pe.wait_ge(*on("pt", i))
                    for key in a["need_v"]:
                        pe.wait_ge(*on(*key))
                    wait_free("O")
                    if what == "A":
                        for c in range(NT):
                            mm = pe.matmul(O, AV[:, h, c * P:(c + 1) * P], PT[:, c, :], start=(c == 0), stop=(c == NT - 1))
                    elif what == "B":
                        v = BV[h % 2]
                        pe.matmul(O, v[:, 0, 0:P], PT[:, 0, :], start=True, stop=False)
                        for g in (1, 2):
                            for c in range(NT):
                                tt = slice(c * P, (c + 1) * P)
                                pe.matmul(O[:, tt], v[:, g, tt], PT[:, 3 + g, tt], start=False, stop=False,
                                          skip_group_check=True)
                        for c in range(1, NT):
                            mm = pe.matmul(O, v[:, 0, c * P:(c + 1) * P], PT[:, c, :], start=False, stop=(c == NT - 1))
                    elif what == "C":
                        for c in range(2):
                            mm = pe.matmul(O, CV[:, h, c * P:(c + 1) * P], PT[:, c, :], start=(c == 0), stop=(c == 1))
                    else:
                        for c in range(2):
                            mm = pe.matmul(O, XV[:, 2 * h, c * P:(c + 1) * P], PT[:, c, :], start=(c == 0), stop=(c == 1))
                        mm.then_inc(*sig("pv", (i, 0)))
                        wait_free("T")
                        for c in range(2):
                            mm = pe.matmul(TR[:, 0:T], XV[:, 2 * h + 1, c * P:(c + 1) * P], PT[:, c, :],
                                           start=(c == 0), stop=(c == 1))
                        free["T"] = ("olo", ("X", a["l"], 2 * h + 1))
                    mm.then_inc(*sig("pv", i))
                    free["O"] = ("pvd", ("A", h)) if what == "A" else ("olo", out_key(a))
                elif kind == "ffn":
                    n, u0 = a["n"], a["unit0"]
                    fg0, fu0 = counts.value("fg", ("base", n)), counts.value("fu", ("base", n))
                    for slot in "ST":
                        wait_free(slot)

                    def gate_up(i):
                        for jj in range(2):
                            for w, (name, first) in enumerate((("fg", fg0), ("fu", fu0))):
                                c = 2 * jj + w
                                pe.wait_ge(sems["unit_ready"], i * 4 + (u0 + c + 1))
                                if not isinstance(i, int):
                                    pe.wait_ge(sems[name], i * 2 + (first + jj - 1))
                                for k in range(DC):
                                    if isinstance(i, int) and jj == 0 and w == 0:
                                        pe.wait_ge(*on("xl", (n, k)))
                                    cc = slice(k * P, (k + 1) * P)
                                    r = (u0 + c) % RING
                                    mm = three(PS[:, c, :], whi[r][:, cc], wlo[r][:, cc], XH[:, k, :], XL[:, k, :],
                                               k == 0, k == DC - 1)
                                mm.then_inc(sems["unit_free"], 1)
                                if isinstance(i, int) and jj == 0 and w == 0:
                                    norm_sum("rstd", n)

                    gate_up(0)
                    with pe.Fori(1, NF // 2) as i:
                        gate_up(i)
                    for u in range(2 * NF):
                        counts.mark("unit_free", u0 + u)
                    free["S"] = free["T"] = ("fu", ("end", n))
                elif kind == "level":
                    l, pr, li = a["l"], a["pr"], a["li"]
                    slot, out = ("S", S) if li % 2 == 0 else ("T", TR)
                    pe.wait_ge(*on("hprep", (l, pr)) if li == 0 else on("qkt", (l, pr, li)))
                    wait_free(slot)
                    q, k = (HQ[pr], HK) if li == 0 else (QT, KT)
                    for hh in range(2):
                        o = hh * T
                        if 1 <= li <= 7:
                            size = 1 << (li - 1)
                            for c in range(NT):
                                def second(ap):
                                    return ap.rearrange("p (b two h) -> p b two h", two=2, h=size)[:, :, 1, :]
                                mm = pe.matmul(second(out[:, o + c * P:o + (c + 1) * P]), k[:, hh, c * P:(c + 1) * P],
                                               second(q[:, hh, c * P:(c + 1) * P]), start=True, stop=True)
                            continue
                        if li == 0:
                            pairs = [(c, c, c + 1, c) for c in range(NT)]
                        elif li == 8:
                            pairs = [(0, 1, 2, 0), (2, 3, 4, 1)]
                        else:
                            pairs = [(0, 2, 4, 0), (1, 2, 4, 2)]
                        for sc, t0, t1, at in pairs:
                            w = (t1 - t0) * P
                            mm = pe.matmul(out[:, o + at * P:o + at * P + w], k[:, hh, sc * P:(sc + 1) * P],
                                           q[:, hh, t0 * P:t1 * P], start=True, stop=True)
                    mm.then_inc(*sig("lev", (l, pr, li)))
                    free[slot] = ("lvd", (l, pr, li))
                elif kind == "hout":
                    l, pr, hh = a["l"], a["pr"], a["hh"]
                    pe.wait_ge(*on("lvd", (l, pr, 9)))
                    pe.wait_ge(*on("v", (l, 2 * pr + hh)))
                    wait_free("O")
                    v = HV[pr][:, hh, :]
                    near, far = A128[:, hh, :, :], A256[:, hh, :, :]
                    terms = [[(0, AD[:, hh, 0, :])],
                             [(1, AD[:, hh, 1, :]), (0, near[:, 0, :])],
                             [(2, AD[:, hh, 2, :]), (0, far[:, 0, 0:P]), (1, far[:, 1, 0:P])],
                             [(3, AD[:, hh, 3, :]), (2, near[:, 1, :]), (0, far[:, 0, P:2 * P]), (1, far[:, 1, P:2 * P])]]
                    for t, group in enumerate(terms):
                        for x, (sc, w) in enumerate(group):
                            mm = pe.matmul(O[:, t * P:(t + 1) * P], v[:, sc * P:(sc + 1) * P], w, start=(x == 0),
                                           stop=(x == len(group) - 1))
                    mm.then_inc(*sig("ho_mm", (l, 2 * pr + hh)))
                    free["O"] = ("ho", (l, 2 * pr + hh))
                elif kind == "pool":
                    l, g = a["l"], a["g"]
                    pe.wait_ge(*on("ptmp", (l, g)))
                    pe.wait_ge(sems["d_poolw"], 16 * (l + 1))
                    wait_free("O")
                    pe.matmul(O, PW[:, g, :], UB[:, pool_slot(g), :], start=True, stop=True).then_inc(*sig("pool_mm", (l, g)))
                    free["O"] = ("pooled", (l, g))

        @block.scalar
        def _(act):
            def copy(out, in_, scale=1.0):
                return act.activation(out, in_, ACT.Copy, scale=scale)

            def root(n):
                act.wait_ge(*on("sum", ("rstd", n)))
                act.activation(RSTD[:, :], O, ACT.Sqrt, bias=EPS, scale=1.0 / D).then_inc(*sig("sd", n))

            sd_reader = [None]
            for kind, a in SCHEDULE.steps:
                if kind == "setup":
                    for t, name in ((cols, "cols"), (ones, "ones"), (halves, "halves"), (ident, "ident"),
                                    (masks_f, "masks"), (poolrec, "poolrec")):
                        act.dma_start(t[tuple([slice(None)] * len(t.shape))], dram[name]).then_inc(sems["d_consts"], 16)
                    act.wait_ge(*on("lam_mm"))
                    act.activation(small[:, 2:4], O[:, 0:2], ACT.Exp).then_inc(*sig("lam_exp"))
                    act.wait_ge(*on("setup", "lbd"))
                    act.activation(small[:, 12:20], small[:, 12:20], ACT.Exp).then_inc(*sig("lb_exp"))
                elif kind == "refresh":
                    n, m = a["n"], a["m"]
                    if n == 0:
                        act.wait_ge(sems["d_x"], 16)
                        act.wait_ge(sems["d_consts"], 96)
                    else:
                        act.wait_ge(*on(*a["need"]))
                    if a["sq_free"]:
                        act.wait_ge(*on(*a["sq_free"]))
                    act.activation(SQ[:, a["sq"], :], X[:, m, :], ACT.Square).then_inc(*sig("sq", (n, m)))
                    if a["gain"] != "final_norm_2":
                        copy(XH[:, m, :], X[:, m, :], col(a["gain"], m)).then_inc(*sig("xh", (n, m)))
                elif kind == "memload":
                    if a["after"]:
                        act.wait_ge(*on(*a["after"]))
                    if a["n"] == 0:
                        act.dma_start(MRAW[:, :, :], dram["mem0"]).then_inc(sems["d_mem"], 16)
                    else:
                        for x in range(2):
                            act.dma_start(MRAW2[x][:, :, :], dram["mem1"][:, 4 * x:4 * x + 4, :])\
                                .then_inc(sems["d_mem"], 16)
                elif kind == "memfresh":
                    n, m = a["n"], a["m"]
                    act.wait_ge(sems["d_mem"], 16 * (2 * n + 1))
                    raw_m, hi, _ = mem_tensors(n, m)
                    act.wait_ge(*on(*a["sq_free"]))
                    act.activation(SQ[:, a["sq"], 0:NM], raw_m, ACT.Square).then_inc(*sig("msq", (n, m)))
                    copy(hi[:, m, :], raw_m, col(a["gain"], m)).then_inc(*sig("mh", (n, m)))
                elif kind == "rstd":
                    root(a["n"])
                elif kind == "rstdm":
                    act.wait_ge(*on("sum", (kind, a["n"])))
                    act.activation(RSTDM[:, :], O[:, 0:NM], ACT.Sqrt, bias=EPS, scale=1.0 / D).then_inc(*sig("msd", a["n"]))
                elif kind == "hsq":
                    for key in a["need"]:
                        act.wait_ge(*on(*key))
                    act.wait_ge(*on(*a["sq_free"]))
                    act.activation(SQ[:, a["sq"], 0:a["n"]], buf(a["src"]), ACT.Square).then_inc(*sig("hsq", a["id"]))
                elif kind == "hnorm":
                    act.wait_ge(*on("hsum", a["id"]))
                    if sd_reader[0] is not None:
                        act.wait_ge(*on("hrec", sd_reader[0]))
                    sd = HSD if a["id"][0] == "H" else SD
                    act.activation(sd[:, 0:a["n"]], O[:, 0:a["n"]], ACT.Sqrt, bias=EPS,
                                   scale=1.0 / a["dim"]).then_inc(*sig("hsd", a["id"]))
                    sd_reader[0] = a["id"]
                elif kind == "vturn":
                    act.wait_ge(*on("vt", a["id"]))
                    for key in a.get("dfree", []):
                        act.wait_ge(*on(*key))
                    copy(buf(a["dst"]), TR[:, 0:a["nt"] * P]).then_inc(*sig("v", a["id"]))
                elif kind == "gate":
                    act.wait_ge(*on(*a["need"]))
                    act.activation(buf(a["dst"]), buf(a["dst"]), ACT.Sigmoid,
                                   bias=col("b_gate", 8 * a["n"] + a["m"])).then_inc(*sig("gate", (a["n"], a["m"])))
                elif kind == "bias":
                    if a["after"]:
                        act.wait_ge(*on(*a["after"]))
                    w = NT * (T if a["kind"] == "A" else 768)
                    act.dma_start(BIAS[:, 0:w], dram["bias" + a["kind"]][a["h"]]).then_inc(sems["d_bias"], 16)
                elif kind == "score":
                    i, what = a["i"], a["kind"]
                    act.wait_ge(*on("nmax", i))
                    nmx, tot = pair_of(48, i), pair_of(52, i)
                    if what == "A":
                        for c in range(2):
                            p = SP[:, i % 2, c * T:(c + 1) * T]
                            act.activation(p, p, ACT.Exp, bias=nmx[:, c:c + 1], accum_out=tot[:, c:c + 1])\
                                .then_inc(*sig("exp", i))
                    elif what == "B":
                        p = SP[:, i % 2, 0:768]
                        act.activation(p, p, ACT.Exp, bias=nmx[:, 0:1], accum_out=tot[:, 0:1]).then_inc(*sig("exp", i))
                    else:
                        if i >= 2:
                            act.wait_ge(*on("turned", i - 2))
                        act.activation(SP[:, i % 2, 0:NM], S[:, 0:NM], ACT.Exp, bias=nmx[:, 0:1],
                                       scale=1.0 if what == "C" else 256 ** -0.5,
                                       accum_out=tot[:, 0:1]).then_inc(*sig("exp", i))
                elif kind == "turn":
                    i, t, nk = a["i"], a["t"], kinds[a["kind"]]
                    act.wait_ge(*on("turned", i))
                    if t == 0 and i:
                        act.wait_ge(*on("pv", i - 1))
                    copy(PT[:, 0:nk, t * P:(t + 1) * P],
                         TR[:, 0:nk * P].rearrange("p (c q) -> p c q", c=nk)).then_inc(*sig("pt", i))
                elif kind == "pv":
                    i, h, what = a["i"], a["h"], a["kind"]
                    if what == "X":
                        act.wait_ge(*on("pv", (i, 0)))
                        copy(XOH[:, 2 * h, :], O).then_inc(*sig("ohi", out_key(a)))
                        act.wait_ge(*on("pv", i))
                        copy(XOH[:, 2 * h + 1, :], TR[:, 0:T]).then_inc(*sig("ohi", ("X", a["l"], 2 * h + 1)))
                    elif what != "A":
                        act.wait_ge(*on("pv", i))
                        copy(parts["O" + what][0][:, h, :], O).then_inc(*sig("ohi", out_key(a)))
                elif kind == "split":
                    for key in a["need"]:
                        act.wait_ge(*on(*key))
                    hi = (OAH if a["dst"][0] == "OA" else MIXH)[:, a["dst"][1], :]
                    copy(hi, buf(a["src"])).then_inc(*sig("ohi", a["id"]))
                elif kind == "evac" and a["evac"] == "branch" and a["b"] == 2:
                    act.wait_ge(*on("y", (2, a["m"])))
                    copy(YH[:, a["m"], :], X[:, a["m"], :]).then_inc(*sig("yhi", a["m"]))
                elif kind == "reload":
                    act.wait_ge(*on("ylo", DC - 1))
                    act.wait_ge(*own("act"))
                    act.dma_start(X[:, :, :], dram["x"]).then_inc(sems["d_reload"], 16)
                elif kind == "ffn":
                    n = a["n"]
                    fg0 = counts.value("fg", ("base", n))
                    counts.at[("silu", ("base", n))] = counts.now.get("silu", 0)
                    root(n)

                    def silu(i):
                        for jj in range(2):
                            act.wait_ge(sems["fg"], i * 2 + (fg0 + jj + 1))
                            act.activation(FS[:, :], FG[:, :], ACT.Silu).then_inc(sems["silu"], 1)

                    silu(0)
                    with act.Fori(1, NF // 2) as i:
                        silu(i)
                    counts.mark("silu", ("end", n), NF)
                    last["act"] = (sems["silu"], counts.now["silu"])
                elif kind == "poolload":
                    act.wait_ge(*on(*a["after"]))
                    act.dma_start(PW[:, :, :], dram["pool_w"][:, a["l"]]).then_inc(sems["d_poolw"], 16)
                elif kind == "hprep":
                    l, pr = a["l"], a["pr"]
                    act.wait_ge(*on(*a["need"]))
                    if pr:
                        act.wait_ge(*on("lvd", (l, 0, 9)))
                    act.activation(HK[:, :, :], HF[pr][:, :, :], ACT.Sigmoid, scale=-1.0).then_inc(*sig("sigm", (l, pr, 0)))
                    act.wait_ge(*own("act"))
                    act.activation(HF[pr][:, :, :], HF[pr][:, :, :], ACT.Sigmoid).then_inc(*sig("sigm", (l, pr, 1)))
                    act.activation(HG[pr][:, :, :], HG[pr][:, :, :], ACT.Silu).then_inc(*sig("hgs", (l, pr)))

        @block.vector
        def _(dve):
            def after_own():
                if "dve" in last:
                    dve.wait_ge(*own("dve"))

            def rstd(n):
                dve.wait_ge(*on("sd", n))
                dve.reciprocal(RSTD[:, :], RSTD[:, :]).then_inc(*sig("rstd", n))

            for kind, a in SCHEDULE.steps:
                if kind == "setup":
                    dve.wait_ge(sems["d_consts"], 96)
                    dve.tensor_copy(masks[:, :, :], masks_f[:, :, :]).then_inc(*sig("setup", "masks"))
                    la = COLS["lambdas"][0]
                    dve.tensor_tensor(small[0:64, 0:2], cols[0:64, la:la + 4:2], cols[0:64, la + 1:la + 4:2],
                                      ALU.mult).then_inc(*sig("setup", "prod"))
                    for name, c in (("a_q_norm", 64 ** -0.5), ("b_q_norm", P ** -0.5), ("c_q_norm", P ** -0.5),
                                    ("a_subln", 1.0 - LAMBDA_INIT)):
                        dve.tensor_scalar(col(name), col(name), c, None, ALU.mult).then_inc(*sig("setup", name))
                    l0, l1 = (cols[:, COLS[f"lb_logits_2_{l}"][0]:COLS[f"lb_logits_2_{l}"][0] + 4] for l in range(2))
                    mx, e0, e1, tot = small[:, 8:12], small[:, 12:16], small[:, 16:20], small[:, 20:24]
                    dve.tensor_tensor(mx, l0, l1, ALU.max).then_inc(*sig("setup", "lbm"))
                    after_own()
                    dve.tensor_tensor(e0, l0, mx, ALU.subtract).then_inc(*sig("setup", "lbd0"))
                    dve.tensor_tensor(e1, l1, mx, ALU.subtract).then_inc(*sig("setup", "lbd"))
                    dve.wait_ge(*on("lb_exp"))
                    dve.tensor_tensor(tot, e0, e1, ALU.add).then_inc(*sig("setup", "lbs"))
                    after_own()
                    dve.reciprocal(small[:, 24:28], tot).then_inc(*sig("setup", "lbr"))
                    after_own()
                    dve.memset(small[:, 28:32], 0.0).then_inc(*sig("setup", "lb0"))
                    dve.memset(small[:, 32:36], 1.0).then_inc(*sig("setup", "lb0n"))
                    dve.tensor_tensor(small[:, 36:40], e1, small[:, 24:28], ALU.mult).then_inc(*sig("setup", "lb1"))
                    dve.tensor_tensor(small[:, 40:44], e0, small[:, 24:28], ALU.mult).then_inc(*sig("setup", "lb1n"))
                    dve.wait_ge(*on("lam_exp"))
                    dve.scalar_tensor_tensor(LAM, small[:, 2:3], LAMBDA_INIT, small[:, 3:4], ALU.add, ALU.subtract)\
                        .then_inc(*sig("setup", "lam"))
                elif kind in ("refresh", "memfresh"):
                    n, m = a["n"], a["m"]
                    mem = kind == "memfresh"
                    w = NM if mem else T
                    sq = SQ[:, a["sq"], 0:w]
                    after_own()
                    dve.wait_ge(*on("msq" if mem else "sq", (n, m)))
                    if m == 0:
                        if a["ssum_free"]:
                            dve.wait_ge(*on(*a["ssum_free"]))
                        dve.tensor_copy(SSUM[:, 0:w], sq).then_inc(*sig("ms" if mem else "xs", (n, m)))
                    else:
                        dve.tensor_tensor(SSUM[:, 0:w], SSUM[:, 0:w], sq, ALU.add)\
                            .then_inc(*sig("ms" if mem else "xs", (n, m)))
                    if a["gain"] != "final_norm_2":
                        src, hi, lo = mem_tensors(n, m) if mem else (X[:, m, :], XH, XL)
                        dve.wait_ge(*on("mh" if mem else "xh", (n, m)))
                        dve.scalar_tensor_tensor(lo[:, m, :], src, col(a["gain"], m),
                                                 hi[:, m, :].bitcast(F32), ALU.mult, ALU.subtract)\
                            .then_inc(*sig("ml" if mem else "xl", (n, m)))
                elif kind == "rstd":
                    rstd(a["n"])
                elif kind == "rstdm":
                    dve.wait_ge(*on("msd", a["n"]))
                    dve.reciprocal(RSTDM[:, :], RSTDM[:, :]).then_inc(*sig("rstdm", a["n"]))
                elif kind == "evac":
                    out = bank(a["j"])[:, 0:a["n"]]
                    m = a.get("m")
                    for key in a.get("free", []):
                        dve.wait_ge(*on(*key))
                    after_own()
                    dve.wait_ge(*job_done(a))
                    if a["evac"] in ("scale", "scalem"):
                        r = RSTD[:, :] if a["evac"] == "scale" else RSTDM[:, :]
                        dve.tensor_tensor(buf(a["dst"])[:, 0:a["n"]], out, r, ALU.mult).then_inc(*sig("evac", a["j"]))
                    elif a["evac"] == "resid":
                        if a["rhs"] == "y" and m == 0:
                            dve.wait_ge(sems["d_reload"], 16)
                        dve.scalar_tensor_tensor(X[:, m, :], out, a["c"], X[:, m, :], ALU.mult, ALU.add)\
                            .then_inc(*sig("evac", a["j"]))
                    elif a["evac"] == "back":
                        dve.tensor_tensor(FG[:, :], out, X[:, m, :], ALU.add).then_inc(*sig("evac", a["j"]))
                        after_own()
                        dve.tensor_copy(X[:, m, :].rearrange("p (s r) -> p s r", r=NT),
                                        FG[:, :].rearrange("p (r s) -> p s r", r=NT)).then_inc(*sig("x", m))
                    else:
                        b = a["b"]
                        dve.wait_ge(*on("gate", (b, m)))
                        y = X[:, m, :]
                        if b == 0:
                            dve.tensor_tensor(y, out, y, ALU.mult).then_inc(*sig("evac", a["j"]))
                        else:
                            g = buf(a["gate"])
                            dve.tensor_tensor(g, out, g, ALU.mult).then_inc(*sig("evac", a["j"]))
                            after_own()
                            dve.tensor_tensor(y, y, g, ALU.add).then_inc(*sig("y", (b, m)))
                            if b == 2:
                                dve.wait_ge(*on("yhi", m))
                                dve.tensor_tensor(YL[:, m, :], y, YH[:, m, :].bitcast(F32), ALU.subtract)\
                                    .then_inc(*sig("ylo", m))
                elif kind == "hnorm":
                    n = a["n"]
                    sd, rec = (HSD, HREC[a["id"][2] // 2]) if a["id"][0] == "H" else (SD, REC)
                    after_own()
                    dve.wait_ge(*on("hsd", a["id"]))
                    dve.reciprocal(rec[:, 0:n], sd[:, 0:n]).then_inc(*sig("hrec", a["id"]))
                    after_own()
                    dve.scalar_tensor_tensor(buf(a["src"]), buf(a["src"]), gain_of(a["gain"]), rec[:, 0:n],
                                             ALU.mult, ALU.mult).then_inc(*sig("hn", a["id"]))
                elif kind == "score":
                    i, t, what = a["i"], a["t"], a["kind"]
                    mx, nmx = pair_of(44, i), pair_of(48, i)
                    after_own()
                    if t == 0 and what in "AB":
                        dve.wait_ge(sems["d_bias"], 16 * a["nbias"])
                    if i >= 2 and what in "AB":
                        dve.wait_ge(*on("turned", i - 2))
                    dve.wait_ge(*on("score", i))
                    n = 1
                    if what == "A":
                        n = 2
                        for c in range(2):
                            dve.tensor_tensor_reduce(SP[:, i % 2, c * T:(c + 1) * T], S[:, c * T:(c + 1) * T],
                                                     BIAS[:, t * T:(t + 1) * T], 1.0, -1e30, ALU.add, ALU.max,
                                                     mx[:, c:c + 1]).then_inc(*sig("max", i))
                    elif what == "B":
                        dve.tensor_tensor_reduce(SP[:, i % 2, 0:768], S[:, 0:768], BIAS[:, t * 768:(t + 1) * 768],
                                                 1.0, -1e30, ALU.add, ALU.max, mx[:, 0:1]).then_inc(*sig("max", i))
                    else:
                        dve.tensor_reduce(mx[:, 0:1], S[:, 0:NM], AX.X, ALU.max).then_inc(*sig("max", i))
                    after_own()
                    dve.tensor_scalar(nmx[:, 0:n], mx[:, 0:n], -(256 ** -0.5) if what == "X" else -1.0, None,
                                      ALU.mult).then_inc(*sig("nmax", i))
                elif kind == "turn":
                    i, what = a["i"], a["kind"]
                    tot, rs = pair_of(52, i), pair_of(56, i)
                    n = 2 if what == "A" else 1
                    w = kinds[what] * P
                    after_own()
                    dve.wait_ge(*on("exp", i))
                    dve.reciprocal(rs[:, 0:n], tot[:, 0:n]).then_inc(*sig("ptmp", ("r", i)))
                    after_own()
                    p = SP[:, i % 2, 0:w]
                    if what == "A":
                        q = SP[:, i % 2, T:2 * T]
                        dve.tensor_scalar(q, q, rs[:, 1:2], LAM, ALU.mult, ALU.mult).then_inc(*sig("ptmp", ("q", i)))
                        after_own()
                        dve.scalar_tensor_tensor(p, p, rs[:, 0:1], q, ALU.mult, ALU.subtract).then_inc(*sig("pn", i))
                    else:
                        dve.tensor_scalar(p, p, rs[:, 0:1], None, ALU.mult).then_inc(*sig("pn", i))
                elif kind == "pv":
                    h, what = a["h"], a["kind"]
                    after_own()
                    if what == "A":
                        dve.wait_ge(*on("pv", a["i"]))
                        dve.tensor_copy(AO[:, h, :], O).then_inc(*sig("pvd", ("A", h)))
                    elif what == "X":
                        for c, src in ((0, O), (1, TR[:, 0:T])):
                            key = ("X", a["l"], 2 * h + c)
                            dve.wait_ge(*on("ohi", key))
                            dve.tensor_tensor(XOL[:, 2 * h + c, :], src, XOH[:, 2 * h + c, :].bitcast(F32),
                                              ALU.subtract).then_inc(*sig("olo", key))
                    else:
                        hi, lo = parts["O" + what]
                        dve.wait_ge(*on("ohi", out_key(a)))
                        dve.tensor_tensor(lo[:, h, :], O, hi[:, h, :].bitcast(F32), ALU.subtract)\
                            .then_inc(*sig("olo", out_key(a)))
                elif kind == "split":
                    hi, lo = (OAH, OAL) if a["dst"][0] == "OA" else (MIXH, MIXL)
                    c = a["dst"][1]
                    after_own()
                    dve.wait_ge(*on("ohi", a["id"]))
                    dve.tensor_tensor(lo[:, c, :], buf(a["src"]), hi[:, c, :].bitcast(F32), ALU.subtract)\
                        .then_inc(*sig("olo", a["id"]))
                elif kind == "ffn":
                    n, u0 = a["n"], a["unit0"]
                    first = {w: counts.now.get(w, 0) for w in ("fg", "fu", "fm", "fhh", "fhl")}
                    for w in first:
                        counts.at[(w, ("base", n))] = first[w]
                    silu0 = counts.value("silu", ("base", n))
                    rstd(n)
                    three_d = [P, 1, T]

                    def chunk(i, jj):
                        peeled = isinstance(i, int)
                        f = i * 2 + jj

                        def at(w):
                            return i * 2 + (first[w] + jj + 1)
                        if peeled and jj == 0:
                            after_own()
                        else:
                            dve.wait_ge(sems["fhl"], i * 2 + (first["fhl"] + jj))
                        dve.wait_ge(sems["unit_free"], i * 4 + (u0 + 2 * jj + 1))
                        dve.tensor_tensor(FG[:, :], PS[:, 2 * jj, :], RSTD[:, :], ALU.mult).then_inc(sems["fg"], 1)
                        dve.wait_ge(sems["unit_free"], i * 4 + (u0 + 2 * jj + 2))
                        dve.tensor_tensor(FU[:, :], PS[:, 2 * jj + 1, :], RSTD[:, :], ALU.mult).then_inc(sems["fu"], 1)
                        dve.wait_ge(sems["silu"], i * 2 + (silu0 + jj + 1))
                        dve.wait_ge(sems["fu"], at("fu"))
                        dve.tensor_tensor(FM[:, :], FS[:, :], FU[:, :], ALU.mult).then_inc(sems["fm"], 1)
                        dve.wait_ge(sems["fm"], at("fm"))
                        fm = FM[:, :].rearrange("p (a n) -> p a n", a=1)
                        hh = HH[:, f:f + 1, :] if peeled else HH[:, bass.ds(f, 1), :]
                        hl = HL[:, f:f + 1, :] if peeled else HL[:, bass.ds(f, 1), :]
                        dve.tensor_scalar(hh, fm, 1.0, None, ALU.mult).then_inc(sems["fhh"], 1)
                        dve.wait_ge(sems["fhh"], at("fhh"))
                        dve.tensor_tensor(hl, fm, hh.bitcast(F32), ALU.subtract).then_inc(sems["fhl"], 1)

                    for jj in range(2):
                        chunk(0, jj)
                    with dve.Fori(1, NF // 2) as i:
                        for jj in range(2):
                            chunk(i, jj)
                    for w in first:
                        counts.mark(w, ("end", n), NF)
                    last["dve"] = (sems["fhl"], counts.now["fhl"])
                elif kind == "hprep":
                    l, pr = a["l"], a["pr"]
                    after_own()
                    dve.memset(HS[:, :, :], 1.0).then_inc(*sig("hprep", (l, pr, "s")))
                    for hh in range(2):
                        h = 2 * pr + hh
                        dve.wait_ge(*on("sigm", (l, pr, 1)))
                        dve.tensor_scalar(HK[:, hh, :], HK[:, hh, :], one_minus_lb(l, h), None, ALU.mult)\
                            .then_inc(*sig("hprep", (l, pr, "k", hh)))
                        dve.tensor_scalar(HF[pr][:, hh, :], HF[pr][:, hh, :], one_minus_lb(l, h), lb(l, h),
                                          ALU.mult, ALU.add).then_inc(*sig("hprep", (l, pr) if hh else (l, pr, "f")))
                elif kind == "level":
                    l, pr, li = a["l"], a["pr"], a["li"]

                    def blocks(t, h):
                        return t[:, :, :].rearrange("p a t -> p (a t)").rearrange("p (b two h) -> p b two h", two=2, h=h)
                    q, pre, size = HQ[pr], HF[pr], 1 << max(li - 1, 0)
                    if li == 1:
                        after_own()
                        dve.tensor_tensor(QT[:, :, :], q[:, :, :], pre[:, :, :], ALU.mult)\
                            .then_inc(*sig("qkt", (l, pr, "q", li)))
                        dve.tensor_copy(KT[:, :, :], HK[:, :, :]).then_inc(*sig("qkt", (l, pr, li)))
                    elif li > 1:
                        after_own()
                        dve.wait_ge(*on("lev", (l, pr, li - 1)))
                        dve.tensor_tensor(blocks(QT, size)[:, :, 1, :], blocks(q, size)[:, :, 1, :],
                                          blocks(pre, size)[:, :, 1, :], ALU.mult).then_inc(*sig("qkt", (l, pr, "q", li)))
                        dve.tensor_tensor(blocks(KT, size)[:, :, 0, :], blocks(HK, size)[:, :, 0, :],
                                          blocks(HS, size)[:, :, 0, :], ALU.mult).then_inc(*sig("qkt", (l, pr, li)))
                    if 1 <= li < 9:
                        b, s = blocks(pre, size), blocks(HS, size)
                        nb = 2 * T // (2 * size)
                        after_own()
                        dve.tensor_tensor(s[:, :, 0, :], s[:, :, 0, :],
                                          b[:, :, 1, size - 1:size].broadcast_to([P, nb, size]), ALU.mult)\
                            .then_inc(*sig("qkt", (l, pr, "s", li)))
                        after_own()
                        dve.tensor_tensor(b[:, :, 1, :], b[:, :, 1, :],
                                          b[:, :, 0, size - 1:size].broadcast_to([P, nb, size]), ALU.mult)\
                            .then_inc(*sig("qkt", (l, pr, "p", li)))
                    src = S if li % 2 == 0 else TR
                    tiles = src.rearrange("p (c t) -> p c t", t=P)
                    ad = AD[:, :, :, :].rearrange("p a c t -> p (a c) t")
                    after_own()
                    dve.wait_ge(*on("lev", (l, pr, li)))
                    if li == 0:
                        dve.tensor_tensor(ad, tiles, ident[:, :].rearrange("p (a t) -> p a t", a=1)
                                          .broadcast_to([P, 2 * NT, P]), ALU.mult).then_inc(*sig("lvd", (l, pr, li)))
                    elif li <= 7:
                        def second(ap):
                            return ap.rearrange("p c (b two h) -> p c b two h", two=2, h=size)[:, :, :, 1, :]
                        mask = masks[:, li - 1, :].rearrange("p (b two h) -> p b two h", two=2, h=size)[:, :, 1, :]
                        mask = mask.rearrange("p b h -> p () b h").broadcast_to([P, 2 * NT, P // 2 // size, size])
                        dve.copy_predicated(second(ad), mask, second(tiles)).then_inc(*sig("lvd", (l, pr, li)))
                    elif li == 8:
                        dve.tensor_copy(A128[:, :, :, :].rearrange("p a c t -> p a (c t)"),
                                        src.rearrange("p (a t) -> p a t", a=2)[:, :, 0:2 * P])\
                            .then_inc(*sig("lvd", (l, pr, li)))
                    else:
                        dve.tensor_copy(A256[:, :, :, :].rearrange("p a c t -> p (a c t)"), src)\
                            .then_inc(*sig("lvd", (l, pr, li)))
                elif kind == "hout":
                    h = 2 * a["pr"] + a["hh"]
                    after_own()
                    dve.wait_ge(*on("ho_mm", (a["l"], h)))
                    dve.tensor_copy(HO[a["pr"]][:, a["hh"], :], O).then_inc(*sig("ho", (a["l"], h)))
                elif kind == "hgate":
                    h = 2 * a["pr"] + a["hh"]
                    after_own()
                    dve.wait_ge(*on("hgs", (a["l"], a["pr"])))
                    dve.tensor_tensor(HO[a["pr"]][:, a["hh"], :], HO[a["pr"]][:, a["hh"], :], HG[a["pr"]][:, a["hh"], :], ALU.mult)\
                        .then_inc(*sig("hgated", (a["l"], h)))
                elif kind == "poolsum":
                    l, g = a["l"], a["g"]
                    w = 2 << g
                    cur, d = 0, 1
                    while d < w:
                        nxt = 1 if cur != 1 else 2
                        after_own()
                        dve.tensor_tensor(UB[:, nxt, d:T], UB[:, cur, d:T], UB[:, cur, 0:T - d], ALU.add)\
                            .then_inc(*sig("ptmp", (l, g, d)))
                        dve.tensor_copy(UB[:, nxt, 0:d], UB[:, cur, 0:d]).then_inc(*sig("ptmp", (l, g, d, "h")))
                        cur, d = nxt, 2 * d
                    assert cur == pool_slot(g)
                    s = UB[:, cur, :]
                    after_own()
                    dve.tensor_tensor(s[:, 0:w], s[:, 0:w], poolrec[:, g, 0:w], ALU.mult).then_inc(*sig("ptmp", (l, g, "a")))
                    after_own()
                    dve.tensor_tensor(s[:, 0:w], s[:, 0:w], UB[:, 0, 0:w], ALU.subtract).then_inc(*sig("ptmp", (l, g, "b")))
                    dve.scalar_tensor_tensor(s[:, w:T], s[:, w:T], 1.0 / w, UB[:, 0, w:T], ALU.mult, ALU.subtract)\
                        .then_inc(*sig("ptmp", (l, g)))
                elif kind == "pool":
                    l, g = a["l"], a["g"]
                    after_own()
                    dve.wait_ge(*on("pool_mm", (l, g)))
                    dve.tensor_scalar(UB[:, 1, :], O, col(f"pool_scale_2_{l}", g), None, ALU.mult)\
                        .then_inc(*sig("pooled", (l, g)))
                elif kind == "final":
                    for m in range(DC):
                        after_own()
                        dve.scalar_tensor_tensor(X[:, m, :], X[:, m, :], col("final_norm_2", m), RSTD[:, :],
                                                 ALU.mult, ALU.mult).then_inc(*sig("fin", m))


def pool_slot(g):
    return 1 if g % 2 == 0 else 2


def tokens_by_residue(a):
    return a.reshape(T // NT, NT, *a.shape[1:]).swapaxes(0, 1).reshape(a.shape)


def feature_major(a):
    return np.ascontiguousarray(a.T.reshape(DC, P, a.shape[0]).transpose(1, 0, 2))


def distance_constants():
    pos = tokens_by_residue(np.arange(T))
    dist = np.abs(pos[:, None] - pos[None, :]).astype(np.float32)
    out_of = np.float32(-1e30)
    slopes_a = [2.0 ** (-8.0 * (i + 1) / NHEAD) for i in range(NHEAD)]
    slopes_b = np.exp2(-8.0 * np.arange(1, 13, dtype=np.float32) / np.float32(12)).astype(np.float32).reshape(3, NHEAD)
    bias_a = np.stack([(-np.float32(s) * dist).reshape(NT, P, T).transpose(1, 0, 2).reshape(P, -1) for s in slopes_a])
    sub = np.arange(P)
    rel = np.abs(sub[:, None] - sub[None, :])
    bias_b = []
    for h in range(NHEAD):
        g0 = np.where(dist <= 64, -slopes_b[0, h] * dist, out_of).reshape(NT, P, T).transpose(1, 0, 2)
        g1 = np.where(rel <= 64, -slopes_b[1, h] * (4 * rel).astype(np.float32), out_of)
        g2 = np.where(rel % 4 == 0, -slopes_b[2, h] * (4 * rel).astype(np.float32), out_of)
        rest = np.broadcast_to(np.concatenate([g1, g2], 1)[:, None, :], (P, NT, 2 * P))
        bias_b.append(np.concatenate([g0, rest], 2).reshape(P, -1))
    return bias_a.astype(np.float32), np.stack(bias_b).astype(np.float32)


def constants():
    t = np.arange(P)
    masks = []
    for li in range(7):
        h = 1 << li
        same = t[:, None] // (2 * h) == t[None, :] // (2 * h)
        masks.append(same & (t[:, None] % (2 * h) < h) & (t[None, :] % (2 * h) >= h))
    rec = np.zeros((P, 4, 16), np.float32)
    for g in range(4):
        rec[:, g, :] = 1.0 / np.minimum(np.arange(1, 17), 2 << g)
    half = (t[:, None] // 64 == t[None, :] // 64).astype(np.float32)
    bias_a, bias_b = distance_constants()
    return {"ones": np.ones((P, P), np.float32), "halves": half, "ident": np.eye(P, dtype=np.float32),
            "masks": np.ascontiguousarray(np.stack(masks, 1)).astype(np.float32), "poolrec": rec,
            "biasA": bias_a, "biasB": bias_b}


def weight_units(inputs):
    out = np.empty((NU, P, UT * P), np.float32)
    for u, (name, l, tiles) in enumerate(SCHEDULE.units):
        w = inputs[name][0, l] if name == "w_branch" else inputs[name][l]
        for c, (r, k) in enumerate(tiles):
            out[u, :, c * P:(c + 1) * P] = w[r * P:(r + 1) * P, k * P:(k + 1) * P]
    return out


def vector_columns(inputs):
    out = np.zeros((P, NCOL), np.float32)
    for name, (at, n) in COLS.items():
        if name == "lambdas":
            for c, w in enumerate(("a_lambda_q1", "a_lambda_k1", "a_lambda_q2", "a_lambda_k2")):
                out[0:64, at + c] = inputs[w][0]
            continue
        base, l = (name[:-2], int(name[-1])) if name[-2:] in ("_0", "_1") else (name, 0)
        v = inputs[base] if base == "final_norm_2" else inputs[base][l]
        if v.size == 64:
            out[0:64, at] = out[64:P, at] = v
        else:
            out[:, at:at + n] = v.reshape(n, P).T
    return out


def kernel(**inputs):
    import concourse.bacc as bacc
    from concourse.bass_utils import run_bass_kernel_spmd as run

    inputs = {k: np.asarray(v) for k, v in inputs.items()}
    arrays = {"weights": weight_units(inputs), "cols": vector_columns(inputs),
              "x": feature_major(tokens_by_residue(inputs["x"][0])),
              "mem0": feature_major(inputs["mem"][0]), "mem1": feature_major(inputs["mem_2"][0]),
              "pool_w": np.ascontiguousarray(inputs["pool_w_2"].transpose(2, 0, 1, 3)), **constants()}
    known = None
    for _ in range(2):
        nc = bacc.Bacc("TRN2", target_bir_lowering=False, num_devices=1)
        dram = {k: nc.dram_tensor(f"in_{k}", a.shape, mybir.dt.from_np(a.dtype), kind="ExternalInput").ap()
                for k, a in arrays.items()}
        dram["out"] = nc.dram_tensor("out_x", (P, DC, T), F32, kind="ExternalOutput").ap()
        counts = Counts(known)
        program(nc, dram, counts)
        known = counts.at
    got = run(nc, [{f"in_{k}": a for k, a in arrays.items()}], core_ids=[0])
    out = got.results[0]["out_x"]
    return out.transpose(2, 1, 0).reshape(1, T, D)
```

```python
import math
from contextlib import ExitStack

import numpy as np

import concourse.bass as bass
from concourse import mybir

P = 128
F32 = mybir.dt.float32
F32R = mybir.dt.float32r
U8 = mybir.dt.uint8
ACT = mybir.ActivationFunctionType
ALU = mybir.AluOpType
AX = mybir.AxisListType

T = 512
NT = T // P
D = 1024
DC = D // P
NM = 256
NF = 2816 // P
EPS = 1e-6
NHEAD = 4
UT = 8
RAW = 3
SQS = 2
BIAS_SLOTS = 4
SPS = 4
RING = 4
LAMBDA_INIT = 0.8 - 0.6 * math.exp(0.0)
LAYERS = 2

KB = 1024


def column_plan():
    plan, at = {}, 0
    names = [("norm_mix", 8), ("norm_ffn", 8), ("b_gate", 24), ("mem_norm", 8), ("a_q_norm", 1), ("a_k_norm", 1),
             ("a_subln", 1), ("b_q_norm", 1), ("b_k_norm", 1), ("c_q_norm", 1), ("c_k_norm", 1)]
    for l in range(LAYERS):
        names += [(f"ffn1_norm_2_{l}", 8), (f"mix_norm_2_{l}", 8), (f"hgrn_norm_2_{l}", 4), (f"pool_scale_2_{l}", 4),
                  (f"xa_norm_2_{l}", 8), (f"mem_norm_2_{l}", 8), (f"ffn2_norm_2_{l}", 8), (f"lb_logits_2_{l}", 4)]
    names += [("final_norm_2", 8), ("lambdas", 4)]
    for name, n in names:
        plan[name] = (at, n)
        at += n
    return plan, at


COLS, NCOL = column_plan()


class Schedule:

    def __init__(self):
        self.steps = []
        self.units = []
        self.njobs = 0
        self.nsq = 0
        self.sq_reader = {}
        self.last_sum = None
        self.norms = []
        self.later = []

    def step(self, kind, /, **a):
        if kind in ("refresh", "memfresh", "hsq"):
            a["sq"] = self.nsq % SQS
            a["sq_free"] = self.sq_reader.get(a["sq"])
            self.nsq += 1
            self.sq_reader[a["sq"]] = (("hsum", a["id"]) if kind == "hsq" else
                                       ("xs" if kind == "refresh" else "ms", (a["n"], a["m"])))
        if kind in ("refresh", "memfresh") and a["m"] == 0:
            a["ssum_free"] = self.last_sum
        if kind in ("rstd", "rstdm"):
            self.last_sum = ("sum", (kind, a["n"]))
        self.steps.append((kind, a))

    def unit(self, name, l, tiles):
        self.units.append((name, l, tiles))

    def job(self, tile0, nk, /, **a):
        j = self.njobs
        self.njobs += 1
        self.step("job", j=j, tile0=tile0, nk=nk, **a)
        norms, self.norms = self.norms, []
        for kind, n in norms:
            self.step(kind, n=n)
        self.step("evac", j=j, tile0=tile0, nk=nk, **a)
        self.flush()
        return j

    def column(self, name, l, column, /, **a):
        t0 = len(self.units) * UT
        self.unit(name, l, [(k, column) for k in a.get("rows", range(DC))])
        return self.job(t0, DC, **a)

    def flush(self):
        later, self.later = self.later, []
        for go in later:
            go()

    def defer(self, go):
        self.later.append(go)


def spread(work, slots):
    state = [0, 0]

    def fill():
        state[1] += 1
        upto = len(work) * min(state[1], slots) // slots
        while state[0] < upto:
            state[0] += 1
            work[state[0] - 1]()
    return fill


def build_schedule():
    s = Schedule()
    step, column = s.step, s.column
    step("setup")
    for m in range(DC):
        step("refresh", n=0, m=m, gain="norm_mix")
    s.norms.append(("rstd", 0))

    def hnorm(id, src, gain, ones, n, dim, need):
        step("hsq", id=id, src=src, n=n, need=need)
        sq = s.steps[-1][1]["sq"]

        def rest():
            step("hnorm", id=id, ones=ones, n=n, dim=dim, sq=sq)
            step("hscale", id=id, src=src, gain=gain, n=n)
        s.defer(rest)

    def vturn(**a):
        s.defer(lambda: step("vturn", **a))

    needx = {k: [("xl", (0, k))] for k in range(DC)}
    for h in range(NHEAD):
        for w, (c, g) in enumerate((("Q", "a_q_norm"), ("K", "a_k_norm"))):
            j = column("w_in", 0, 4 * w + h, rhs="x", n=T, evac="scale", dst=("A" + c, h), need=needx)
            needx = {}
            if j == 0:
                step("consts")
            hnorm(("A" + c, h), ("A" + c, h), g, "halves", T, 64, [("evac", j)])
        if h == 0:
            step("masks")
            for i in range(BIAS_SLOTS):
                step("bias", kind="A", i=i, h=0, t=i)
        j = column("w_in", 0, 8 + h, rhs="x", n=T, evac="scale", dst=("VT", h % 2), free=[("v", ("A", h - 2))] if h >= 2 else [])
        vturn(id=("A", h), src=("VT", h % 2), nt=NT, dst=("AV", h), need=("evac", j))

    gates = []

    def gate_chunk(n, m, dst, free=()):
        j = column("w_gate", 0, 8 * n + m, rhs="x", n=T, evac="scale", dst=dst, free=list(free))
        gates.append(dict(n=n, m=m, dst=dst, need=("evac", j)))
        if n == 1 or m % 2 == 0 or m == DC - 1:
            for a in gates:
                step("gate", **a)
            gates.clear()

    ntiles = 0

    def attend(tiles, work, after_pv=None):
        nonlocal ntiles
        kind = tiles[0]["kind"]
        ahead = 1 if kind in "AB" else 2
        before = ntiles - 1
        fill = spread(work, 20 if kind == "X" else 2 * len(tiles))

        due = []

        def pv():
            for a in due:
                step("pv", **a)
                if after_pv:
                    after_pv(a["h"])
            due.clear()

        def turn(a):
            pv()
            step("turn", **a)
            if a["t"] == NT - 1:
                due.append(a)
            fill()

        for k, a in enumerate(tiles):
            a["i"] = ntiles
            if k < SPS and before >= 0:
                a["before"] = before
            step("score", **a)
            if kind in "AB":
                step("probs", **a)
                bias(ntiles + BIAS_SLOTS)
            elif k:
                step("probs", **tiles[k - 1])
            fill()
            if k >= ahead:
                turn(tiles[k - ahead])
            ntiles += 1
        if kind not in "AB":
            step("probs", **tiles[-1])
        for a in tiles[-ahead:]:
            turn(a)
        pv()

    def bias(i):
        if i < 2 * NHEAD * NT:
            kind, rest = ("A", i) if i < NHEAD * NT else ("B", i - NHEAD * NT)
            step("bias", kind=kind, i=i, h=rest // NT, t=rest % NT)

    def branch(n, o, gate_dst, gates_done):
        for jj in range(DC // 2):
            if not gates_done:
                for m in (2 * jj, 2 * jj + 1):
                    gate_chunk(n, m, gate_dst(m))
            t0 = len(s.units) * UT
            s.unit("w_branch", n, [(k, 2 * jj + mm) for mm in range(2) for k in range(4)])
            for mm in range(2):
                m = 2 * jj + mm
                need = {k: [("olo", ("ABC"[n], k))] for k in range(4)} if m == 0 else {}
                s.job(t0 + 4 * mm, 4, rhs=o, n=T, evac="branch", b=n, m=m, need=need, gate=gate_dst(m))

    def b_jobs(h):
        out = []
        for g in range(3):
            for w, (c, gain) in enumerate((("Q", "b_q_norm"), ("K", "b_k_norm"))):
                def go(g=g, w=w, c=c, gain=gain):
                    dst = (f"B{c}{h % 2}", g)
                    free = [("score", b_tiles[h - 2][-1]["i"])] if h >= 2 else []
                    j = column("w_in", 0, 12 + 12 * w + 4 * g + h, rhs="x", n=T, evac="scale", dst=dst, free=free)
                    hnorm((f"B{c}{g}", h), dst, gain, "ones", T, P, [("evac", j)])
                out.append(go)

            def go(g=g):
                nv = 3 * h + g
                free = [("v", ("B", *divmod(nv - 2, 3)))] if nv >= 2 else [("v", ("A", 2 + nv))]
                j = column("w_in", 0, 36 + 4 * g + h, rhs="x", n=T, evac="scale", dst=("VT", nv % 2), free=free)
                vturn(id=("B", h, g), src=("VT", nv % 2), nt=NT, dst=(f"BV{h % 2}", g), need=("evac", j),
                      dfree=[("pv", b_tiles[h - 2][-1]["i"])] if h >= 2 else [])
            out.append(go)
        return out

    b_tiles = [[dict(kind="B", h=h, t=t, need=[("hn", (f"B{c}{g}", h)) for c in "QK" for g in range(3)],
                     need_v=[("v", ("B", h, g)) for g in range(3)]) for t in range(NT)] for h in range(NHEAD)]
    a_tiles = [dict(kind="A", h=h, t=t, need=[("hn", ("AQ", h)), ("hn", ("AK", h))], need_v=[("v", ("A", h))])
               for h in range(NHEAD) for t in range(NT)]
    gates_a = [lambda m=m: gate_chunk(0, m, ("Y", m)) for m in range(DC)]
    first_b = b_jobs(0)
    gates_a[0]()
    attend(a_tiles, gates_a[1:] + first_b[:7],
           lambda h: hnorm(("AO", h), ("AO", h), "a_subln", "ones", T, P, [("pvd", ("A", h))]))
    first_b[7]()
    for h in range(NHEAD):
        step("split", id=("A", h), src=("AO", h), dst=("OA", h), need=[("hn", ("AO", h))])
    first_b[8]()
    branch(0, "OA", lambda m: ("Y", m), True)
    s.flush()

    c_queries = []
    for h in range(NHEAD):
        def go(h=h):
            j = column("w_in", 0, 48 + h, rhs="x", n=T, evac="scale", dst=("CQ", h))
            hnorm(("CQ", h), ("CQ", h), "c_q_norm", "ones", T, P, [("evac", j)])
        c_queries.append(go)
    for h in range(NHEAD):
        attend(b_tiles[h], b_jobs(h + 1) if h + 1 < NHEAD else c_queries)
        s.flush()

    def memory(n, which, gain):
        return ([lambda: step("memload", n=n, which=which, after=("evac", s.njobs - 1))]
                + [lambda m=m: step("memfresh", n=n, m=m, gain=gain, after=("evac", s.njobs - 1)) for m in range(DC)]
                + [lambda: s.norms.append(("rstdm", n))])

    for go in memory(0, 0, "mem_norm"):
        go()
    norms, s.norms = s.norms, []
    branch(1, "OB", lambda m: ("GT", m % 2), False)
    s.norms = norms
    needm = {k: [("ml", (0, k))] for k in range(DC)}
    for h in range(NHEAD):
        j = column("w_mem_kv", 0, h, rhs="mem", n=NM, evac="scalem", dst=("CK", h), need=needm)
        needm = {}
        hnorm(("CK", h), ("CK", h), "c_k_norm", "ones", NM, P, [("evac", j)])
        j = column("w_mem_kv", 0, 4 + h, rhs="mem", n=NM, evac="scalem", dst=("VT", h % 2),
                   free=[("v", ("C", h - 2))] if h >= 2 else [("v", ("B", 3, 2))])
        vturn(id=("C", h), src=("VT", h % 2), nt=NM // P, dst=("CV", h), need=("evac", j))
    gates_c = [lambda m=m: gate_chunk(2, m, ("GC", m)) for m in range(DC)]
    gates_c[0]()
    attend([dict(kind="C", h=h, t=t, need=[("hn", ("CQ", h)), ("hn", ("CK", h))], need_v=[("v", ("C", h))])
            for h in range(NHEAD) for t in range(NT)], gates_c[1:])
    branch(2, "OC", lambda m: ("GC", m), True)
    step("reload")
    norm = 1
    for m in range(DC):
        need = {k: [("ylo", k)] for k in range(DC)} if m == 0 else {}
        j = column("w_out", 0, m, rhs="y", n=T, evac="resid", m=m, c=1.0, need=need)
        step("refresh", n=norm, m=m, gain="norm_ffn", need=("evac", j))

    def ffn(w1, w3, w2, l, c, n, gain_next, back=False):
        t0 = len(s.units) * UT
        for f in range(NF):
            for w in (w1, w3):
                s.unit(w, l, [(k, f) for k in range(DC)])
        step("ffn", n=n, unit0=t0 // UT)
        t1 = len(s.units) * UT
        order = [(k, m) for m in range(DC) for k in range(NF)]
        for u in range(0, len(order), UT):
            s.unit(w2, l, order[u:u + UT])
        for m in range(DC):
            j = s.job(t1 + m * NF, NF, rhs="h", n=T, evac="back" if back else "resid", m=m, c=c, first=(m == 0), norm=n)
            step("refresh", n=n + 1, m=m, gain=gain_next, need=("x", m) if back else ("evac", j))

    ffn("w_ffn_gate", "w_ffn_up", "w_ffn_down", 0, 1.0, 1, "ffn1_norm_2_0", back=True)
    norm = 2

    for l in range(LAYERS):
        ffn("ffn1_w1_2", "ffn1_w3_2", "ffn1_w2_2", l, 0.5, norm, f"mix_norm_2_{l}")
        norm += 1
        s.norms.append(("rstd", norm))
        needx = {k: [("xl", (norm, k))] for k in range(DC)}

        def pair_jobs(pr):
            out = []
            for ws, hhs in (((0, 1), (0, 1)), ((2,), (0, 1)), ((3,), (0, 1))):
                for hh, w in [(hh, w) for hh in hhs for w in ws]:
                    h = 2 * pr + hh
                    c = ("HQ", "HF", None, "HG")[w]

                    def go(h=h, hh=hh, w=w, c=c):
                        nonlocal needx
                        if c:
                            column("w_in_2", l, 4 * w + h, rhs="x", n=T, evac="scale", dst=(f"{c}{pr}", hh), need=needx)
                            needx = {}
                        else:
                            free = [("v", (l, h - 2))] if h >= 2 else []
                            j = column("w_in_2", l, 8 + h, rhs="x", n=T, evac="scale", dst=("HVT", hh), free=free)
                            vturn(id=(l, h), src=("HVT", hh), nt=NT, dst=(f"HV{pr}", hh), need=("evac", j))
                    out.append(go)
            return out

        def pool_job(g):
            column("w_in_2", l, 16 + g, rhs="x", n=T, evac="scale", dst=("U", 0))
            step("poolsum", l=l, g=g)

        def pool_rest(g):
            step("pool", l=l, g=g)
            step("split", id=("M", l, 4 + g), src=("U", 1), dst=("MIX", 4 + g), need=[("pooled", (l, g))])

        def levels(pr, plan):
            for li in range(10):
                step("level", l=l, pr=pr, li=li)
                for go in plan[li]:
                    go()
            s.flush()

        def hprep(pr, j):
            step("hprep", l=l, pr=pr, need=("evac", j))

        def heads_out(pr, between):
            def norm_of(hh):
                h = 2 * pr + hh
                step("hsq", id=("H", l, h), src=(f"HO{pr}", hh), n=T, need=[("ho", (l, h))])
                sq = s.steps[-1][1]["sq"]
                return lambda: step("hnorm", id=("H", l, h), ones="ones", n=T, dim=P, sq=sq)

            def end(hh):
                h = 2 * pr + hh
                step("hscale", id=("H", l, h), src=(f"HO{pr}", hh), gain=f"hgrn_norm_2_{l}:{h}", n=T)
                step("hgate", l=l, pr=pr, hh=hh)
                step("split", id=("M", l, h), src=(f"HO{pr}", hh), dst=("MIX", h), need=[("hgated", (l, h))])
            step("hout", l=l, pr=pr, hh=0)
            first = norm_of(0)
            between()
            step("hout", l=l, pr=pr, hh=1)
            second = norm_of(1)
            return first, lambda: end(0), second, lambda: end(1)

        step("poolload", l=l, after=("evac", s.njobs - 1))
        first_pair = pair_jobs(0)
        for go in first_pair[:4]:
            go()
        hprep(0, s.njobs - 1)
        for go in first_pair[4:]:
            go()
        step("hsilu", l=l, pr=0, need=("evac", s.njobs - 1))
        second_pair = pair_jobs(1)
        levels(0, [[second_pair[0]], [second_pair[1]], [second_pair[2]], [second_pair[3]],
                   [lambda: pool_job(0)], [second_pair[4], lambda: pool_rest(0)], [lambda: pool_job(1)],
                   [second_pair[5], lambda: pool_rest(1)], [lambda: pool_job(2)],
                   [lambda: pool_rest(2)]])
        def between():
            hprep(1, s.njobs - 1)
            pool_job(3)
        first_sum, first_end, second_sum, second_end = heads_out(0, between)
        second_pair[6]()
        pool_rest(3)
        memload, *memparts, memsum = memory(1 + l, 1, f"mem_norm_2_{l}")
        memload()
        first_sum()
        jk, vids = {}, []
        needm = {k: [("ml", (1 + l, k))] for k in range(DC)}

        def key_job(c):
            nonlocal needm
            jk[c] = column("xa_wkv_2", l, c, rhs="mem2", n=NM, evac="scalem", dst=("XK", c), need=needm)
            needm = {}

        def value_job(c):
            nonlocal needm
            free = [("v", vids[-2])] if len(vids) >= 2 else []
            vt = ("VT", len(vids) % 2)
            vids.append(("X", l, c))
            j = column("xa_wkv_2", l, 8 + c, rhs="mem2", n=NM, evac="scalem", dst=vt, free=free, need=needm)
            needm = {}
            vturn(id=("X", l, c), src=vt, nt=NM // P, dst=("XV", c), need=("evac", j))

        kv = [lambda make=make, c=c: make(c) for make, c in
              [(key_job, 6), (key_job, 7)] + [(value_job, c) for c in range(4, DC)] + [(key_job, 0), (key_job, 1)]
              + [(value_job, 0), (value_job, 1), (key_job, 2), (value_job, 2), (value_job, 3)]
              + [(key_job, c) for c in (3, 4, 5)]]
        levels(1, [[first_end, second_pair[7], second_sum] + memparts[:4], memparts[4:] + [memsum],
                   [kv[0], kv[1], second_end], kv[2:4],
                   [lambda: step("hsilu", l=l, pr=1, need=("hn", ("H", l, 1)))] + kv[4:6],
                   kv[6:7], kv[7:8], kv[8:9], kv[9:11], kv[11:12]])
        first_sum, first_end, second_sum, second_end = heads_out(1, kv[12])
        kv[13]()
        first_sum()
        first_end()
        kv[14]()
        second_sum()
        second_end()
        kv[15]()
        s.flush()
        norm += 1
        for m in range(DC):
            need = {k: [("olo", ("M", l, k))] for k in range(DC)} if m == 0 else {}
            j = column("w_out_2", l, m, rows=(4, 5, 6, 7, 0, 1, 2, 3), rhs="mix", n=T, evac="resid", m=m, c=1.0, need=need)
            step("refresh", n=norm, m=m, gain=f"xa_norm_2_{l}", need=("evac", j))
        s.norms.append(("rstd", norm))
        needx, jq = {k: [("xl", (norm, k))] for k in range(DC)}, {}
        queries = []
        for c in range(DC):
            def go(c=c):
                nonlocal needx
                column("xa_wq_2", l, c, rhs="x", n=T, evac="scale", dst=("XQ", c), need=needx)
                jq[c] = s.njobs - 1
                needx = {}
            queries.append(go)
        for go in queries[:4]:
            go()
        attend([dict(kind="X", h=h, t=t, l=l, need=[("evac", jk[2 * h + 1])], queries=(jq, 2 * h + 1),
                     need_v=[("v", ("X", l, 2 * h + 1))]) for h in range(NHEAD) for t in range(NT)], queries[4:])
        norm += 1
        for m in range(DC):
            need = {k: [("olo", ("X", l, k))] for k in range(DC)} if m == 0 else {}
            j = column("xa_wo_2", l, m, rhs="xo", n=T, evac="resid", m=m, c=1.0, need=need)
            step("refresh", n=norm, m=m, gain=f"ffn2_norm_2_{l}", need=("evac", j))
        last = l == LAYERS - 1
        ffn("ffn2_w1_2", "ffn2_w3_2", "ffn2_w2_2", l, 0.5, norm, "final_norm_2" if last else f"ffn1_norm_2_{l + 1}")
        norm += 1
    step("rstd", n=norm)
    step("final", n=norm)
    return s


SCHEDULE = build_schedule()
NU = len(SCHEDULE.units)


class Counts:

    def __init__(self, known=None):
        self.known = known
        self.now = {}
        self.at = {}

    def mark(self, name, key, n=1):
        self.now[name] = self.now.get(name, 0) + n
        self.at[(name, key)] = self.now[name]

    def value(self, name, key):
        if self.known is None:
            return 1
        return self.known[(name, key)]


RAISES = {
    "pe": ["unit_free", "job_mid", "sum", "hsum", "score", "turned", "vt", "pv", "lev", "ho_mm", "pool_mm", "lam_mm"],
    "act": ["sq", "xh", "sd", "msq", "mh", "msd", "hsq", "hsd", "exp", "pt", "v", "ohi", "gate", "yhi", "silu",
            "sigm", "lam_exp", "lb_exp", "hgs"],
    "dve": ["setup", "xs", "xl", "rstd", "ms", "ml", "rstdm", "evac", "x", "hrec", "hn", "max", "nmax", "pn", "pvd",
            "olo", "y", "ylo", "fg", "fu", "fm", "fhh", "fhl", "fin", "hprep", "qkt", "lvd", "ho", "hgated",
            "pooled", "ptmp"],
    "pool": ["unit_hi", "unit_ready"],
}
DMAS = ["d_cols", "d_consts", "d_masks", "d_mem", "d_reload", "d_poolw", "d_out"]


def program(nc, dram, counts):
    ctx = ExitStack()
    with ctx:
        sems = {n: ctx.enter_context(nc.semaphore(n)) for ns in RAISES.values() for n in ns}
        sems.update({n: ctx.enter_context(nc.semaphore(n)) for n in DMAS})
        d_bias = [ctx.enter_context(nc.semaphore(f"d_bias{k}")) for k in range(BIAS_SLOTS)]
        d_x = [ctx.enter_context(nc.semaphore(f"d_x{m}")) for m in range(DC)]
        raw_landed = [ctx.enter_context(nc.semaphore(f"raw_landed{k}")) for k in range(RAW)]
        engine_of = {n: e for e, ns in RAISES.items() for n in ns}
        last = {}

        def sig(name, key=None):
            counts.mark(name, key)
            last[engine_of[name]] = (sems[name], counts.now[name])
            return sems[name], 1

        def on(name, key=None):
            return sems[name], counts.value(name, key)

        def own(engine):
            return last[engine]

        base = (nc.sbuf_base + 31) // 32 * 32
        top = [base]

        def fixed(name, shape, dt=F32):
            size = int(np.prod(shape[1:])) * (1 if dt == U8 else 4)
            t = nc.alloc_sbuf_tensor_at(name, shape, dt, offset=top[0])
            top[0] += (size + 31) // 32 * 32
            return t

        raw = [fixed(f"raw{k}", [P, UT * P]) for k in range(RAW)]
        whi = [fixed(f"whi{k}", [P, UT * P], F32R) for k in range(RING)]
        wlo = [fixed(f"wlo{k}", [P, UT * P], F32R) for k in range(RING)]
        X = fixed("x_res", [P, DC, T])
        xh_at = top[0]
        XH = fixed("x_hi", [P, DC, T], F32R)
        XL = fixed("x_lo", [P, DC, T], F32R)
        RSTD = fixed("rstd_x", [P, T])
        RSTDM = fixed("rstd_mem", [P, NM])
        SSUM = fixed("sq_sum", [P, T])
        SQ = fixed("sq", [P, 2, T])
        cols = fixed("cols", [P, NCOL])
        ones = fixed("ones", [P, P])
        halves = fixed("halves", [P, P])
        ident = fixed("ident", [P, P])
        masks = fixed("masks", [P, 7, P], U8)
        poolrec = fixed("poolrec", [P, 4, 16])
        small = fixed("small", [P, 96])
        arena = top[0]

        def area(name, kb, shape, dt=F32):
            size = int(np.prod(shape[1:])) * 4
            assert arena + kb * KB + size <= nc.sbuf_usable_end, (name, kb, size, nc.sbuf_usable_end - arena)
            return nc.alloc_sbuf_tensor_at(name, shape, dt, offset=arena + int(kb * KB))

        masks_f = area("masks_f", 98, [P, 7, P])
        AQ, AK, AV = (area(n, o, [P, NHEAD, T]) for n, o in (("a_q", 0), ("a_k", 8), ("a_v", 16)))
        AO = area("a_out", 42, [P, NHEAD, T])
        OAH, OAL = (area(n, o, [P, NHEAD, T], F32R) for n, o in (("oa_hi", 0), ("oa_lo", 8)))
        BQ = [area(f"b_q{s}", o, [P, 3, T]) for s, o in ((0, 24), (1, 0))]
        BK = [area(f"b_k{s}", o + 6, [P, 3, T]) for s, o in ((0, 24), (1, 0))]
        BV = [area(f"b_v{s}", o + 12, [P, 3, T]) for s, o in ((0, 24), (1, 0))]
        OBH, OBL = (area(n, o, [P, NHEAD, T], F32R) for n, o in (("ob_hi", 42), ("ob_lo", 50)))
        BIAS = area("bias", 58, [P, BIAS_SLOTS, 768])
        CQ = area("c_q", 24, [P, NHEAD, T])
        CK = area("c_k", 32, [P, NHEAD, NM])
        CV = area("c_v", 36, [P, NHEAD, NM])
        OCH, OCL = (area(n, o, [P, NHEAD, T], F32R) for n, o in (("oc_hi", 0), ("oc_lo", 8)))
        GC = area("gate_c", 54, [P, DC, T])
        MRAW = area("mem_raw", 16, [P, DC, NM])
        MH, ML = (area(n, o, [P, DC, NM], F32R) for n, o in (("mem_hi", 0), ("mem_lo", 8)))
        MRAW2 = [area("mem_raw2a", 58, [P, DC // 2, NM]), area("mem_raw2b", 94, [P, DC // 2, NM])]
        MH2 = nc.alloc_sbuf_tensor_at("mem2_hi", [P, DC, NM], F32R, offset=xh_at)
        ML2 = nc.alloc_sbuf_tensor_at("mem2_lo", [P, DC, NM], F32R, offset=xh_at + 8 * KB)

        def mem_tensors(n, m):
            if n == 0:
                return MRAW[:, m, :], MH, ML
            return MRAW2[m // 4][:, m % 4, :], MH2, ML2
        SP = area("probs", 70, [P, 2, 1024])
        SP4 = SP[:, :, :].rearrange("p a n -> p (a n)").rearrange("p (a n) -> p a n", a=SPS)
        PT = area("probs_t", 78, [P, 6, T])
        SD = area("sd", 90, [P, T])
        REC = area("rec", 92, [P, T])
        VT = area("vt_sb", 94, [P, 2, T])
        GT = area("gate_sb", 98, [P, 2, T])
        HH, HL = (area(n, o, [P, NF, T], F32R) for n, o in (("h_hi", 0), ("h_lo", 44)))
        FG, FU, FS, FM = (area(n, o, [P, T]) for n, o in (("ffn_g", 88), ("ffn_u", 90), ("ffn_s", 92), ("ffn_m", 94)))
        HQ = [area(f"h_q{s}", o, [P, 2, T]) for s, o in ((0, 0), (1, 42))]
        HF = [area(f"h_f{s}", o, [P, 2, T]) for s, o in ((0, 4), (1, 46))]
        HK = area("h_k", 8, [P, 2, T])
        HS = area("h_suf", 12, [P, 2, T])
        QT, KT = (area(n, o, [P, 2, T]) for n, o in (("h_qt", 16), ("h_kt", 20)))
        HG = [area(f"h_g{s}", o, [P, 2, T]) for s, o in ((0, 24), (1, 50))]
        HV = [area(f"h_v{s}", o, [P, 2, T]) for s, o in ((0, 28), (1, 54))]
        AD = area("h_ad", 32, [P, 2, NT, P])
        A128 = area("h_a128", 36, [P, 2, 2, P])
        A256 = area("h_a256", 38, [P, 2, 2, 2 * P])
        HVT = area("hvt_sb", 58, [P, 2, T])
        MIXH, MIXL = (area(n, o, [P, DC, T], F32R) for n, o in (("mix_hi", 62), ("mix_lo", 78)))
        UB = area("pool_u", 94, [P, 3, T])
        HSD = area("h_sd", 100, [P, T])
        HREC = [area(f"h_rec{s}", o, [P, T]) for s, o in ((0, 4), (1, 46))]
        HO = [area(f"h_o{s}", o, [P, 2, T]) for s, o in ((0, 0), (1, 42))]
        PW = area("pool_w_sb", 68, [P, 4, P])
        XQ = area("x_q", 8, [P, DC, T])
        XK = area("x_k", 0, [P, DC, NM])
        XV = area("x_v", 24, [P, DC, NM])
        XOH, XOL = (area(n, o, [P, DC, T], F32R) for n, o in (("xo_hi", 32), ("xo_lo", 48)))
        YH, YL = (area(n, o, [P, DC, T], F32R) for n, o in (("y_hi", 32), ("y_lo", 48)))

        bufs = {"AQ": AQ, "AK": AK, "AV": AV, "AO": AO, "VT": VT, "GT": GT, "Y": X, "CQ": CQ, "CK": CK, "CV": CV,
                "BQ0": BQ[0], "BQ1": BQ[1], "BK0": BK[0], "BK1": BK[1], "BV0": BV[0], "BV1": BV[1],
                "HQ0": HQ[0], "HQ1": HQ[1], "HF0": HF[0], "HF1": HF[1], "HG0": HG[0], "HG1": HG[1],
                "HV0": HV[0], "HV1": HV[1], "HVT": HVT, "HO0": HO[0], "HO1": HO[1], "GC": GC, "U": UB, "XQ": XQ, "XK": XK, "XV": XV}
        parts = {"x": (XH, XL), "h": (HH, HL), "mem": (MH, ML), "mem2": (MH2, ML2), "OA": (OAH, OAL), "OB": (OBH, OBL),
                 "OC": (OCH, OCL), "mix": (MIXH, MIXL), "xo": (XOH, XOL), "y": (YH, YL)}

        def buf(where):
            return bufs[where[0]][:, where[1], :]

        def col(name, m=0):
            return cols[:, COLS[name][0] + m:COLS[name][0] + m + 1]

        def gain_of(name):
            base, _, m = name.partition(":")
            return col(base, int(m or 0))

        LAM = small[:, 4:5]

        def lb(l, m):
            return small[:, 28 + 8 * l + m:29 + 8 * l + m]

        def one_minus_lb(l, m):
            return small[:, 32 + 8 * l + m:33 + 8 * l + m]

        def pair_of(first, i):
            return small[:, first + 2 * (i % SPS):first + 2 * (i % SPS) + 2]

        MAX, NEG_MAX, TOTAL, RECIP = 48, 56, 64, 72

        PS = ctx.enter_context(nc.psum_tensor("ps", [P, 8, T], F32))
        flat = PS[:, :, :].rearrange("p b n -> p (b n)")
        S = flat[:, 0:2 * T]
        TR = flat[:, 2 * T:4 * T]
        O = PS[:, 7, :]

        def bank(j):
            return PS[:, 4 + j % 3, :]

        def job_done(a):
            end = a["tile0"] + a["nk"]
            return on("unit_free", end // UT - 1) if end % UT == 0 else on("job_mid", a["j"])

        jobs = [a for k, a in SCHEDULE.steps if k == "job"]
        def probs(a):
            return SP[:, a["i"] % 2, :] if a["kind"] in "AB" else SP4[:, a["i"] % SPS, :]

        def score_bank(a):
            return ((0, 1), S) if a["kind"] in "AB" else ((a["i"] % 2,), PS[:, a["i"] % 2, 0:NM])

        kinds = {"A": 4, "B": 6, "C": 2, "X": 2}

        def out_key(a):
            return ("X", a["l"], 2 * a["h"]) if a["kind"] == "X" else (a["kind"], a["h"])

        block = ctx.enter_context(nc.Block())

        @block.sync
        def _(sp):
            step = RAW * RING

            def load(i, c):
                if not (isinstance(i, int) and i * step + c < RAW):
                    sp.wait_ge(sems["unit_ready"], i * step + (c - RAW + 1))
                src = dram["weights"][bass.ds(i * step + c, 1)].rearrange("a p n -> (a p) n")
                sp.dma_start(raw[c % RAW][:, :], src).then_inc(raw_landed[c % RAW], 16)

            for m in range(DC):
                sp.dma_start(X[:, m, :], dram["x"][:, m, :]).then_inc(d_x[m], 16)
                if m == 1:
                    load(0, 0)
            for c in range(1, step):
                load(0, c)
            with sp.Fori(1, NU // step) as i:
                for c in range(step):
                    load(i, c)
            assert NU % step
            for c in range(NU % step):
                load(NU // step, c)
            for m in range(DC):
                sp.wait_ge(*on("fin", m))
                sp.dma_start(dram["out"][:, m, :], X[:, m, :]).then_inc(sems["d_out"], 16)
            sp.wait_ge(sems["d_out"], 16 * DC)

        @block.gpsimd
        def _(pool):
            step = RAW * RING

            def await_unit(i, c):
                pool.wait_ge(raw_landed[c % RAW], (i * RING + (c // RAW + 1)) * 16)
                if not (isinstance(i, int) and i * step + c < RING):
                    pool.wait_ge(sems["unit_free"], i * step + (c - RING + 1))

            def high(c):
                pool.tensor_scalar(whi[c % RING][:, :], raw[c % RAW][:, :], 1.0, 0.0, ALU.mult,
                                   ALU.add).then_inc(sems["unit_hi"], 1)

            def split(i, c, more=True):
                first = isinstance(i, int) and i * step + c == 0
                if more and not first:
                    await_unit(i, c + 1)
                pool.wait_ge(sems["unit_hi"], i * step + (c + 1))
                pool.tensor_tensor(wlo[c % RING][:, :], raw[c % RAW][:, :], whi[c % RING][:, :].bitcast(F32),
                                   ALU.subtract).then_inc(sems["unit_ready"], 1)
                if first:
                    await_unit(i, c + 1)
                if more:
                    high(c + 1)

            await_unit(0, 0)
            high(0)
            for c in range(step):
                split(0, c)
            with pool.Fori(1, NU // step) as i:
                for c in range(step):
                    split(i, c)
            for c in range(NU % step):
                split(NU // step, c, c + 1 < NU % step)

        @block.tensor
        def _(pe):
            free = {}

            def wait_free(*slots):
                for step in {free[slot]: 1 for slot in slots if slot in free}:
                    pe.wait_ge(*on(*step))

            def three(out, hi, lo, xhi, xlo, start, stop):
                pe.matmul(out, hi, xhi, start=start, stop=False)
                pe.matmul(out, hi, xlo, start=False, stop=False)
                return pe.matmul(out, lo, xhi, start=False, stop=stop)

            def norm_sum(kind, norm):
                mem = kind == "rstdm"
                n = NM if mem else T
                pe.wait_ge(*on("ms" if mem else "xs", (norm, DC - 1)))
                wait_free("O")
                pe.matmul(O[:, 0:n], ones[:, :], SSUM[:, 0:n], start=True, stop=True)\
                    .then_inc(*sig("sum", (kind, norm)))
                free["O"] = ("msd" if mem else "sd", norm)

            for kind, a in SCHEDULE.steps:
                if kind == "setup":
                    pe.wait_ge(sems["d_cols"], 32)
                    pe.wait_ge(*on("setup", "prod"))
                    pe.matmul(O[:, 0:2], ones[0:64, :], small[0:64, 0:2], start=True, stop=True)\
                        .then_inc(*sig("lam_mm"))
                    free["O"] = ("lam_exp", None)
                elif kind == "consts":
                    pe.wait_ge(sems["d_consts"], 48)
                elif kind in ("rstd", "rstdm"):
                    norm_sum(kind, a["n"])
                elif kind == "job":
                    xhi, xlo = parts[a["rhs"]]
                    n = a["n"]
                    out = bank(a["j"])[:, 0:n]
                    if a["j"] >= 3:
                        pe.wait_ge(*on("evac", a["j"] - 3))
                    for k in range(a["nk"]):
                        tile = a["tile0"] + k
                        c = tile % UT
                        if c == 0 or k == 0:
                            pe.wait_ge(sems["unit_ready"], tile // UT + 1)
                        for key in a.get("need", {}).get(a["rows"][k] if "rows" in a else k, []):
                            pe.wait_ge(*on(*key))
                        if a.get("first"):
                            pe.wait_ge(sems["fhl"], counts.value("fhl", ("base", a["norm"])) + k + 1)
                        kk = a["rows"][k] if "rows" in a else k
                        hi = whi[tile // UT % RING][:, c * P:(c + 1) * P]
                        lo = wlo[tile // UT % RING][:, c * P:(c + 1) * P]
                        mm = three(out, hi, lo, xhi[:, kk, 0:n], xlo[:, kk, 0:n], k == 0, k == a["nk"] - 1)
                        if c == UT - 1:
                            mm.then_inc(*sig("unit_free", tile // UT))
                        elif k == a["nk"] - 1:
                            mm.then_inc(*sig("job_mid", a["j"]))
                elif kind == "hnorm":
                    pe.wait_ge(*on("hsq", a["id"]))
                    wait_free("O")
                    lhs = halves if a["ones"] == "halves" else ones
                    pe.matmul(O[:, 0:a["n"]], lhs[:, :], SQ[:, a["sq"], 0:a["n"]], start=True, stop=True)\
                        .then_inc(*sig("hsum", a["id"]))
                    free["O"] = ("hsd", a["id"])
                elif kind == "vturn":
                    pe.wait_ge(*on(*a["need"]))
                    wait_free("T0")
                    src = buf(a["src"])
                    for t in range(a["nt"]):
                        mm = pe.transpose(TR[:, t * P:(t + 1) * P], src[:, t * P:(t + 1) * P], ident[:, :])
                    mm.then_inc(*sig("vt", a["id"]))
                    free["T0"] = ("v", a["id"])
                elif kind == "score":
                    i, h, t, what = a["i"], a["h"], a["t"], a["kind"]
                    if t == 0:
                        for key in a["need"]:
                            pe.wait_ge(*on(*key))
                        if what == "X":
                            jq, c = a["queries"]
                            pe.wait_ge(*on("evac", jq[c]))
                    slots, sc = score_bank(a)
                    wait_free(*(f"S{b}" for b in slots))
                    tt = slice(t * P, (t + 1) * P)
                    if what == "A":
                        for c in range(2):
                            r = slice(64 * c, 64 * c + 64)
                            mm = pe.matmul(sc[:, c * T:(c + 1) * T], AQ[r, h, tt], AK[r, h, :], start=True, stop=True)
                    elif what == "B":
                        q, k = BQ[h % 2], BK[h % 2]
                        pe.matmul(sc[:, 0:T], q[:, 0, tt], k[:, 0, :], start=True, stop=True)
                        for g in (1, 2):
                            o = T + (g - 1) * P
                            mm = pe.matmul(sc[:, o:o + P], q[:, g, tt], k[:, g, tt], start=True, stop=True)
                    elif what == "C":
                        mm = pe.matmul(sc, CQ[:, h, tt], CK[:, h, :], start=True, stop=True)
                    else:
                        for c in range(2):
                            mm = pe.matmul(sc, XQ[:, 2 * h + c, tt], XK[:, 2 * h + c, :],
                                           start=(c == 0), stop=(c == 1))
                    mm.then_inc(*sig("score", i))
                    for b in slots:
                        free[f"S{b}"] = ("nmax", i) if what in "AB" else ("exp", i)
                elif kind == "turn":
                    i = a["i"]
                    pe.wait_ge(*on("pn", i))
                    wait_free("T0", "T1") if a["kind"] == "B" else wait_free("T0")
                    for c in range(kinds[a["kind"]]):
                        mm = pe.transpose(TR[:, c * P:(c + 1) * P], probs(a)[:, c * P:(c + 1) * P], ident[:, :])
                    mm.then_inc(*sig("turned", i))
                    free["T0"] = ("pt", i)
                    if a["kind"] == "B":
                        free["T1"] = ("pt", i)
                elif kind == "pv":
                    i, h, what = a["i"], a["h"], a["kind"]
                    pe.wait_ge(*on("pt", i))
                    for key in a["need_v"]:
                        pe.wait_ge(*on(*key))
                    wait_free("O")
                    if what == "A":
                        for c in range(NT):
                            mm = pe.matmul(O, AV[:, h, c * P:(c + 1) * P], PT[:, c, :], start=(c == 0), stop=(c == NT - 1))
                    elif what == "B":
                        v = BV[h % 2]
                        pe.matmul(O, v[:, 0, 0:P], PT[:, 0, :], start=True, stop=False)
                        for g in (1, 2):
                            for c in range(NT):
                                tt = slice(c * P, (c + 1) * P)
                                pe.matmul(O[:, tt], v[:, g, tt], PT[:, 3 + g, tt], start=False, stop=False,
                                          skip_group_check=True)
                        for c in range(1, NT):
                            mm = pe.matmul(O, v[:, 0, c * P:(c + 1) * P], PT[:, c, :], start=False, stop=(c == NT - 1))
                    elif what == "C":
                        for c in range(2):
                            mm = pe.matmul(O, CV[:, h, c * P:(c + 1) * P], PT[:, c, :], start=(c == 0), stop=(c == 1))
                    else:
                        for c in range(2):
                            mm = pe.matmul(O, XV[:, 2 * h, c * P:(c + 1) * P], PT[:, c, :], start=(c == 0), stop=(c == 1))
                        mm.then_inc(*sig("pv", (i, 0)))
                        wait_free("T1")
                        for c in range(2):
                            mm = pe.matmul(TR[:, T:2 * T], XV[:, 2 * h + 1, c * P:(c + 1) * P], PT[:, c, :],
                                           start=(c == 0), stop=(c == 1))
                        free["T1"] = ("olo", ("X", a["l"], 2 * h + 1))
                    mm.then_inc(*sig("pv", i))
                    free["O"] = ("pvd", ("A", h)) if what == "A" else ("olo", out_key(a))
                elif kind == "ffn":
                    n, u0 = a["n"], a["unit0"]
                    fg0, fu0 = counts.value("fg", ("base", n)), counts.value("fu", ("base", n))
                    wait_free("S0", "S1", "T0", "T1")

                    def gate_up(i):
                        for jj in range(2):
                            for w, (name, first) in enumerate((("fg", fg0), ("fu", fu0))):
                                c = 2 * jj + w
                                pe.wait_ge(sems["unit_ready"], i * 4 + (u0 + c + 1))
                                if not isinstance(i, int):
                                    pe.wait_ge(sems[name], i * 2 + (first + jj - 1))
                                for k in range(DC):
                                    if isinstance(i, int) and jj == 0 and w == 0:
                                        pe.wait_ge(*on("xl", (n, k)))
                                    cc = slice(k * P, (k + 1) * P)
                                    r = (u0 + c) % RING
                                    mm = three(PS[:, c, :], whi[r][:, cc], wlo[r][:, cc], XH[:, k, :], XL[:, k, :],
                                               k == 0, k == DC - 1)
                                mm.then_inc(sems["unit_free"], 1)
                                if isinstance(i, int) and jj == 0 and w == 0:
                                    norm_sum("rstd", n)

                    gate_up(0)
                    with pe.Fori(1, NF // 2) as i:
                        gate_up(i)
                    for u in range(2 * NF):
                        counts.mark("unit_free", u0 + u)
                    for slot in ("S0", "S1", "T0", "T1"):
                        free[slot] = ("fu", ("end", n))
                elif kind == "level":
                    l, pr, li = a["l"], a["pr"], a["li"]
                    slots, out = (("S0", "S1"), S) if li % 2 == 0 else (("T0", "T1"), TR)
                    pe.wait_ge(*on("hprep", (l, pr)) if li == 0 else on("qkt", (l, pr, li)))
                    wait_free(*slots)
                    q, k = (HQ[pr], HK) if li == 0 else (QT, KT)
                    for hh in range(2):
                        o = hh * T
                        if 1 <= li <= 7:
                            size = 1 << (li - 1)
                            for c in range(NT):
                                def second(ap):
                                    return ap.rearrange("p (b two h) -> p b two h", two=2, h=size)[:, :, 1, :]
                                mm = pe.matmul(second(out[:, o + c * P:o + (c + 1) * P]), k[:, hh, c * P:(c + 1) * P],
                                               second(q[:, hh, c * P:(c + 1) * P]), start=True, stop=True)
                            continue
                        if li == 0:
                            pairs = [(c, c, c + 1, c) for c in range(NT)]
                        elif li == 8:
                            pairs = [(0, 1, 2, 0), (2, 3, 4, 1)]
                        else:
                            pairs = [(0, 2, 4, 0), (1, 2, 4, 2)]
                        for sc, t0, t1, at in pairs:
                            w = (t1 - t0) * P
                            mm = pe.matmul(out[:, o + at * P:o + at * P + w], k[:, hh, sc * P:(sc + 1) * P],
                                           q[:, hh, t0 * P:t1 * P], start=True, stop=True)
                    mm.then_inc(*sig("lev", (l, pr, li)))
                    for slot in slots:
                        free[slot] = ("lvd", (l, pr, li))
                elif kind == "hout":
                    l, pr, hh = a["l"], a["pr"], a["hh"]
                    pe.wait_ge(*on("lvd", (l, pr, 9)))
                    pe.wait_ge(*on("v", (l, 2 * pr + hh)))
                    wait_free("O")
                    v = HV[pr][:, hh, :]
                    near, far = A128[:, hh, :, :], A256[:, hh, :, :]
                    terms = [[(0, AD[:, hh, 0, :])],
                             [(1, AD[:, hh, 1, :]), (0, near[:, 0, :])],
                             [(2, AD[:, hh, 2, :]), (0, far[:, 0, 0:P]), (1, far[:, 1, 0:P])],
                             [(3, AD[:, hh, 3, :]), (2, near[:, 1, :]), (0, far[:, 0, P:2 * P]), (1, far[:, 1, P:2 * P])]]
                    for t, group in enumerate(terms):
                        for x, (sc, w) in enumerate(group):
                            mm = pe.matmul(O[:, t * P:(t + 1) * P], v[:, sc * P:(sc + 1) * P], w, start=(x == 0),
                                           stop=(x == len(group) - 1))
                    mm.then_inc(*sig("ho_mm", (l, 2 * pr + hh)))
                    free["O"] = ("ho", (l, 2 * pr + hh))
                elif kind == "pool":
                    l, g = a["l"], a["g"]
                    pe.wait_ge(*on("ptmp", (l, g)))
                    pe.wait_ge(sems["d_poolw"], 16 * (l + 1))
                    wait_free("O")
                    pe.matmul(O, PW[:, g, :], UB[:, pool_slot(g), :], start=True, stop=True).then_inc(*sig("pool_mm", (l, g)))
                    free["O"] = ("pooled", (l, g))

        @block.scalar
        def _(act):
            def copy(out, in_, scale=1.0):
                return act.activation(out, in_, ACT.Copy, scale=scale)

            def root(n):
                act.wait_ge(*on("sum", ("rstd", n)))
                act.activation(RSTD[:, :], O, ACT.Sqrt, bias=EPS, scale=1.0 / D).then_inc(*sig("sd", n))

            sd_reader = [None]
            for kind, a in SCHEDULE.steps:
                if kind == "setup":
                    for t, name, landed in ((cols, "cols", "d_cols"), (ones, "ones", "d_cols"),
                                            (halves, "halves", "d_consts"), (ident, "ident", "d_consts"),
                                            (poolrec, "poolrec", "d_consts")):
                        act.dma_start(t[tuple([slice(None)] * len(t.shape))], dram[name]).then_inc(sems[landed], 16)
                    act.wait_ge(*on("lam_mm"))
                    act.activation(small[:, 2:4], O[:, 0:2], ACT.Exp).then_inc(*sig("lam_exp"))
                    act.wait_ge(*on("setup", "lbd"))
                    act.activation(small[:, 12:20], small[:, 12:20], ACT.Exp).then_inc(*sig("lb_exp"))
                elif kind == "consts":
                    act.dma_start(masks_f[:, :, :], dram["masks"]).then_inc(sems["d_masks"], 16)
                elif kind == "refresh":
                    n, m = a["n"], a["m"]
                    if n == 0:
                        act.wait_ge(d_x[m], 16)
                        act.wait_ge(sems["d_cols"], 32)
                    else:
                        act.wait_ge(*on(*a["need"]))
                    if a["sq_free"]:
                        act.wait_ge(*on(*a["sq_free"]))
                    act.activation(SQ[:, a["sq"], :], X[:, m, :], ACT.Square).then_inc(*sig("sq", (n, m)))
                    if a["gain"] != "final_norm_2":
                        copy(XH[:, m, :], X[:, m, :], col(a["gain"], m)).then_inc(*sig("xh", (n, m)))
                elif kind == "memload":
                    if a["after"]:
                        act.wait_ge(*on(*a["after"]))
                    if a["n"]:
                        act.wait_ge(*on("olo", ("M", a["n"] - 1, DC - 1)))
                    if a["n"] == 0:
                        act.dma_start(MRAW[:, :, :], dram["mem0"]).then_inc(sems["d_mem"], 16)
                    else:
                        for x in range(2):
                            act.dma_start(MRAW2[x][:, :, :], dram["mem1"][:, 4 * x:4 * x + 4, :])\
                                .then_inc(sems["d_mem"], 16)
                elif kind == "memfresh":
                    n, m = a["n"], a["m"]
                    act.wait_ge(sems["d_mem"], 16 * (2 * n + 1))
                    if n and m == 0:
                        act.wait_ge(*on(*a["after"]))
                    raw_m, hi, _ = mem_tensors(n, m)
                    act.wait_ge(*on(*a["sq_free"]))
                    act.activation(SQ[:, a["sq"], 0:NM], raw_m, ACT.Square).then_inc(*sig("msq", (n, m)))
                    copy(hi[:, m, :], raw_m, col(a["gain"], m)).then_inc(*sig("mh", (n, m)))
                elif kind == "rstd":
                    root(a["n"])
                elif kind == "rstdm":
                    act.wait_ge(*on("sum", (kind, a["n"])))
                    act.activation(RSTDM[:, :], O[:, 0:NM], ACT.Sqrt, bias=EPS, scale=1.0 / D).then_inc(*sig("msd", a["n"]))
                elif kind == "hsq":
                    for key in a["need"]:
                        act.wait_ge(*on(*key))
                    act.wait_ge(*on(*a["sq_free"]))
                    act.activation(SQ[:, a["sq"], 0:a["n"]], buf(a["src"]), ACT.Square).then_inc(*sig("hsq", a["id"]))
                elif kind == "hnorm":
                    act.wait_ge(*on("hsum", a["id"]))
                    if sd_reader[0] is not None:
                        act.wait_ge(*on("hrec", sd_reader[0]))
                    sd = HSD if a["id"][0] == "H" else SD
                    act.activation(sd[:, 0:a["n"]], O[:, 0:a["n"]], ACT.Sqrt, bias=EPS,
                                   scale=1.0 / a["dim"]).then_inc(*sig("hsd", a["id"]))
                    sd_reader[0] = a["id"]
                elif kind == "vturn":
                    act.wait_ge(*on("vt", a["id"]))
                    for key in a.get("dfree", []):
                        act.wait_ge(*on(*key))
                    copy(buf(a["dst"]), TR[:, 0:a["nt"] * P]).then_inc(*sig("v", a["id"]))
                elif kind == "gate":
                    act.wait_ge(*on(*a["need"]))
                    act.activation(buf(a["dst"]), buf(a["dst"]), ACT.Sigmoid,
                                   bias=col("b_gate", 8 * a["n"] + a["m"])).then_inc(*sig("gate", (a["n"], a["m"])))
                elif kind == "bias":
                    i, w = a["i"], T if a["kind"] == "A" else 768
                    if i >= BIAS_SLOTS:
                        act.wait_ge(*on("nmax", i - BIAS_SLOTS))
                    act.dma_start(BIAS[:, i % BIAS_SLOTS, 0:w], dram["bias" + a["kind"]][a["h"], :, a["t"]])\
                        .then_inc(d_bias[i % BIAS_SLOTS], 16)
                elif kind == "score":
                    i, what = a["i"], a["kind"]
                    act.wait_ge(*on("nmax", i))
                    nmx, tot = pair_of(NEG_MAX, i), pair_of(TOTAL, i)
                    if what == "A":
                        for c in range(2):
                            p = probs(a)[:, c * T:(c + 1) * T]
                            act.activation(p, p, ACT.Exp, bias=nmx[:, c:c + 1], accum_out=tot[:, c:c + 1])\
                                .then_inc(*sig("exp", i))
                    elif what == "B":
                        p = probs(a)[:, 0:768]
                        act.activation(p, p, ACT.Exp, bias=nmx[:, 0:1], accum_out=tot[:, 0:1]).then_inc(*sig("exp", i))
                    else:
                        act.wait_ge(*on("turned", a.get("before", i - SPS)))
                        act.activation(probs(a)[:, 0:NM], score_bank(a)[1], ACT.Exp, bias=nmx[:, 0:1],
                                       scale=1.0 if what == "C" else 256 ** -0.5,
                                       accum_out=tot[:, 0:1]).then_inc(*sig("exp", i))
                elif kind == "turn":
                    i, t, nk = a["i"], a["t"], kinds[a["kind"]]
                    act.wait_ge(*on("turned", i))
                    if t == 0 and i:
                        act.wait_ge(*on("pv", i - 1))
                    copy(PT[:, 0:nk, t * P:(t + 1) * P],
                         TR[:, 0:nk * P].rearrange("p (c q) -> p c q", c=nk)).then_inc(*sig("pt", i))
                elif kind == "pv":
                    i, h, what = a["i"], a["h"], a["kind"]
                    if what == "X":
                        act.wait_ge(*on("pv", (i, 0)))
                        copy(XOH[:, 2 * h, :], O).then_inc(*sig("ohi", out_key(a)))
                        act.wait_ge(*on("pv", i))
                        copy(XOH[:, 2 * h + 1, :], TR[:, T:2 * T]).then_inc(*sig("ohi", ("X", a["l"], 2 * h + 1)))
                    elif what != "A":
                        act.wait_ge(*on("pv", i))
                        copy(parts["O" + what][0][:, h, :], O).then_inc(*sig("ohi", out_key(a)))
                elif kind == "split":
                    for key in a["need"]:
                        act.wait_ge(*on(*key))
                    hi = (OAH if a["dst"][0] == "OA" else MIXH)[:, a["dst"][1], :]
                    copy(hi, buf(a["src"])).then_inc(*sig("ohi", a["id"]))
                elif kind == "evac" and a["evac"] == "branch" and a["b"] == 2:
                    act.wait_ge(*on("y", (2, a["m"])))
                    copy(YH[:, a["m"], :], X[:, a["m"], :]).then_inc(*sig("yhi", a["m"]))
                elif kind == "reload":
                    act.wait_ge(*on("ylo", DC - 1))
                    act.wait_ge(*own("act"))
                    act.dma_start(X[:, :, :], dram["x"]).then_inc(sems["d_reload"], 16)
                elif kind == "ffn":
                    n = a["n"]
                    fg0 = counts.value("fg", ("base", n))
                    counts.at[("silu", ("base", n))] = counts.now.get("silu", 0)
                    root(n)

                    def silu(i):
                        for jj in range(2):
                            act.wait_ge(sems["fg"], i * 2 + (fg0 + jj + 1))
                            act.activation(FS[:, :], FG[:, :], ACT.Silu).then_inc(sems["silu"], 1)

                    silu(0)
                    with act.Fori(1, NF // 2) as i:
                        silu(i)
                    counts.mark("silu", ("end", n), NF)
                    last["act"] = (sems["silu"], counts.now["silu"])
                elif kind == "poolload":
                    act.wait_ge(*on(*a["after"]))
                    act.dma_start(PW[:, :, :], dram["pool_w"][:, a["l"]]).then_inc(sems["d_poolw"], 16)
                elif kind == "hprep":
                    l, pr = a["l"], a["pr"]
                    act.wait_ge(*on(*a["need"]))
                    if pr:
                        act.wait_ge(*on("lvd", (l, 0, 9)))
                    act.activation(HK[:, :, :], HF[pr][:, :, :], ACT.Sigmoid, scale=-1.0).then_inc(*sig("sigm", (l, pr, 0)))
                    act.wait_ge(*own("act"))
                    act.activation(HF[pr][:, :, :], HF[pr][:, :, :], ACT.Sigmoid).then_inc(*sig("sigm", (l, pr, 1)))
                elif kind == "hsilu":
                    l, pr = a["l"], a["pr"]
                    act.wait_ge(*on(*a["need"]))
                    act.activation(HG[pr][:, :, :], HG[pr][:, :, :], ACT.Silu).then_inc(*sig("hgs", (l, pr)))

        @block.vector
        def _(dve):
            def after_own():
                if "dve" in last:
                    dve.wait_ge(*own("dve"))

            def rstd(n):
                dve.wait_ge(*on("sd", n))
                dve.reciprocal(RSTD[:, :], RSTD[:, :]).then_inc(*sig("rstd", n))

            for kind, a in SCHEDULE.steps:
                if kind == "setup":
                    dve.wait_ge(sems["d_cols"], 32)
                    la = COLS["lambdas"][0]
                    dve.tensor_tensor(small[0:64, 0:2], cols[0:64, la:la + 4:2], cols[0:64, la + 1:la + 4:2],
                                      ALU.mult).then_inc(*sig("setup", "prod"))
                    for name, c in (("a_q_norm", 64 ** -0.5), ("b_q_norm", P ** -0.5), ("c_q_norm", P ** -0.5),
                                    ("a_subln", 1.0 - LAMBDA_INIT)):
                        dve.tensor_scalar(col(name), col(name), c, None, ALU.mult).then_inc(*sig("setup", name))
                    l0, l1 = (cols[:, COLS[f"lb_logits_2_{l}"][0]:COLS[f"lb_logits_2_{l}"][0] + 4] for l in range(2))
                    mx, e0, e1, tot = small[:, 8:12], small[:, 12:16], small[:, 16:20], small[:, 20:24]
                    dve.tensor_tensor(mx, l0, l1, ALU.max).then_inc(*sig("setup", "lbm"))
                    after_own()
                    dve.tensor_tensor(e0, l0, mx, ALU.subtract).then_inc(*sig("setup", "lbd0"))
                    dve.tensor_tensor(e1, l1, mx, ALU.subtract).then_inc(*sig("setup", "lbd"))
                    dve.wait_ge(*on("lb_exp"))
                    dve.tensor_tensor(tot, e0, e1, ALU.add).then_inc(*sig("setup", "lbs"))
                    after_own()
                    dve.reciprocal(small[:, 24:28], tot).then_inc(*sig("setup", "lbr"))
                    after_own()
                    dve.memset(small[:, 28:32], 0.0).then_inc(*sig("setup", "lb0"))
                    dve.memset(small[:, 32:36], 1.0).then_inc(*sig("setup", "lb0n"))
                    dve.tensor_tensor(small[:, 36:40], e1, small[:, 24:28], ALU.mult).then_inc(*sig("setup", "lb1"))
                    dve.tensor_tensor(small[:, 40:44], e0, small[:, 24:28], ALU.mult).then_inc(*sig("setup", "lb1n"))
                    dve.wait_ge(*on("lam_exp"))
                    dve.scalar_tensor_tensor(LAM, small[:, 2:3], LAMBDA_INIT, small[:, 3:4], ALU.add, ALU.subtract)\
                        .then_inc(*sig("setup", "lam"))
                elif kind == "masks":
                    dve.wait_ge(sems["d_consts"], 48)
                    dve.wait_ge(sems["d_masks"], 16)
                    dve.tensor_copy(masks[:, :, :], masks_f[:, :, :]).then_inc(*sig("setup", "masks"))
                elif kind in ("refresh", "memfresh"):
                    n, m = a["n"], a["m"]
                    mem = kind == "memfresh"
                    w = NM if mem else T
                    sq = SQ[:, a["sq"], 0:w]
                    after_own()
                    dve.wait_ge(*on("msq" if mem else "sq", (n, m)))
                    if m == 0:
                        if a["ssum_free"]:
                            dve.wait_ge(*on(*a["ssum_free"]))
                        dve.tensor_copy(SSUM[:, 0:w], sq).then_inc(*sig("ms" if mem else "xs", (n, m)))
                    else:
                        dve.tensor_tensor(SSUM[:, 0:w], SSUM[:, 0:w], sq, ALU.add)\
                            .then_inc(*sig("ms" if mem else "xs", (n, m)))
                    if a["gain"] != "final_norm_2":
                        src, hi, lo = mem_tensors(n, m) if mem else (X[:, m, :], XH, XL)
                        dve.wait_ge(*on("mh" if mem else "xh", (n, m)))
                        dve.scalar_tensor_tensor(lo[:, m, :], src, col(a["gain"], m),
                                                 hi[:, m, :].bitcast(F32), ALU.mult, ALU.subtract)\
                            .then_inc(*sig("ml" if mem else "xl", (n, m)))
                elif kind == "rstd":
                    rstd(a["n"])
                elif kind == "rstdm":
                    dve.wait_ge(*on("msd", a["n"]))
                    dve.reciprocal(RSTDM[:, :], RSTDM[:, :]).then_inc(*sig("rstdm", a["n"]))
                elif kind == "evac":
                    out = bank(a["j"])[:, 0:a["n"]]
                    m = a.get("m")
                    for key in a.get("free", []):
                        dve.wait_ge(*on(*key))
                    after_own()
                    dve.wait_ge(*job_done(a))
                    if a["evac"] in ("scale", "scalem"):
                        r = RSTD[:, :] if a["evac"] == "scale" else RSTDM[:, :]
                        dve.tensor_tensor(buf(a["dst"])[:, 0:a["n"]], out, r, ALU.mult).then_inc(*sig("evac", a["j"]))
                    elif a["evac"] == "resid":
                        if a["rhs"] == "y" and m == 0:
                            dve.wait_ge(sems["d_reload"], 16)
                        dve.scalar_tensor_tensor(X[:, m, :], out, a["c"], X[:, m, :], ALU.mult, ALU.add)\
                            .then_inc(*sig("evac", a["j"]))
                    elif a["evac"] == "back":
                        dve.tensor_tensor(FG[:, :], out, X[:, m, :], ALU.add).then_inc(*sig("evac", a["j"]))
                        after_own()
                        dve.tensor_copy(X[:, m, :].rearrange("p (s r) -> p s r", r=NT),
                                        FG[:, :].rearrange("p (r s) -> p s r", r=NT)).then_inc(*sig("x", m))
                    else:
                        b = a["b"]
                        dve.wait_ge(*on("gate", (b, m)))
                        y = X[:, m, :]
                        if b == 0:
                            dve.tensor_tensor(y, out, y, ALU.mult).then_inc(*sig("evac", a["j"]))
                        else:
                            g = buf(a["gate"])
                            dve.tensor_tensor(g, out, g, ALU.mult).then_inc(*sig("evac", a["j"]))
                            after_own()
                            dve.tensor_tensor(y, y, g, ALU.add).then_inc(*sig("y", (b, m)))
                            if b == 2:
                                dve.wait_ge(*on("yhi", m))
                                dve.tensor_tensor(YL[:, m, :], y, YH[:, m, :].bitcast(F32), ALU.subtract)\
                                    .then_inc(*sig("ylo", m))
                elif kind == "hscale":
                    n = a["n"]
                    sd, rec = (HSD, HREC[a["id"][2] // 2]) if a["id"][0] == "H" else (SD, REC)
                    after_own()
                    dve.wait_ge(*on("hsd", a["id"]))
                    dve.reciprocal(rec[:, 0:n], sd[:, 0:n]).then_inc(*sig("hrec", a["id"]))
                    after_own()
                    dve.scalar_tensor_tensor(buf(a["src"]), buf(a["src"]), gain_of(a["gain"]), rec[:, 0:n],
                                             ALU.mult, ALU.mult).then_inc(*sig("hn", a["id"]))
                elif kind == "score":
                    i, t, what = a["i"], a["t"], a["kind"]
                    mx, nmx = pair_of(MAX, i), pair_of(NEG_MAX, i)
                    after_own()
                    if what in "AB":
                        dve.wait_ge(d_bias[i % BIAS_SLOTS], 16 * (i // BIAS_SLOTS + 1))
                    if i >= 2 and what in "AB":
                        dve.wait_ge(*on("turned", i - 2))
                    dve.wait_ge(*on("score", i))
                    n = 1
                    if what == "A":
                        n = 2
                        for c in range(2):
                            dve.tensor_tensor_reduce(probs(a)[:, c * T:(c + 1) * T], S[:, c * T:(c + 1) * T],
                                                     BIAS[:, i % BIAS_SLOTS, 0:T], 1.0, -1e30, ALU.add, ALU.max,
                                                     mx[:, c:c + 1]).then_inc(*sig("max", i))
                    elif what == "B":
                        dve.tensor_tensor_reduce(probs(a)[:, 0:768], S[:, 0:768], BIAS[:, i % BIAS_SLOTS, :],
                                                 1.0, -1e30, ALU.add, ALU.max, mx[:, 0:1]).then_inc(*sig("max", i))
                    else:
                        dve.tensor_reduce(mx[:, 0:1], score_bank(a)[1], AX.X, ALU.max).then_inc(*sig("max", i))
                    after_own()
                    dve.tensor_scalar(nmx[:, 0:n], mx[:, 0:n], -(256 ** -0.5) if what == "X" else -1.0, None,
                                      ALU.mult).then_inc(*sig("nmax", i))
                elif kind == "probs":
                    i, what = a["i"], a["kind"]
                    tot, rs = pair_of(TOTAL, i), pair_of(RECIP, i)
                    n = 2 if what == "A" else 1
                    w = kinds[what] * P
                    after_own()
                    dve.wait_ge(*on("exp", i))
                    dve.reciprocal(rs[:, 0:n], tot[:, 0:n]).then_inc(*sig("ptmp", ("r", i)))
                    after_own()
                    p = probs(a)[:, 0:w]
                    if what == "A":
                        q = probs(a)[:, T:2 * T]
                        dve.tensor_scalar(q, q, rs[:, 1:2], LAM, ALU.mult, ALU.mult).then_inc(*sig("ptmp", ("q", i)))
                        after_own()
                        dve.scalar_tensor_tensor(p, p, rs[:, 0:1], q, ALU.mult, ALU.subtract).then_inc(*sig("pn", i))
                    else:
                        dve.tensor_scalar(p, p, rs[:, 0:1], None, ALU.mult).then_inc(*sig("pn", i))
                elif kind == "pv":
                    h, what = a["h"], a["kind"]
                    after_own()
                    if what == "A":
                        dve.wait_ge(*on("pv", a["i"]))
                        dve.tensor_copy(AO[:, h, :], O).then_inc(*sig("pvd", ("A", h)))
                    elif what == "X":
                        for c, src in ((0, O), (1, TR[:, T:2 * T])):
                            key = ("X", a["l"], 2 * h + c)
                            dve.wait_ge(*on("ohi", key))
                            dve.tensor_tensor(XOL[:, 2 * h + c, :], src, XOH[:, 2 * h + c, :].bitcast(F32),
                                              ALU.subtract).then_inc(*sig("olo", key))
                    else:
                        hi, lo = parts["O" + what]
                        dve.wait_ge(*on("ohi", out_key(a)))
                        dve.tensor_tensor(lo[:, h, :], O, hi[:, h, :].bitcast(F32), ALU.subtract)\
                            .then_inc(*sig("olo", out_key(a)))
                elif kind == "split":
                    hi, lo = (OAH, OAL) if a["dst"][0] == "OA" else (MIXH, MIXL)
                    c = a["dst"][1]
                    after_own()
                    dve.wait_ge(*on("ohi", a["id"]))
                    dve.tensor_tensor(lo[:, c, :], buf(a["src"]), hi[:, c, :].bitcast(F32), ALU.subtract)\
                        .then_inc(*sig("olo", a["id"]))
                elif kind == "ffn":
                    n, u0 = a["n"], a["unit0"]
                    first = {w: counts.now.get(w, 0) for w in ("fg", "fu", "fm", "fhh", "fhl")}
                    for w in first:
                        counts.at[(w, ("base", n))] = first[w]
                    silu0 = counts.value("silu", ("base", n))
                    rstd(n)
                    three_d = [P, 1, T]

                    def chunk(i, jj):
                        peeled = isinstance(i, int)
                        f = i * 2 + jj

                        def at(w):
                            return i * 2 + (first[w] + jj + 1)
                        if peeled and jj == 0:
                            after_own()
                        else:
                            dve.wait_ge(sems["fhl"], i * 2 + (first["fhl"] + jj))
                        dve.wait_ge(sems["unit_free"], i * 4 + (u0 + 2 * jj + 1))
                        dve.tensor_tensor(FG[:, :], PS[:, 2 * jj, :], RSTD[:, :], ALU.mult).then_inc(sems["fg"], 1)
                        dve.wait_ge(sems["unit_free"], i * 4 + (u0 + 2 * jj + 2))
                        dve.tensor_tensor(FU[:, :], PS[:, 2 * jj + 1, :], RSTD[:, :], ALU.mult).then_inc(sems["fu"], 1)
                        dve.wait_ge(sems["silu"], i * 2 + (silu0 + jj + 1))
                        dve.wait_ge(sems["fu"], at("fu"))
                        dve.tensor_tensor(FM[:, :], FS[:, :], FU[:, :], ALU.mult).then_inc(sems["fm"], 1)
                        dve.wait_ge(sems["fm"], at("fm"))
                        fm = FM[:, :].rearrange("p (a n) -> p a n", a=1)
                        hh = HH[:, f:f + 1, :] if peeled else HH[:, bass.ds(f, 1), :]
                        hl = HL[:, f:f + 1, :] if peeled else HL[:, bass.ds(f, 1), :]
                        dve.tensor_scalar(hh, fm, 1.0, None, ALU.mult).then_inc(sems["fhh"], 1)
                        dve.wait_ge(sems["fhh"], at("fhh"))
                        dve.tensor_tensor(hl, fm, hh.bitcast(F32), ALU.subtract).then_inc(sems["fhl"], 1)

                    for jj in range(2):
                        chunk(0, jj)
                    with dve.Fori(1, NF // 2) as i:
                        for jj in range(2):
                            chunk(i, jj)
                    for w in first:
                        counts.mark(w, ("end", n), NF)
                    last["dve"] = (sems["fhl"], counts.now["fhl"])
                elif kind == "hprep":
                    l, pr = a["l"], a["pr"]
                    after_own()
                    dve.memset(HS[:, :, :], 1.0).then_inc(*sig("hprep", (l, pr, "s")))
                    for hh in range(2):
                        h = 2 * pr + hh
                        dve.wait_ge(*on("sigm", (l, pr, 1)))
                        dve.tensor_scalar(HK[:, hh, :], HK[:, hh, :], one_minus_lb(l, h), None, ALU.mult)\
                            .then_inc(*sig("hprep", (l, pr, "k", hh)))
                        dve.tensor_scalar(HF[pr][:, hh, :], HF[pr][:, hh, :], one_minus_lb(l, h), lb(l, h),
                                          ALU.mult, ALU.add).then_inc(*sig("hprep", (l, pr) if hh else (l, pr, "f")))
                elif kind == "level":
                    l, pr, li = a["l"], a["pr"], a["li"]

                    def blocks(t, h):
                        return t[:, :, :].rearrange("p a t -> p (a t)").rearrange("p (b two h) -> p b two h", two=2, h=h)
                    q, pre, size = HQ[pr], HF[pr], 1 << max(li - 1, 0)
                    if 1 <= li < 9:
                        b, s = blocks(pre, size), blocks(HS, size)
                        nb = 2 * T // (2 * size)
                        after_own()
                        dve.tensor_tensor(s[:, :, 0, :], s[:, :, 0, :],
                                          b[:, :, 1, size - 1:size].broadcast_to([P, nb, size]), ALU.mult)\
                            .then_inc(*sig("qkt", (l, pr, "s", li)))
                        after_own()
                        dve.tensor_tensor(b[:, :, 1, :], b[:, :, 1, :],
                                          b[:, :, 0, size - 1:size].broadcast_to([P, nb, size]), ALU.mult)\
                            .then_inc(*sig("qkt", (l, pr, "p", li)))
                    src = S if li % 2 == 0 else TR
                    tiles = src.rearrange("p (c t) -> p c t", t=P)
                    ad = AD[:, :, :, :].rearrange("p a c t -> p (a c) t")
                    after_own()
                    dve.wait_ge(*on("lev", (l, pr, li)))
                    if li == 0:
                        dve.tensor_tensor(ad, tiles, ident[:, :].rearrange("p (a t) -> p a t", a=1)
                                          .broadcast_to([P, 2 * NT, P]), ALU.mult).then_inc(*sig("lvd", (l, pr, li)))
                    elif li <= 7:
                        def second(ap):
                            return ap.rearrange("p c (b two h) -> p c b two h", two=2, h=size)[:, :, :, 1, :]
                        mask = masks[:, li - 1, :].rearrange("p (b two h) -> p b two h", two=2, h=size)[:, :, 1, :]
                        mask = mask.rearrange("p b h -> p () b h").broadcast_to([P, 2 * NT, P // 2 // size, size])
                        dve.copy_predicated(second(ad), mask, second(tiles)).then_inc(*sig("lvd", (l, pr, li)))
                    elif li == 8:
                        dve.tensor_copy(A128[:, :, :, :].rearrange("p a c t -> p a (c t)"),
                                        src.rearrange("p (a t) -> p a t", a=2)[:, :, 0:2 * P])\
                            .then_inc(*sig("lvd", (l, pr, li)))
                    else:
                        dve.tensor_copy(A256[:, :, :, :].rearrange("p a c t -> p (a c t)"), src)\
                            .then_inc(*sig("lvd", (l, pr, li)))
                    if li == 0:
                        after_own()
                        dve.tensor_tensor(QT[:, :, :], q[:, :, :], pre[:, :, :], ALU.mult)\
                            .then_inc(*sig("qkt", (l, pr, "q", 1)))
                        dve.tensor_copy(KT[:, :, :], HK[:, :, :]).then_inc(*sig("qkt", (l, pr, 1)))
                    elif li < 9:
                        size = 1 << li
                        after_own()
                        dve.tensor_tensor(blocks(QT, size)[:, :, 1, :], blocks(q, size)[:, :, 1, :],
                                          blocks(pre, size)[:, :, 1, :], ALU.mult)\
                            .then_inc(*sig("qkt", (l, pr, "q", li + 1)))
                        dve.tensor_tensor(blocks(KT, size)[:, :, 0, :], blocks(HK, size)[:, :, 0, :],
                                          blocks(HS, size)[:, :, 0, :], ALU.mult).then_inc(*sig("qkt", (l, pr, li + 1)))
                elif kind == "hout":
                    h = 2 * a["pr"] + a["hh"]
                    after_own()
                    dve.wait_ge(*on("ho_mm", (a["l"], h)))
                    dve.tensor_copy(HO[a["pr"]][:, a["hh"], :], O).then_inc(*sig("ho", (a["l"], h)))
                elif kind == "hgate":
                    h = 2 * a["pr"] + a["hh"]
                    after_own()
                    dve.wait_ge(*on("hgs", (a["l"], a["pr"])))
                    dve.tensor_tensor(HO[a["pr"]][:, a["hh"], :], HO[a["pr"]][:, a["hh"], :], HG[a["pr"]][:, a["hh"], :], ALU.mult)\
                        .then_inc(*sig("hgated", (a["l"], h)))
                elif kind == "poolsum":
                    l, g = a["l"], a["g"]
                    w = 2 << g
                    cur, d = 0, 1
                    while d < w:
                        nxt = 1 if cur != 1 else 2
                        after_own()
                        dve.tensor_tensor(UB[:, nxt, d:T], UB[:, cur, d:T], UB[:, cur, 0:T - d], ALU.add)\
                            .then_inc(*sig("ptmp", (l, g, d)))
                        dve.tensor_copy(UB[:, nxt, 0:d], UB[:, cur, 0:d]).then_inc(*sig("ptmp", (l, g, d, "h")))
                        cur, d = nxt, 2 * d
                    assert cur == pool_slot(g)
                    s = UB[:, cur, :]
                    after_own()
                    dve.tensor_tensor(s[:, 0:w], s[:, 0:w], poolrec[:, g, 0:w], ALU.mult).then_inc(*sig("ptmp", (l, g, "a")))
                    after_own()
                    dve.tensor_tensor(s[:, 0:w], s[:, 0:w], UB[:, 0, 0:w], ALU.subtract).then_inc(*sig("ptmp", (l, g, "b")))
                    dve.scalar_tensor_tensor(s[:, w:T], s[:, w:T], 1.0 / w, UB[:, 0, w:T], ALU.mult, ALU.subtract)\
                        .then_inc(*sig("ptmp", (l, g)))
                elif kind == "pool":
                    l, g = a["l"], a["g"]
                    after_own()
                    dve.wait_ge(*on("pool_mm", (l, g)))
                    dve.tensor_scalar(UB[:, 1, :], O, col(f"pool_scale_2_{l}", g), None, ALU.mult)\
                        .then_inc(*sig("pooled", (l, g)))
                elif kind == "final":
                    for m in range(DC):
                        after_own()
                        dve.scalar_tensor_tensor(X[:, m, :], X[:, m, :], col("final_norm_2", m), RSTD[:, :],
                                                 ALU.mult, ALU.mult).then_inc(*sig("fin", m))


def pool_slot(g):
    return 1 if g % 2 == 0 else 2


def tokens_by_residue(a):
    return a.reshape(T // NT, NT, *a.shape[1:]).swapaxes(0, 1).reshape(a.shape)


def feature_major(a):
    return np.ascontiguousarray(a.T.reshape(DC, P, a.shape[0]).transpose(1, 0, 2))


def distance_constants():
    pos = tokens_by_residue(np.arange(T))
    dist = np.abs(pos[:, None] - pos[None, :]).astype(np.float32)
    out_of = np.float32(-1e30)
    slopes_a = [2.0 ** (-8.0 * (i + 1) / NHEAD) for i in range(NHEAD)]
    slopes_b = np.exp2(-8.0 * np.arange(1, 13, dtype=np.float32) / np.float32(12)).astype(np.float32).reshape(3, NHEAD)
    bias_a = np.stack([(-np.float32(s) * dist).reshape(NT, P, T).transpose(1, 0, 2) for s in slopes_a])
    sub = np.arange(P)
    rel = np.abs(sub[:, None] - sub[None, :])
    bias_b = []
    for h in range(NHEAD):
        g0 = np.where(dist <= 64, -slopes_b[0, h] * dist, out_of).reshape(NT, P, T).transpose(1, 0, 2)
        g1 = np.where(rel <= 64, -slopes_b[1, h] * (4 * rel).astype(np.float32), out_of)
        g2 = np.where(rel % 4 == 0, -slopes_b[2, h] * (4 * rel).astype(np.float32), out_of)
        rest = np.broadcast_to(np.concatenate([g1, g2], 1)[:, None, :], (P, NT, 2 * P))
        bias_b.append(np.concatenate([g0, rest], 2))
    return bias_a.astype(np.float32), np.stack(bias_b).astype(np.float32)


def constants():
    t = np.arange(P)
    masks = []
    for li in range(7):
        h = 1 << li
        same = t[:, None] // (2 * h) == t[None, :] // (2 * h)
        masks.append(same & (t[:, None] % (2 * h) < h) & (t[None, :] % (2 * h) >= h))
    rec = np.zeros((P, 4, 16), np.float32)
    for g in range(4):
        rec[:, g, :] = 1.0 / np.minimum(np.arange(1, 17), 2 << g)
    half = (t[:, None] // 64 == t[None, :] // 64).astype(np.float32)
    bias_a, bias_b = distance_constants()
    return {"ones": np.ones((P, P), np.float32), "halves": half, "ident": np.eye(P, dtype=np.float32),
            "masks": np.ascontiguousarray(np.stack(masks, 1)).astype(np.float32), "poolrec": rec,
            "biasA": bias_a, "biasB": bias_b}


def weight_units(inputs):
    out = np.empty((NU, P, UT * P), np.float32)
    for u, (name, l, tiles) in enumerate(SCHEDULE.units):
        w = inputs[name][0, l] if name == "w_branch" else inputs[name][l]
        for c, (r, k) in enumerate(tiles):
            out[u, :, c * P:(c + 1) * P] = w[r * P:(r + 1) * P, k * P:(k + 1) * P]
    return out


def vector_columns(inputs):
    out = np.zeros((P, NCOL), np.float32)
    for name, (at, n) in COLS.items():
        if name == "lambdas":
            for c, w in enumerate(("a_lambda_q1", "a_lambda_k1", "a_lambda_q2", "a_lambda_k2")):
                out[0:64, at + c] = inputs[w][0]
            continue
        base, l = (name[:-2], int(name[-1])) if name[-2:] in ("_0", "_1") else (name, 0)
        v = inputs[base] if base == "final_norm_2" else inputs[base][l]
        if v.size == 64:
            out[0:64, at] = out[64:P, at] = v
        else:
            out[:, at:at + n] = v.reshape(n, P).T
    return out


def kernel(**inputs):
    import concourse.bacc as bacc
    from concourse.bass_utils import run_bass_kernel_spmd as run

    inputs = {k: np.asarray(v) for k, v in inputs.items()}
    arrays = {"weights": weight_units(inputs), "cols": vector_columns(inputs),
              "x": feature_major(tokens_by_residue(inputs["x"][0])),
              "mem0": feature_major(inputs["mem"][0]), "mem1": feature_major(inputs["mem_2"][0]),
              "pool_w": np.ascontiguousarray(inputs["pool_w_2"].transpose(2, 0, 1, 3)), **constants()}
    known = None
    for _ in range(2):
        nc = bacc.Bacc("TRN2", target_bir_lowering=False, num_devices=1)
        dram = {k: nc.dram_tensor(f"in_{k}", a.shape, mybir.dt.from_np(a.dtype), kind="ExternalInput").ap()
                for k, a in arrays.items()}
        dram["out"] = nc.dram_tensor("out_x", (P, DC, T), F32, kind="ExternalOutput").ap()
        counts = Counts(known)
        program(nc, dram, counts)
        known = counts.at
    got = run(nc, [{f"in_{k}": a for k, a in arrays.items()}], core_ids=[0])
    out = got.results[0]["out_x"]
    return out.transpose(2, 1, 0).reshape(1, T, D)
```
